# Optimizing a Trainium2 kernel written in Bass

```python
import jax, jax.numpy as jnp
from jax import lax
import numpy as np

D_MODEL = 1024
BATCH = 1
SEQ = 256
DEPTH = 2

D_MIX = D_MODEL
CONV_WIDTH = D_MIX // 4
CONV_GROUPS = 4
CONV_K = 31
MLA_HEADS = 8
MLA_NOPE = 64
MLA_ROPE = 32
MLA_QK = MLA_NOPE + MLA_ROPE
MLA_V = 64
MLA_WIDTH = MLA_HEADS * MLA_V
Q_LORA = 768
KV_LORA = 256
ROPE_THETA = 10000.0
Q_BLOCK = 128
SG_WIDTH = D_MIX - CONV_WIDTH - MLA_WIDTH
SG_HEADS = 4
SG_HEAD_DIM = SG_WIDTH // SG_HEADS
SG_CHUNK = 128
IN_SIZES = (CONV_WIDTH, CONV_WIDTH, CONV_WIDTH,
            Q_LORA, KV_LORA, MLA_ROPE, MLA_WIDTH,
            SG_WIDTH, SG_WIDTH, SG_WIDTH)
IN_COLS = 3 * CONV_WIDTH + Q_LORA + KV_LORA + MLA_ROPE + MLA_WIDTH + 3 * SG_WIDTH
EPS = 1e-6


def _rms_norm(x, g):
    xf = x.astype(jnp.float32)
    y = xf * lax.rsqrt(jnp.mean(xf * xf, axis=-1, keepdims=True) + EPS)
    return (y * g.astype(jnp.float32)).astype(x.dtype)

def _layer_norm(x, g, b):
    xf = x.astype(jnp.float32)
    mu = jnp.mean(xf, axis=-1, keepdims=True)
    var = jnp.mean(jnp.square(xf - mu), axis=-1, keepdims=True)
    y = (xf - mu) * lax.rsqrt(var + EPS) * g.astype(jnp.float32) + b.astype(jnp.float32)
    return y.astype(x.dtype)

def _rope_tables(seq):
    half = MLA_ROPE // 2
    inv_freq = ROPE_THETA ** (-jnp.arange(half, dtype=jnp.float32) / half)
    ang = jnp.arange(seq, dtype=jnp.float32)[:, None] * inv_freq[None, :]
    return jnp.cos(ang), jnp.sin(ang)

def _apply_rope(x, cos, sin):
    half = MLA_ROPE // 2
    c = cos[None, :, None, :].astype(x.dtype)
    s = sin[None, :, None, :].astype(x.dtype)
    x1, x2 = x[..., :half], x[..., half:]
    return jnp.concatenate([x1 * c - x2 * s, x1 * s + x2 * c], axis=-1)

def _conv_branch(a, a_glu, conv_w, conv_b, ln_g, ln_b, pw_w, pw_b):
    y = a * jax.nn.sigmoid(a_glu)
    y = lax.conv_general_dilated(
        y, conv_w[:, None, :], window_strides=(1,),
        padding=[(CONV_K - 1, 0)],
        dimension_numbers=('NWC', 'WIO', 'NWC'),
        feature_group_count=CONV_WIDTH) + conv_b
    y = jax.nn.silu(_layer_norm(y, ln_g, ln_b))
    return y @ pw_w + pw_b

def _causal_attention(q, k, v):
    B, S, H, Dq = q.shape
    nb = S // Q_BLOCK
    scale = Dq ** -0.5
    q_blocks = jnp.moveaxis(q.reshape(B, nb, Q_BLOCK, H, Dq), 1, 0)
    k_pos = jnp.arange(S)

    def block(args):
        qb, i = args
        q_pos = i * Q_BLOCK + jnp.arange(Q_BLOCK)
        s = jnp.einsum('bqhd,bkhd->bhqk', qb, k).astype(jnp.float32) * scale
        s = jnp.where(k_pos[None, :] <= q_pos[:, None], s, -jnp.inf)
        p = jax.nn.softmax(s, axis=-1).astype(v.dtype)
        return jnp.einsum('bhqk,bkhd->bqhd', p, v)

    out = lax.map(block, (q_blocks, jnp.arange(nb)))
    return jnp.moveaxis(out, 0, 1).reshape(B, S, H * v.shape[-1])

def _mla_branch(c_q, c_kv, k_rope, q_norm_g, w_uq, kv_norm_g, w_ukv,
                qk_q_g, qk_k_g, cos, sin):
    B, S, _ = c_q.shape
    q = (_rms_norm(c_q, q_norm_g) @ w_uq).reshape(B, S, MLA_HEADS, MLA_QK)
    kv = (_rms_norm(c_kv, kv_norm_g) @ w_ukv).reshape(B, S, MLA_HEADS, MLA_NOPE + MLA_V)
    k_nope, v = kv[..., :MLA_NOPE], kv[..., MLA_NOPE:]
    k_r = jnp.broadcast_to(k_rope[:, :, None, :], (B, S, MLA_HEADS, MLA_ROPE))
    k = jnp.concatenate([k_nope, k_r], axis=-1)
    q = _rms_norm(q, qk_q_g)
    k = _rms_norm(k, qk_k_g)
    q = jnp.concatenate([q[..., :MLA_NOPE], _apply_rope(q[..., MLA_NOPE:], cos, sin)], axis=-1)
    k = jnp.concatenate([k[..., :MLA_NOPE], _apply_rope(k[..., MLA_NOPE:], cos, sin)], axis=-1)
    return _causal_attention(q, k, v)

def _sgu_branch(u, v, ln_g, ln_b, sg_w, sg_b):
    B, S, _ = u.shape
    nc = S // SG_CHUNK
    u = jax.nn.gelu(u)
    v = _layer_norm(jax.nn.gelu(v), ln_g, ln_b)
    v = v.reshape(B, nc, SG_CHUNK, SG_HEADS, SG_HEAD_DIM)
    mask = jnp.tril(jnp.ones((SG_CHUNK, SG_CHUNK), dtype=bool))
    w = jnp.where(mask[None], sg_w, jnp.zeros_like(sg_w))
    mixed = jnp.einsum('gts,bcsgd->bctgd', w, v) + sg_b.T[None, None, :, :, None]
    return u * mixed.reshape(B, S, SG_WIDTH)

def _layer(x, cos, sin, norm_g, w_in, conv_w, conv_b, conv_ln_g, conv_ln_b,
           conv_pw_w, conv_pw_b, q_norm_g, w_uq, kv_norm_g, w_ukv, qk_q_g, qk_k_g,
           sg_ln_g, sg_ln_b, sg_w, sg_b, branch_norm_g, w_out):
    h = _rms_norm(x, norm_g)
    proj = h @ w_in
    idx = np.cumsum(IN_SIZES)[:-1].tolist()
    (a, a_glu, z_conv, c_q, c_kv, k_rope, z_mla,
     u_sg, v_sg, z_sg) = jnp.split(proj, idx, axis=-1)

    y_conv = _conv_branch(a, a_glu, conv_w, conv_b, conv_ln_g, conv_ln_b,
                          conv_pw_w, conv_pw_b) * jax.nn.silu(z_conv)
    y_mla = _mla_branch(c_q, c_kv, k_rope, q_norm_g, w_uq, kv_norm_g, w_ukv,
                        qk_q_g, qk_k_g, cos, sin) * jax.nn.silu(z_mla)
    y_sg = _sgu_branch(u_sg, v_sg, sg_ln_g, sg_ln_b, sg_w, sg_b) * jax.nn.silu(z_sg)

    g_conv = branch_norm_g[:CONV_WIDTH]
    g_mla = branch_norm_g[CONV_WIDTH:CONV_WIDTH + MLA_WIDTH]
    g_sg = branch_norm_g[CONV_WIDTH + MLA_WIDTH:]
    y = jnp.concatenate([_rms_norm(y_conv, g_conv),
                         _rms_norm(y_mla, g_mla),
                         _rms_norm(y_sg, g_sg)], axis=-1)
    return x + y @ w_out

def first_inputs(seed: int = 0) -> dict:
    key = jax.random.key(seed)
    ks = jax.random.split(key, 24)
    f32 = jnp.float32

    def nrm(k, shape, scale):
        return jax.random.normal(k, shape, f32) * scale

    def gain(k, shape):
        return 1.0 + 0.02 * jax.random.normal(k, shape, f32)

    L = DEPTH
    return {
        'x': jax.random.normal(ks[0], (BATCH, SEQ, D_MODEL), f32),
        'norm_g': gain(ks[1], (L, D_MODEL)),
        'w_in': nrm(ks[2], (L, D_MODEL, IN_COLS), D_MODEL ** -0.5),
        'conv_w': nrm(ks[3], (L, CONV_K, CONV_WIDTH), CONV_K ** -0.5),
        'conv_b': nrm(ks[4], (L, CONV_WIDTH), 0.01),
        'conv_ln_g': gain(ks[5], (L, CONV_WIDTH)),
        'conv_ln_b': nrm(ks[6], (L, CONV_WIDTH), 0.01),
        'conv_pw_w': nrm(ks[7], (L, CONV_WIDTH, CONV_WIDTH), CONV_WIDTH ** -0.5),
        'conv_pw_b': nrm(ks[8], (L, CONV_WIDTH), 0.01),
        'q_norm_g': gain(ks[9], (L, Q_LORA)),
        'w_uq': nrm(ks[10], (L, Q_LORA, MLA_HEADS * MLA_QK), Q_LORA ** -0.5),
        'kv_norm_g': gain(ks[11], (L, KV_LORA)),
        'w_ukv': nrm(ks[12], (L, KV_LORA, MLA_HEADS * (MLA_NOPE + MLA_V)), KV_LORA ** -0.5),
        'qk_q_g': gain(ks[13], (L, MLA_QK)),
        'qk_k_g': gain(ks[14], (L, MLA_QK)),
        'sg_ln_g': gain(ks[15], (L, SG_WIDTH)),
        'sg_ln_b': nrm(ks[16], (L, SG_WIDTH), 0.01),
        'sg_w': nrm(ks[17], (L, SG_HEADS, SG_CHUNK, SG_CHUNK), SG_CHUNK ** -0.5),
        'sg_b': 1.0 + nrm(ks[18], (L, SG_HEADS, SG_CHUNK), 0.1),
        'branch_norm_g': gain(ks[19], (L, D_MIX)),
        'w_out': nrm(ks[20], (L, D_MIX, D_MODEL), D_MIX ** -0.5),
    }

def first_block(x, norm_g, w_in, conv_w, conv_b, conv_ln_g, conv_ln_b, conv_pw_w,
              conv_pw_b, q_norm_g, w_uq, kv_norm_g, w_ukv, qk_q_g, qk_k_g,
              sg_ln_g, sg_ln_b, sg_w, sg_b, branch_norm_g, w_out):
    cos, sin = _rope_tables(x.shape[1])
    for l in range(DEPTH):
        x = _layer(x, cos, sin, norm_g[l], w_in[l], conv_w[l], conv_b[l],
                   conv_ln_g[l], conv_ln_b[l], conv_pw_w[l], conv_pw_b[l],
                   q_norm_g[l], w_uq[l], kv_norm_g[l], w_ukv[l], qk_q_g[l], qk_k_g[l],
                   sg_ln_g[l], sg_ln_b[l], sg_w[l], sg_b[l], branch_norm_g[l], w_out[l])
    return x


N_MIXERS = 2
N_A_LAYERS = (DEPTH + N_MIXERS - 1) // N_MIXERS
N_B_LAYERS = DEPTH // N_MIXERS

HG_HEADS = 8
HG_DK = D_MODEL // HG_HEADS
HG_DV = D_MODEL // HG_HEADS
HG_CHUNK = 128
LRU_WIDTH = D_MODEL
LRU_BLOCKS = 4
LRU_BW = LRU_WIDTH // LRU_BLOCKS
CONV_W = 4
CONV_LEFT = 2
LRU_C = 8.0
PEER_HEADS = 8
PEER_NKEYS = 128
PEER_NEXPERTS = PEER_NKEYS * PEER_NKEYS
PEER_DQ = 256
PEER_TOPK = 16
PEER_BLOCK = 128


def rms_norm(x, gain):
    xf = x.astype(jnp.float32)
    inv = lax.rsqrt(jnp.mean(xf * xf, axis=-1, keepdims=True) + EPS)
    return (xf * inv).astype(x.dtype) * gain

def hgrn2_chunk_scan(q, k, v, log_f):
    B, S, H, DK = q.shape
    DV = v.shape[-1]
    C = HG_CHUNK
    nc = S // C

    def to_chunks(t):
        return t.reshape(B, nc, C, H, t.shape[-1]).transpose(1, 0, 3, 2, 4)

    qc, kc, vc, gc = to_chunks(q), to_chunks(k), to_chunks(v), to_chunks(log_f)
    lower = jnp.tril(jnp.ones((C, C), dtype=bool))[:, :, None]

    def step(state, inp):
        qi, ki, vi, gi = inp
        b = jnp.cumsum(gi.astype(jnp.float32), axis=-2)
        b_last = b[..., -1:, :]
        rel = b[..., :, None, :] - b[..., None, :, :]
        decay = jnp.exp(jnp.where(lower, rel, -jnp.inf))
        attn = jnp.sum((qi[..., :, None, :] * ki[..., None, :, :]) * decay, axis=-1)
        o_intra = jnp.einsum('bhts,bhsv->bhtv', attn, vi)
        o_inter = jnp.einsum('bhtd,bhdv->bhtv', qi * jnp.exp(b), state)
        k_dec = ki * jnp.exp(b_last - b)
        new_state = state * jnp.exp(b_last[..., 0, :])[..., None] + jnp.einsum('bhsd,bhsv->bhdv', k_dec, vi)
        return new_state, o_intra + o_inter

    state0 = jnp.zeros((B, H, DK, DV), jnp.float32)
    _, o = lax.scan(step, state0, (qc, kc, vc, gc))
    return o.transpose(1, 0, 3, 2, 4).reshape(B, S, H, DV)

def hgrn2_mixer(h, w_in, lb, norm_g, w_out):
    B, S, _ = h.shape
    proj = h @ w_in
    q, f_fw, f_bw, i_in, g = jnp.split(proj, 5, axis=-1)

    def heads(t):
        return t.reshape(B, S, HG_HEADS, -1)

    q, v, g = heads(q), heads(i_in), heads(g)

    def gates(f_logit):
        f = lb + (1.0 - lb) * jax.nn.sigmoid(f_logit.astype(jnp.float32))
        return heads(jnp.log(f)), heads(1.0 - f)

    logf_fw, k_fw = gates(f_fw)
    logf_bw, k_bw = gates(f_bw)
    rev = lambda t: t[:, ::-1]
    o_fw = hgrn2_chunk_scan(q, k_fw, v, logf_fw)
    o_bw = rev(hgrn2_chunk_scan(rev(q), rev(k_bw), rev(v), rev(logf_bw)))
    o = rms_norm(o_fw + o_bw, norm_g.reshape(HG_HEADS, HG_DV)) * jax.nn.silu(g)
    return o.reshape(B, S, D_MODEL) @ w_out

def block_diag_linear(x, w, b):
    B, S, _ = x.shape
    xr = x.reshape(B, S, LRU_BLOCKS, LRU_BW)
    return jnp.einsum('bsnk,nkj->bsnj', xr, w).reshape(B, S, LRU_WIDTH) + b

def lin_combine(left, right):
    a_l, b_l = left
    a_r, b_r = right
    return a_l * a_r, a_r * b_l + b_r

def rglru_mixer(h, w_in, conv_w, conv_b, w_a, b_a, w_x, b_x, lam, w_out):
    B, S, _ = h.shape
    proj = h @ w_in
    xb, yb = jnp.split(proj, 2, axis=-1)
    y_gate = jax.nn.gelu(yb)
    xp = jnp.pad(xb, ((0, 0), (CONV_LEFT, CONV_W - 1 - CONV_LEFT), (0, 0)))
    xc = sum(xp[:, j:j + S] * conv_w[j] for j in range(CONV_W)) + conv_b

    def direction(d, reverse):
        r = jax.nn.sigmoid(block_diag_linear(xc, w_a[d], b_a[d]).astype(jnp.float32))
        ig = jax.nn.sigmoid(block_diag_linear(xc, w_x[d], b_x[d]).astype(jnp.float32))
        log_a = -LRU_C * r * jax.nn.softplus(-lam[d].astype(jnp.float32))
        a = jnp.exp(log_a)
        mult = jnp.sqrt(-jnp.expm1(2.0 * log_a))
        _, hs = lax.associative_scan(lin_combine, (a, mult * ig * xc), axis=1, reverse=reverse)
        return hs

    hsum = direction(0, False) + direction(1, True)
    return (hsum * y_gate) @ w_out

def peer_ffn(h, w_q, sub_keys, u_tab, v_tab):
    B, S, D = h.shape
    q = (h @ w_q).reshape(B, S, PEER_HEADS, 2, PEER_DQ // 2)
    scores = jnp.einsum('bshpd,hpkd->bshpk', q, sub_keys).astype(jnp.float32)
    s1, i1 = lax.top_k(scores[..., 0, :], PEER_TOPK)
    s2, i2 = lax.top_k(scores[..., 1, :], PEER_TOPK)
    cand_s = (s1[..., :, None] + s2[..., None, :]).reshape(B, S, PEER_HEADS, PEER_TOPK * PEER_TOPK)
    cand_id = (i1[..., :, None] * PEER_NKEYS + i2[..., None, :]).reshape(B, S, PEER_HEADS, PEER_TOPK * PEER_TOPK)
    top_s, top_pos = lax.top_k(cand_s, PEER_TOPK)
    ids = jnp.take_along_axis(cand_id, top_pos, axis=-1)
    gate = jax.nn.softmax(top_s, axis=-1)

    nb = (B * S) // PEER_BLOCK
    hb = h.reshape(nb, PEER_BLOCK, D)
    idb = ids.reshape(nb, PEER_BLOCK, PEER_HEADS, PEER_TOPK)
    gb = gate.reshape(nb, PEER_BLOCK, PEER_HEADS, PEER_TOPK)

    def block(args):
        hx, idx, g = args
        u = u_tab[idx]
        act = jax.nn.gelu(jnp.einsum('thkd,td->thk', u, hx).astype(jnp.float32))
        return jnp.einsum('thk,thkd->td', g * act, v_tab[idx])

    out = lax.map(block, (hb, idb, gb))
    return out.reshape(B, S, D)

def second_inputs(seed: int = 0) -> dict:
    key = jax.random.key(seed)
    ks = iter(jax.random.split(key, 32))
    D = D_MODEL

    def nrm(shape, scale):
        return jax.random.normal(next(ks), shape, jnp.float32) * scale

    x = nrm((BATCH, SEQ, D), 1.0)
    c = nrm((BATCH, D), 1.0)
    w_ada = nrm((DEPTH, D, 6 * D), 0.5 * D ** -0.5)
    b_ada = nrm((DEPTH, 6 * D), 0.02)
    norm_g = 1.0 + nrm((DEPTH, 2, D), 0.02)
    hg_w_in = nrm((N_A_LAYERS, D, 5 * D), D ** -0.5)
    hg_lb = nrm((N_A_LAYERS, D), 1.0)
    hg_norm_g = 1.0 + nrm((N_A_LAYERS, D), 0.02)
    hg_w_out = nrm((N_A_LAYERS, D, D), D ** -0.5)
    lru_w_in = nrm((N_B_LAYERS, D, 2 * LRU_WIDTH), D ** -0.5)
    lru_conv_w = nrm((N_B_LAYERS, CONV_W, LRU_WIDTH), 0.5)
    lru_conv_b = nrm((N_B_LAYERS, LRU_WIDTH), 0.02)
    lru_w_a = nrm((N_B_LAYERS, 2, LRU_BLOCKS, LRU_BW, LRU_BW), LRU_BW ** -0.5)
    lru_b_a = nrm((N_B_LAYERS, 2, LRU_WIDTH), 0.02)
    lru_w_x = nrm((N_B_LAYERS, 2, LRU_BLOCKS, LRU_BW, LRU_BW), LRU_BW ** -0.5)
    lru_b_x = nrm((N_B_LAYERS, 2, LRU_WIDTH), 0.02)
    a_c = jax.random.uniform(next(ks), (N_B_LAYERS, 2, LRU_WIDTH), jnp.float32, 0.9, 0.999)
    a_base = a_c ** (1.0 / LRU_C)
    lru_lam = jnp.log(a_base) - jnp.log1p(-a_base)
    lru_w_out = nrm((N_B_LAYERS, LRU_WIDTH, D), LRU_WIDTH ** -0.5)
    peer_w_q = nrm((DEPTH, D, PEER_HEADS * PEER_DQ), D ** -0.5)
    peer_keys = nrm((DEPTH, PEER_HEADS, 2, PEER_NKEYS, PEER_DQ // 2), (PEER_DQ // 2) ** -0.5)
    peer_u = nrm((DEPTH, PEER_NEXPERTS, D), D ** -0.5)
    peer_v = nrm((DEPTH, PEER_NEXPERTS, D), PEER_HEADS ** -0.5)
    final_g = 1.0 + nrm((D,), 0.02)
    return {"x": x, "c": c, "w_ada": w_ada, "b_ada": b_ada, "norm_g": norm_g,
            "hg_w_in": hg_w_in, "hg_lb": hg_lb, "hg_norm_g": hg_norm_g, "hg_w_out": hg_w_out,
            "lru_w_in": lru_w_in, "lru_conv_w": lru_conv_w, "lru_conv_b": lru_conv_b,
            "lru_w_a": lru_w_a, "lru_b_a": lru_b_a, "lru_w_x": lru_w_x, "lru_b_x": lru_b_x,
            "lru_lam": lru_lam, "lru_w_out": lru_w_out,
            "peer_w_q": peer_w_q, "peer_keys": peer_keys, "peer_u": peer_u, "peer_v": peer_v,
            "final_g": final_g}

def second_block(x, c, w_ada, b_ada, norm_g, hg_w_in, hg_lb, hg_norm_g, hg_w_out,
              lru_w_in, lru_conv_w, lru_conv_b, lru_w_a, lru_b_a, lru_w_x, lru_b_x,
              lru_lam, lru_w_out, peer_w_q, peer_keys, peer_u, peer_v, final_g):
    p = jax.nn.softmax(hg_lb.astype(jnp.float32), axis=0)
    lbs = jnp.cumsum(p, axis=0) - p[0]
    cond = jax.nn.silu(c)
    for i in range(DEPTH):
        mod = (cond @ w_ada[i] + b_ada[i])[:, None, :]
        sh1, sc1, g1, sh2, sc2, g2 = jnp.split(mod, 6, axis=-1)
        h = rms_norm(x, norm_g[i, 0]) * (1.0 + sc1) + sh1
        j = i // N_MIXERS
        if i % N_MIXERS == 0:
            y = hgrn2_mixer(h, hg_w_in[j], lbs[j], hg_norm_g[j], hg_w_out[j])
        else:
            y = rglru_mixer(h, lru_w_in[j], lru_conv_w[j], lru_conv_b[j], lru_w_a[j], lru_b_a[j],
                            lru_w_x[j], lru_b_x[j], lru_lam[j], lru_w_out[j])
        x = x + g1 * y
        h = rms_norm(x, norm_g[i, 1]) * (1.0 + sc2) + sh2
        x = x + g2 * peer_ffn(h, peer_w_q[i], peer_keys[i], peer_u[i], peer_v[i])
    return rms_norm(x, final_g)


def setup_inputs(seed=0):
    out = dict(first_inputs(seed))
    for name, value in second_inputs(seed + 1).items():
        if name != "x":
            out[name + "_2"] = value
    return out


def reference(
    x, norm_g, w_in, conv_w, conv_b, conv_ln_g, conv_ln_b, conv_pw_w, conv_pw_b, q_norm_g, w_uq,
    kv_norm_g, w_ukv, qk_q_g, qk_k_g, sg_ln_g, sg_ln_b, sg_w, sg_b, branch_norm_g, w_out, c_2,
    w_ada_2, b_ada_2, norm_g_2, hg_w_in_2, hg_lb_2, hg_norm_g_2, hg_w_out_2, lru_w_in_2,
    lru_conv_w_2, lru_conv_b_2, lru_w_a_2, lru_b_a_2, lru_w_x_2, lru_b_x_2, lru_lam_2,
    lru_w_out_2, peer_w_q_2, peer_keys_2, peer_u_2, peer_v_2, final_g_2,
):
    x = first_block(
        x, norm_g, w_in, conv_w, conv_b, conv_ln_g, conv_ln_b, conv_pw_w, conv_pw_b, q_norm_g,
        w_uq, kv_norm_g, w_ukv, qk_q_g, qk_k_g, sg_ln_g, sg_ln_b, sg_w, sg_b, branch_norm_g,
        w_out,
    )
    return second_block(
        x, c_2, w_ada_2, b_ada_2, norm_g_2, hg_w_in_2, hg_lb_2, hg_norm_g_2, hg_w_out_2,
        lru_w_in_2, lru_conv_w_2, lru_conv_b_2, lru_w_a_2, lru_b_a_2, lru_w_x_2, lru_b_x_2,
        lru_lam_2, lru_w_out_2, peer_w_q_2, peer_keys_2, peer_u_2, peer_v_2, final_g_2,
    )


_drawn_inputs = setup_inputs


def setup_inputs(seed=0):
    import zlib

    import numpy as np

    out = dict(_drawn_inputs(seed))
    spreads = {}
    factors = {'conv_b': 4.064,
     'conv_ln_g': 3.832,
     'conv_ln_b': 7.373,
     'conv_pw_b': 5.03,
     'q_norm_g': 3.666,
     'qk_q_g': 3.71,
     'qk_k_g': 4.058,
     'sg_ln_g': 8.0,
     'sg_ln_b': 8.0,
     'norm_g_2': 5.044,
     'hg_norm_g_2': 8.0,
     'lru_conv_b_2': 2.864,
     'lru_b_a_2': 41.224,
     'lru_b_x_2': 32.484,
     'final_g_2': 8.646}
    for name, (base, spread) in spreads.items():
        noise = np.random.default_rng([zlib.crc32(name.encode()), seed]).standard_normal(out[name].shape)
        drawn = base * np.exp(spread * noise) if base else spread * noise
        out[name] = __import__('jax').numpy.asarray(drawn.astype(out[name].dtype))
    for name, factor in factors.items():
        out[name] = (out[name] * factor).astype(out[name].dtype)
    return out
```

```python
from contextlib import ExitStack, contextmanager

import numpy as np

import concourse.bass as bass
from concourse import mybir

F32 = mybir.dt.float32
U32 = mybir.dt.uint32
I32 = mybir.dt.int32
U8 = mybir.dt.uint8
ALU = mybir.AluOpType
ACT = mybir.ActivationFunctionType
AX = mybir.AxisListType

P = 128
SEQ = 256
TT = SEQ // P
D = 1024
KD = D // P
DEPTH = 2
EPS = 1e-6
NEG = -1e30

CONV_W = 256
CONV_K = 31
HEADS = 8
NOPE = 64
ROPE = 32
HALF = ROPE // 2
QK = NOPE + ROPE
VD = 64
MLA_W = HEADS * VD
Q_LORA = 768
KV_LORA = 256
SG_W = 256
SG_HEADS = 4
SG_D = SG_W // SG_HEADS

C_ZCONV = 2 * CONV_W
C_CQ = 3 * CONV_W
C_ROWS = C_CQ + Q_LORA + KV_LORA
IN_COLS = C_ROWS + ROPE + MLA_W + 3 * SG_W
N_ROWS = IN_COLS - C_ROWS
R_ROPE, R_ZMLA, R_U = 0, ROPE, ROPE + MLA_W
R_V, R_ZSG = R_U + SG_W, R_U + 2 * SG_W

STAGE_SEMS = 28


class Names:
    pass


class Link:

    def __init__(self, engine, sem, base=0):
        self.engine, self.sem, self.base, self.n = engine, sem, base, 0

    def __call__(self, instruction):
        instruction.then_inc(self.sem, 1)
        self.n += 1
        self.engine.wait_ge(self.sem, self.base + self.n)
        return instruction


class Area:

    def __init__(self, arena, at=0):
        self.arena, self.at = arena, at

    def take(self, *dims, parts=P):
        n = int(np.prod(dims))
        piece = self.arena[0:parts, self.at:self.at + n]
        self.at += n + n % 2
        if len(dims) == 1:
            return piece
        names = "abcd"[:len(dims)]
        sizes = {c: d for c, d in zip(names, dims)}
        return piece.rearrange(f"p ({' '.join(names)}) -> p {' '.join(names)}", **sizes)


class Stages:

    def __init__(self, nc):
        self.nc, self.turn = nc, 0
        self.banks = []
        for b in range(2):
            handles = [nc.alloc_semaphore(f"stage_bank{b}_{i}") for i in range(STAGE_SEMS)]
            self.banks.append(handles)

    @contextmanager
    def open(self):
        nc = self.nc
        idle, mine = self.banks[1 - self.turn], list(self.banks[self.turn])
        nums = sorted(s.num for s in idle)
        assert nums == list(range(nums[0], nums[0] + STAGE_SEMS))
        nc.gpsimd.sem_clear(range(nums[0], nums[-1] + 1))
        with nc.Block(no_gpsimd_drain=True) as block:
            yield block, (lambda name: mine.pop(0))
        self.turn = 1 - self.turn


def load_cols(dma, out, src, chunks):
    return dma(out, src.rearrange("a (k p) -> p (a k)", k=chunks))


def cast_rows(src):
    return src.broadcast_to([P, src.shape[1]])



class NormTranspose:

    def __init__(self, K, sem, area):
        self.K = K
        self.xn = area.take(TT, D)
        self.sq = area.take(D)
        self.stat = area.take(3, TT)
        self.ms_ready = sem("ms_ready")
        self.var_ready = sem("var_ready")
        self.sd_ready = sem("sd_ready")
        self.xn_ready = sem("xn_ready")
        self.xt_ready = sem("xt_ready")

    def act(self, act):
        K, nc = self.K, self.K.nc
        for t in range(TT):
            nc.scalar.activation(self.xn[:, t], K.x[:, t], ACT.Square,
                                 accum_out=self.stat[:, 0, t:t + 1]).then_inc(self.ms_ready, 1)
        act.wait_ge(self.var_ready, 1)
        nc.scalar.activation(self.stat[:, 2], self.stat[:, 1], ACT.Sqrt).then_inc(self.sd_ready, 1)

    def dve_norm(self, dve, link):
        K, nc = self.K, self.K.nc
        dve.wait_ge(self.ms_ready, TT)
        nc.vector.tensor_scalar(self.stat[:, 1], self.stat[:, 0], 1.0 / D, EPS, ALU.mult,
                                ALU.add).then_inc(self.var_ready, 1)
        dve.wait_ge(self.sd_ready, 1)
        link(nc.vector.reciprocal(self.stat[:, 0], self.stat[:, 2]))
        for t in range(TT):
            nc.vector.tensor_scalar(self.xn[:, t], K.x[:, t], self.stat[:, 0, t:t + 1], None,
                                    ALU.mult).then_inc(self.xn_ready, 1)

    def pe(self, pe):
        K, nc = self.K, self.K.nc
        for t in range(TT):
            pe.wait_ge(self.xn_ready, t + 1)
            for k in range(KD):
                last = nc.tensor.transpose(K.ps_low[:, k, t * P:(t + 1) * P],
                                           self.xn[:, t, k * P:(k + 1) * P], K.ident[:])
            last.then_inc(self.xt_ready, 1)

    def dve_scale(self, dve, gain, shift, h_ready):
        K, nc = self.K, self.K.nc
        dve.wait_ge(self.xt_ready, TT)
        for k in range(KD):
            if shift is None:
                ins = nc.vector.tensor_scalar(K.h_t[:, k], K.ps_low[:, k], gain[:, k:k + 1], None,
                                              ALU.mult)
            else:
                ins = nc.vector.tensor_scalar(K.h_t[:, k], K.ps_low[:, k], gain[:, k:k + 1],
                                              shift[:, k:k + 1], ALU.mult, ALU.add)
            ins.then_inc(h_ready, 1)


def matmul_rows(nc, out, lhs_t, w, t, chunks):
    for k in range(chunks):
        last = nc.tensor.matmul(out, lhs_t[:, k, t * P:(t + 1) * P], w[:, k],
                                start=(k == 0), stop=(k == chunks - 1))
    return last


def matmul_cols(nc, out, w, rhs_t, c, chunks):
    for k in range(chunks):
        last = nc.tensor.matmul(out, w[:, k, c * P:(c + 1) * P], rhs_t[:, k],
                                start=(k == 0), stop=(k == chunks - 1))
    return last



def stage_setup(K, S):
    nc = K.nc
    with S.open() as (block, sem):
        loaded, zeroed, made = sem("loaded"), sem("zeroed"), sem("made")

        @block.sync
        def _(sp):
            sp.dma_start(K.x[:], K.i["x"].rearrange("b (t p) d -> p (b t) d", p=P)).then_inc(loaded, 16)
            sp.dma_start(K.invf[:], K.i["inv_freq"].broadcast_to([P, HALF])).then_inc(loaded, 16)
            sp.wait_ge(loaded, 32)

        @block.gpsimd
        def _(pool):
            nc.gpsimd.memset(K.ident[:], 0.0)
            nc.gpsimd.memset(K.ones[:], 1.0)
            nc.gpsimd.memset(K.causal[:], 0.0)
            nc.gpsimd.iota(K.pos[:], pattern=[[P, TT]], base=0, channel_multiplier=1,
                           allow_small_or_imprecise_dtypes=True).then_inc(zeroed, 1)
            pool.wait_ge(zeroed, 1)
            nc.gpsimd.affine_select(out=K.ident[:], in_=K.ident[:], compare_op=ALU.not_equal,
                                    fill=1.0, base=0, pattern=[[-1, P]], channel_multiplier=1)
            nc.gpsimd.affine_select(out=K.causal[:], in_=K.causal[:], compare_op=ALU.is_ge,
                                    fill=NEG, base=0, pattern=[[-1, P]],
                                    channel_multiplier=1).then_inc(made, 1)
            pool.wait_ge(made, 1)


def stage_rope_tables(K, S):
    nc = K.nc
    two_pi = 2 * np.pi
    hi = float(np.float32(6.28125))
    mid = float(np.float32(np.round((two_pi - hi) * 2**20) / 2**20))
    low = float(np.float32(two_pi - hi - mid))
    with S.open() as (block, sem):
        chain, angle_ready, sin_done = sem("chain"), sem("angle_ready"), sem("sin_done")
        area = Area(K.arena)
        ang, turns, red, whole = (area.take(TT, HALF) for _ in range(4))
        whole_i = whole.bitcast(I32)

        @block.vector
        def _(dve):
            link = Link(dve, chain)
            for t in range(TT):
                link(nc.vector.tensor_scalar(ang[:, t], K.invf[:], K.pos[:, t:t + 1], None, ALU.mult))
            for n, (table, shift) in enumerate(((K.sin, 0.0), (K.cos, 0.25))):
                link(nc.vector.tensor_scalar(turns, ang, 1.0 / two_pi, shift, ALU.mult, ALU.add))
                link(nc.vector.tensor_copy(whole_i, turns))
                link(nc.vector.tensor_copy(turns, whole_i))
                link(nc.vector.scalar_tensor_tensor(red, turns, -hi, ang, ALU.mult, ALU.add))
                link(nc.vector.scalar_tensor_tensor(red, turns, -mid, red, ALU.mult, ALU.add))
                link(nc.vector.scalar_tensor_tensor(red, turns, -low, red, ALU.mult, ALU.add))
                if shift:
                    link(nc.vector.tensor_scalar(red, red, float(np.pi / 2), None, ALU.add))
                link(nc.vector.tensor_scalar(table[:], red, float(-np.pi), float(np.pi), ALU.max, ALU.min))
            dve.sem_inc(angle_ready, 1)

        @block.scalar
        def _(act):
            act.wait_ge(angle_ready, 1)
            nc.scalar.activation(K.sin[:], K.sin[:], ACT.Sin)
            nc.scalar.activation(K.cos[:], K.cos[:], ACT.Sin).then_inc(sin_done, 1)
            act.wait_ge(sin_done, 1)



IN_BLOCKS = [("cols", 0, 512), ("rows", C_ZCONV, 256), ("cols", C_CQ, 512),
             ("cols", C_CQ + 512, 512), ("rows", C_ROWS, 512), ("rows", C_ROWS + 512, 512),
             ("rows", C_ROWS + 1024, N_ROWS - 1024)]


def stage_in_projection(K, S, l):
    nc, i = K.nc, K.i
    with S.open() as (block, sem):
        area = Area(K.arena, K.first_end)
        norm = NormTranspose(K, sem, area)
        chain, params, h_ready = sem("chain"), sem("params"), sem("h_ready")
        w_loaded = [sem("w_loaded0"), sem("w_loaded1")]
        proj_ready, proj_out = sem("proj_ready"), sem("proj_out")

        @block.sync
        def _(sp):
            at = {}
            for n, (_, c0, width) in enumerate(IN_BLOCKS):
                if n >= 2:
                    sp.wait_ge(proj_ready, n - 1)
                src = i["w_in"][bass.ds(l, 1), :, c0:c0 + width].rearrange("a (k p) n -> p (a k) n", p=P)
                sp.dma_start(K.wslot[n % 2][:, :, 0:width], src).then_inc(w_loaded[n % 2], 16)

        @block.scalar
        def _(act):
            norm.act(act)
            load = lambda out, name, chunks: load_cols(
                act.dma_start, out, K.layer(name, l), chunks).then_inc(params, 16)
            load(K.g_norm[:], "norm_g", KD)
            load(K.g_q[:], "q_norm_g", Q_LORA // P)
            load(K.g_kv[:], "kv_norm_g", KV_LORA // P)
            load(K.cb[:, 0], "conv_b", 2)
            load(K.cb[:, 1], "conv_ln_g", 2)
            load(K.cb[:, 2], "conv_ln_b", 2)
            load(K.g_branch[:], "branch_norm_g", KD)
            for c in range(2):
                act.dma_start(K.cw[:, c], i["conv_w"][bass.ds(l, 1), :, c * P:(c + 1) * P].rearrange(
                    "a k p -> p (a k)")).then_inc(params, 16)
            act.dma_start(K.sgb[:], i["sg_b"][bass.ds(l, 1)].rearrange("a g t -> t (a g)")).then_inc(params, 16)
            act.dma_start(K.sgw[:], i["sg_w"][bass.ds(l, 1)].rearrange("a g t s -> t (a g) s")).then_inc(params, 16)
            for out, name in ((K.pwb, "conv_pw_b"), (K.gqk[:, 0], "qk_q_g"), (K.gqk[:, 1], "qk_k_g"),
                              (K.sgln[:, 0], "sg_ln_g"), (K.sgln[:, 1], "sg_ln_b")):
                act.dma_start(out,
                               cast_rows(K.layer(name, l))).then_inc(params, 16)

        @block.tensor
        def _(pe):
            norm.pe(pe)
            for n, (kind, c0, width) in enumerate(IN_BLOCKS):
                pe.wait_ge(w_loaded[n % 2], 16 * (n // 2 + 1))
                if n == 0:
                    pe.wait_ge(h_ready, KD)
                if n >= 2:
                    pe.wait_ge(proj_out, n - 1)
                w, ps = K.wslot[n % 2], K.ps_pair[n % 2]
                if kind == "cols":
                    for c in range(width // P):
                        last = matmul_cols(nc, ps[:, c // 2, (c % 2) * SEQ:(c % 2 + 1) * SEQ], w,
                                           K.h_t, c, KD)
                else:
                    for t in range(TT):
                        last = matmul_rows(nc, ps[:, t, 0:width], K.h_t, w[:, :, 0:width], t, KD)
                last.then_inc(proj_ready, 1)

        @block.vector
        def _(dve):
            link = Link(dve, chain)
            norm.dve_norm(dve, link)
            dve.wait_ge(params, 16 * 16)
            norm.dve_scale(dve, K.g_norm, None, h_ready)
            for n, (kind, c0, width) in enumerate(IN_BLOCKS):
                dve.wait_ge(proj_ready, n + 1)
                ps = K.ps_pair[n % 2]
                if kind == "cols":
                    dst = K.glu if c0 == 0 else K.low[:, (c0 - C_CQ) // P:(c0 - C_CQ) // P + 4]
                    ins = nc.vector.tensor_copy(dst.rearrange("p c t -> p (c t)"),
                                                ps.rearrange("p b n -> p (b n)"))
                elif c0 == C_ZCONV:
                    ins = nc.vector.tensor_copy(K.zconv, ps[:, :, 0:width])
                else:
                    ins = nc.vector.tensor_copy(K.rows[:, :, c0 - C_ROWS:c0 - C_ROWS + width],
                                                ps[:, :, 0:width])
                ins.then_inc(proj_out, 1)


def stage_conv(K, S, l):
    nc, i = K.nc, K.i
    with S.open() as (block, sem):
        area = Area(K.arena, K.first_end)
        padded = area.take(2, SEQ + CONV_K - 1)
        gate, acc, xc, sq, rstd = (area.take(2, SEQ) for _ in range(5))
        sz = area.take(TT, CONV_W)
        chain, pw_loaded, gate_ready, acc_ready = sem("chain"), sem("pw_loaded"), sem("gate"), sem("acc")
        mean_ready, xc_ready, sq_ready, var_ready = sem("mean"), sem("xc"), sem("sq"), sem("var")
        veps_ready, sd_ready, ln_ready, silu_ready = sem("veps"), sem("sd"), sem("ln"), sem("silu")
        pw_ready = sem("pw_ready")
        pw = K.ring[:, 0:2 * CONV_W].rearrange("p (k n) -> p k n", k=2)
        mean_ps, var_ps = K.ps[:, 0, 0:SEQ], K.ps[:, 1, 0:SEQ]
        out_ps = K.ps[:, 2:4, 0:CONV_W]

        @block.sync
        def _(sp):
            sp.dma_start(pw, i["conv_pw_w"][bass.ds(l, 1)].rearrange("a (k p) n -> p (a k) n", p=P)
                         ).then_inc(pw_loaded, 16)

        @block.scalar
        def _(act):
            nc.scalar.activation(gate, K.glu[:, 2:4], ACT.Sigmoid).then_inc(gate_ready, 1)
            act.wait_ge(xc_ready, 1)
            nc.scalar.activation(sq, xc, ACT.Square).then_inc(sq_ready, 1)
            act.wait_ge(veps_ready, 1)
            nc.scalar.activation(rstd[:, 1], rstd[:, 0], ACT.Sqrt).then_inc(sd_ready, 1)
            act.wait_ge(ln_ready, 1)
            for c in range(2):
                nc.scalar.activation(acc[:, c], xc[:, c], ACT.Silu, bias=K.cb[:, 2, c:c + 1],
                                     scale=K.cb[:, 1, c:c + 1]).then_inc(silu_ready, 1)
            nc.scalar.activation(sz, K.zconv, ACT.Silu).then_inc(silu_ready, 1)

        @block.tensor
        def _(pe):
            pe.wait_ge(acc_ready, 1)
            for c in range(2):
                last = nc.tensor.matmul(mean_ps, K.ones[:], acc[:, c], start=(c == 0), stop=(c == 1))
            last.then_inc(mean_ready, 1)
            pe.wait_ge(sq_ready, 1)
            for c in range(2):
                last = nc.tensor.matmul(var_ps, K.ones[:], sq[:, c], start=(c == 0), stop=(c == 1))
            last.then_inc(var_ready, 1)
            pe.wait_ge(pw_loaded, 16)
            pe.wait_ge(silu_ready, 2)
            for t in range(TT):
                last = matmul_rows(nc, out_ps[:, t], acc, pw, t, 2)
            last.then_inc(pw_ready, 1)

        @block.vector
        def _(dve):
            link = Link(dve, chain)
            nc.vector.memset(padded[:, :, 0:CONV_K - 1], 0.0)
            dve.wait_ge(gate_ready, 1)
            link(nc.vector.tensor_tensor(padded[:, :, CONV_K - 1:], K.glu[:, 0:2], gate, ALU.mult))
            for j in range(CONV_K):
                for c in range(2):
                    w = K.cw[:, c, j:j + 1]
                    if j == 0:
                        ins = nc.vector.tensor_scalar(acc[:, c], padded[:, c, 0:SEQ], w,
                                                      K.cb[:, 0, c:c + 1], ALU.mult, ALU.add)
                    else:
                        ins = nc.vector.scalar_tensor_tensor(acc[:, c], padded[:, c, j:j + SEQ], w,
                                                             acc[:, c], ALU.mult, ALU.add)
                    if c == 1 and j < CONV_K - 1:
                        link(ins)
            ins.then_inc(acc_ready, 1)
            dve.wait_ge(mean_ready, 1)
            for c in range(2):
                ins = nc.vector.scalar_tensor_tensor(xc[:, c], mean_ps, -1.0 / CONV_W, acc[:, c],
                                                     ALU.mult, ALU.add)
            ins.then_inc(xc_ready, 1)
            dve.wait_ge(var_ready, 1)
            nc.vector.tensor_scalar(rstd[:, 0], var_ps, 1.0 / CONV_W, EPS, ALU.mult,
                                    ALU.add).then_inc(veps_ready, 1)
            dve.wait_ge(sd_ready, 1)
            link(nc.vector.reciprocal(rstd[:, 0], rstd[:, 1]))
            for c in range(2):
                ins = nc.vector.tensor_tensor(xc[:, c], xc[:, c], rstd[:, 0], ALU.mult)
            ins.then_inc(ln_ready, 1)
            dve.wait_ge(silu_ready, 3)
            dve.wait_ge(pw_ready, 1)
            for t in range(TT):
                link(nc.vector.tensor_tensor(K.y[:, t, 0:CONV_W], out_ps[:, t], K.pwb[:], ALU.add))
            link(nc.vector.tensor_tensor(K.y[:, :, 0:CONV_W], K.y[:, :, 0:CONV_W], sz, ALU.mult))


def rms_rstd_dve(nc, link, out, sums, n):
    return nc.vector.tensor_scalar(out, sums, 1.0 / n, EPS, ALU.mult, ALU.add)


def stage_mla_heads(K, S, l):
    nc, i = K.nc, K.i
    NQ, NKV = Q_LORA // P, KV_LORA // P
    with S.open() as (block, sem):
        area = Area(K.arena, K.first_end)
        sq = area.take(NQ + NKV, SEQ)
        q = area.take(TT, HEADS, QK)
        k = area.take(TT, HEADS, QK)
        hsq = area.take(TT, HEADS, QK)
        rot = area.take(4, TT, HEADS, HALF)
        st = area.take(3, 2, TT)
        hst = area.take(3, 2, TT * HEADS)
        chain, w_loaded, sq_ready, st_ready = sem("chain"), sem("w_loaded"), sem("sq"), sem("st")
        scaled, vst_ready, sd_ready, up_ready = sem("scaled"), sem("vst"), sem("sd"), sem("up")
        hv_ready, hsd_ready, qk_ready, tr_ready = sem("hv"), sem("hsd"), sem("qk"), sem("tr")
        tr_out, act_chain = sem("tr_out"), sem("act_chain")
        w_uq = K.ring[:, 0:NQ * HEADS * QK].rearrange("p (k n) -> p k n", k=NQ)
        w_ukv = K.ring[:, NQ * HEADS * QK:NQ * HEADS * QK + NKV * 1024].rearrange("p (k n) -> p k n", k=NKV)
        st_ps = K.ps[:, 7]

        @block.sync
        def _(sp):
            sp.dma_start(w_uq, i["w_uq"][bass.ds(l, 1)].rearrange("a (k p) n -> p (a k) n", p=P)
                         ).then_inc(w_loaded, 16)
            sp.dma_start(w_ukv, i["w_ukv"][bass.ds(l, 1)].rearrange("a (k p) n -> p (a k) n", p=P)
                         ).then_inc(w_loaded, 16)

        @block.scalar
        def _(act):
            nc.scalar.activation(sq, K.low, ACT.Square).then_inc(sq_ready, 1)
            act.wait_ge(sq_ready, 1)
            for c in range(NQ + NKV):
                g = K.g_q[:, c:c + 1] if c < NQ else K.g_kv[:, c - NQ:c - NQ + 1]
                nc.scalar.activation(K.low[:, c], K.low[:, c], ACT.Copy, scale=g).then_inc(scaled, 1)
            act.wait_ge(vst_ready, 1)
            nc.scalar.activation(st[:, 2], st[:, 1], ACT.Sqrt).then_inc(sd_ready, 1)
            act.wait_ge(hv_ready, 1)
            nc.scalar.activation(hst[:, 2], hst[:, 1], ACT.Sqrt).then_inc(hsd_ready, 1)

        @block.tensor
        def _(pe):
            pe.wait_ge(sq_ready, 1)
            for n, (c0, c1) in enumerate(((0, NQ), (NQ, NQ + NKV))):
                for t in range(TT):
                    for c in range(c0, c1):
                        last = nc.tensor.matmul(st_ps[:, n * TT + t:n * TT + t + 1],
                                                sq[:, c, t * P:(t + 1) * P], K.ones[:, 0:1],
                                                start=(c == c0), stop=(c == c1 - 1))
            last.then_inc(st_ready, 1)
            pe.wait_ge(w_loaded, 32)
            pe.wait_ge(scaled, NQ + NKV)
            pe.wait_ge(vst_ready, 1)
            for t in range(TT):
                for half in range(2):
                    matmul_rows(nc, K.ps[:, 4 * t + half, 0:4 * QK], K.low[:, 0:NQ],
                                w_uq[:, :, half * 4 * QK:(half + 1) * 4 * QK], t, NQ)
                for half in range(2):
                    last = matmul_rows(nc, K.ps[:, 4 * t + 2 + half], K.low[:, NQ:],
                                       w_ukv[:, :, half * 512:(half + 1) * 512], t, NKV)
                last.then_inc(up_ready, 1)
            for n, src in enumerate((q, k)):
                pe.wait_ge(qk_ready, n + 1)
                for h in range(HEADS):
                    b = (n * 4 + h // 2)
                    for t in range(TT):
                        last = nc.tensor.transpose(
                            K.ps[0:QK, b, (h % 2) * SEQ + t * P:(h % 2) * SEQ + (t + 1) * P],
                            src[:, t, h], K.ident[:])
                    if h % 2:
                        last.then_inc(tr_ready, 1)

        @block.vector
        def _(dve):
            link = Link(dve, chain)
            dve.wait_ge(st_ready, 1)
            for n, width in enumerate((Q_LORA, KV_LORA)):
                ins = nc.vector.tensor_scalar(st[:, 1, n], st_ps[:, n * TT:(n + 1) * TT], 1.0 / width,
                                              EPS, ALU.mult, ALU.add)
                if n == 0:
                    link(ins)
            ins.then_inc(vst_ready, 1)
            dve.wait_ge(sd_ready, 1)
            link(nc.vector.reciprocal(st[:, 0], st[:, 2]))
            for t in range(TT):
                dve.wait_ge(up_ready, t + 1)
                for half in range(2):
                    hs = slice(4 * half, 4 * half + 4)
                    nc.vector.tensor_scalar(
                        q[:, t, hs].rearrange("p h d -> p (h d)"), K.ps[:, 4 * t + half, 0:4 * QK],
                        st[:, 0, 0, t:t + 1], None, ALU.mult)
                    kv = K.ps[:, 4 * t + 2 + half].rearrange("p (h d) -> p h d", h=4)
                    nc.vector.tensor_scalar(k[:, t, hs, 0:NOPE], kv[:, :, 0:NOPE],
                                            st[:, 0, 1, t:t + 1], None, ALU.mult)
                    nc.vector.tensor_scalar(K.v[:, t, hs], kv[:, :, NOPE:], st[:, 0, 1, t:t + 1],
                                            None, ALU.mult)
                link(nc.vector.tensor_copy(
                    k[:, t, :, NOPE:],
                    K.rows[:, t, R_ROPE:R_ROPE + ROPE].unsqueeze(1).broadcast_to([P, HEADS, ROPE])))
            flat = lambda a: a.rearrange("p t h d -> p (t h) d")
            for n, src in enumerate((q, k)):
                link(nc.vector.tensor_tensor(hsq, src, src, ALU.mult))
                link(nc.vector.tensor_reduce(hst[:, 0, n], flat(hsq), AX.X, ALU.add))
            nc.vector.tensor_scalar(hst[:, 1], hst[:, 0], 1.0 / QK, EPS, ALU.mult,
                                    ALU.add).then_inc(hv_ready, 1)
            dve.wait_ge(hsd_ready, 1)
            link(nc.vector.reciprocal(hst[:, 0], hst[:, 2]))
            for n, src in enumerate((q, k)):
                link(nc.vector.tensor_tensor(
                    flat(src), flat(src),
                    hst[:, 0, n].unsqueeze(2).broadcast_to([P, TT * HEADS, QK]), ALU.mult))
                link(nc.vector.tensor_tensor(
                    flat(src), flat(src),
                    K.gqk[:, n].unsqueeze(1).broadcast_to([P, TT * HEADS, QK]), ALU.mult))
                for t in range(TT):
                    x1, x2 = src[:, t, :, NOPE:NOPE + HALF], src[:, t, :, NOPE + HALF:]
                    cos = K.cos[:, t].unsqueeze(1).broadcast_to([P, HEADS, HALF])
                    sin = K.sin[:, t].unsqueeze(1).broadcast_to([P, HEADS, HALF])
                    nc.vector.tensor_tensor(rot[:, 0, t], x1, cos, ALU.mult)
                    nc.vector.tensor_tensor(rot[:, 1, t], x2, sin, ALU.mult)
                    nc.vector.tensor_tensor(rot[:, 2, t], x1, sin, ALU.mult)
                    link(nc.vector.tensor_tensor(rot[:, 3, t], x2, cos, ALU.mult))
                    nc.vector.tensor_tensor(x1, rot[:, 0, t], rot[:, 1, t], ALU.subtract)
                    ins = nc.vector.tensor_tensor(x2, rot[:, 2, t], rot[:, 3, t], ALU.add)
                    if t == 0:
                        link(ins)
                link(ins)
                dve.sem_inc(qk_ready, 1)
            for n, dst in enumerate((K.q_t, K.k_t)):
                for b in range(4):
                    dve.wait_ge(tr_ready, n * 4 + b + 1)
                    nc.vector.tensor_copy(dst[0:QK, 2 * b:2 * b + 2].rearrange("p h t -> p (h t)"),
                                          K.ps[0:QK, n * 4 + b]).then_inc(tr_out, 1)
            dve.wait_ge(tr_out, 8)


def stage_attention(K, S, l):
    nc = K.nc
    scale = float(QK) ** -0.5
    with S.open() as (block, sem):
        area = Area(K.arena, K.first_end)
        s = area.take(2, 4, SEQ)
        mx = area.take(2, 4)
        sums = area.take(TT, HEADS)
        p_t = area.take(2, 4, TT, P)
        sz = area.take(TT, MLA_W)
        chain, s_ready, s_out = sem("chain"), sem("s_ready"), sem("s_out")
        e_ready, pt_ready, pt_out, o_ready = sem("e_ready"), sem("pt_ready"), sem("pt_out"), sem("o_ready")
        silu_ready, max_ready = sem("silu_ready"), sem("max_ready")
        groups = [(t, g) for t in range(TT) for g in range(2)]

        def s_ps(n, keys):
            return K.ps[:, 2 * (n % 2):2 * (n % 2) + 2].rearrange("p b (h c) -> p (b h) c", h=2)[:, :, 0:keys]

        @block.tensor
        def _(pe):
            def scores(n):
                t, g = groups[n]
                if n >= 2:
                    pe.wait_ge(s_out, n - 1)
                for h in range(4):
                    last = nc.tensor.matmul(s_ps(n, (t + 1) * P)[:, h],
                                            K.q_t[0:QK, 4 * g + h, t * P:(t + 1) * P],
                                            K.k_t[0:QK, 4 * g + h, 0:(t + 1) * P], start=True, stop=True)
                last.then_inc(s_ready, 1)

            scores(0)
            for n, (t, g) in enumerate(groups):
                if n + 1 < len(groups):
                    scores(n + 1)
                pe.wait_ge(e_ready, 4 * (n + 1))
                if n >= 1:
                    pe.wait_ge(pt_out, n)
                for h in range(4):
                    for kt in range(t + 1):
                        last = nc.tensor.transpose(
                            K.ps[:, 4 + h // 2, (h % 2) * SEQ + kt * P:(h % 2) * SEQ + (kt + 1) * P],
                            s[:, n % 2, h, kt * P:(kt + 1) * P], K.ident[:])
                last.then_inc(pt_ready, 1)
                pe.wait_ge(pt_out, n + 1)
                for h in range(4):
                    for kt in range(t + 1):
                        last = nc.tensor.matmul(K.ps[:, 6 + t, (4 * g + h) * VD:(4 * g + h + 1) * VD],
                                                p_t[:, n % 2, h, kt], K.v[:, kt, 4 * g + h],
                                                start=(kt == 0), stop=(kt == t))
                last.then_inc(o_ready, 1)

        @block.scalar
        def _(act):
            nc.scalar.activation(sz, K.rows[:, :, R_ZMLA:R_ZMLA + MLA_W], ACT.Silu).then_inc(silu_ready, 1)
            for n, (t, g) in enumerate(groups):
                keys = (t + 1) * P
                act.wait_ge(max_ready, n + 1)
                for h in range(4):
                    nc.scalar.activation(s[:, n % 2, h, 0:keys], s[:, n % 2, h, 0:keys], ACT.Exp,
                                         bias=mx[:, n % 2, h:h + 1],
                                         accum_out=sums[:, t, 4 * g + h:4 * g + h + 1]
                                         ).then_inc(e_ready, 1)

        @block.vector
        def _(dve):
            link = Link(dve, chain)

            def probabilities_out(n):
                t, g = groups[n]
                dve.wait_ge(pt_ready, n + 1)
                if n >= 2:
                    dve.wait_ge(o_ready, n - 1)
                src = K.ps[:, 4:6].rearrange("p b (h c) -> p (b h) c", h=2)[:, :, 0:(t + 1) * P]
                nc.vector.tensor_copy(p_t[:, n % 2].rearrange("p h a b -> p h (a b)")[:, :, 0:(t + 1) * P],
                                      src).then_inc(pt_out, 1)

            for n, (t, g) in enumerate(groups):
                keys = (t + 1) * P
                dve.wait_ge(s_ready, n + 1)
                if n >= 2:
                    dve.wait_ge(pt_ready, n - 1)
                if t:
                    nc.vector.tensor_scalar(s[:, n % 2, :, 0:t * P], s_ps(n, keys)[:, :, 0:t * P], scale,
                                            None, ALU.mult)
                link(nc.vector.scalar_tensor_tensor(
                    s[:, n % 2, :, t * P:keys], s_ps(n, keys)[:, :, t * P:keys], scale,
                    K.causal[:].unsqueeze(1).broadcast_to([P, 4, P]), ALU.mult, ALU.add))
                dve.sem_inc(s_out, 1)
                if n >= 2:
                    dve.wait_ge(e_ready, 4 * (n - 1))
                link(nc.vector.tensor_reduce(mx[:, n % 2], s[:, n % 2, :, 0:keys], AX.X, ALU.max))
                nc.vector.tensor_scalar(mx[:, n % 2], mx[:, n % 2], -1.0, None,
                                        ALU.mult).then_inc(max_ready, 1)
                if n >= 1:
                    probabilities_out(n - 1)
            probabilities_out(len(groups) - 1)
            dve.wait_ge(o_ready, 4)
            dve.wait_ge(silu_ready, 1)
            link(nc.vector.reciprocal(sums, sums))
            for t in range(TT):
                y = K.y[:, t, CONV_W:CONV_W + MLA_W]
                link(nc.vector.tensor_tensor(
                    y.rearrange("p (h d) -> p h d", h=HEADS),
                    K.ps[:, 6 + t].rearrange("p (h d) -> p h d", h=HEADS),
                    sums[:, t].unsqueeze(2).broadcast_to([P, HEADS, VD]), ALU.mult))
                link(nc.vector.tensor_tensor(y, y, sz[:, t], ALU.mult))


def stage_sgu(K, S, l):
    nc = K.nc
    with S.open() as (block, sem):
        area = Area(K.arena, K.first_end)
        u, v, sz, mixed = (area.take(TT, SG_W) for _ in range(4))
        w_t = area.take(SG_HEADS, P)
        bn = area.take(TT, 6)
        mv = area.take(TT, 2)
        sd = area.take(TT, 2)
        chain, act_done, veps, sd_ready = sem("chain"), sem("act_done"), sem("veps"), sem("sd")
        w_ready, w_out, w_kept, v_ready, mix_ready = (sem("w_ready"), sem("w_out"), sem("w_kept"),
                                                      sem("v_ready"), sem("mix_ready"))

        @block.scalar
        def _(act):
            nc.scalar.activation(v, K.rows[:, :, R_V:R_V + SG_W], ACT.Gelu_apprx_tanh).then_inc(act_done, 1)
            nc.scalar.activation(u, K.rows[:, :, R_U:R_U + SG_W], ACT.Gelu_apprx_tanh).then_inc(act_done, 1)
            act.wait_ge(veps, 1)
            nc.scalar.activation(sd[:, :, 1], sd[:, :, 0], ACT.Sqrt).then_inc(sd_ready, 1)
            nc.scalar.activation(sz, K.rows[:, :, R_ZSG:R_ZSG + SG_W], ACT.Silu).then_inc(act_done, 1)

        @block.gpsimd
        def _(pool):
            pool.wait_ge(w_out, 1)
            nc.gpsimd.affine_select(out=w_t, in_=w_t, compare_op=ALU.is_ge, fill=0.0, base=0,
                                    pattern=[[0, SG_HEADS], [1, P]], channel_multiplier=-1).then_inc(w_kept, 1)

        @block.tensor
        def _(pe):
            for g in range(SG_HEADS):
                last = nc.tensor.transpose(K.ps[:, 0, g * P:(g + 1) * P], K.sgw[:, g], K.ident[:])
            last.then_inc(w_ready, 1)
            pe.wait_ge(w_kept, 1)
            pe.wait_ge(v_ready, 1)
            for t in range(TT):
                for g in range(SG_HEADS):
                    last = nc.tensor.matmul(K.ps[:, 1 + t, g * SG_D:(g + 1) * SG_D], w_t[:, g],
                                            v[:, t, g * SG_D:(g + 1) * SG_D], start=True, stop=True)
            last.then_inc(mix_ready, 1)

        @block.vector
        def _(dve):
            link = Link(dve, chain)
            dve.wait_ge(w_ready, 1)
            nc.vector.tensor_copy(w_t.rearrange("p g s -> p (g s)"), K.ps[:, 0]).then_inc(w_out, 1)
            dve.wait_ge(act_done, 1)
            for t in range(TT):
                link(nc.vector.bn_stats(bn[:, t], v[:, t]))
                link(nc.vector.bn_aggr(mv[:, t], bn[:, t]))
            nc.vector.tensor_scalar(sd[:, :, 0], mv[:, :, 1], EPS, None, ALU.add).then_inc(veps, 1)
            dve.wait_ge(sd_ready, 1)
            link(nc.vector.reciprocal(sd[:, :, 0], sd[:, :, 1]))
            for t in range(TT):
                link(nc.vector.tensor_scalar(v[:, t], v[:, t], mv[:, t, 0:1], sd[:, t, 0:1],
                                             ALU.subtract, ALU.mult))
                link(nc.vector.tensor_tensor(v[:, t], v[:, t], K.sgln[:, 0], ALU.mult))
                link(nc.vector.tensor_tensor(v[:, t], v[:, t], K.sgln[:, 1], ALU.add))
            dve.sem_inc(v_ready, 1)
            dve.wait_ge(act_done, 3)
            link(nc.vector.tensor_tensor(u, u, sz, ALU.mult))
            dve.wait_ge(mix_ready, 1)
            for t in range(TT):
                link(nc.vector.tensor_tensor(
                    mixed[:, t].rearrange("p (g d) -> p g d", g=SG_HEADS),
                    K.ps[:, 1 + t, 0:SG_W].rearrange("p (g d) -> p g d", g=SG_HEADS),
                    K.sgb[:].unsqueeze(2).broadcast_to([P, SG_HEADS, SG_D]), ALU.add))
                link(nc.vector.tensor_tensor(K.y[:, t, CONV_W + MLA_W:], mixed[:, t], u[:, t], ALU.mult))


BRANCHES = ((0, CONV_W), (CONV_W, CONV_W + MLA_W), (CONV_W + MLA_W, D))


def stage_out_projection(K, S, l):
    nc, i = K.nc, K.i
    with S.open() as (block, sem):
        area = Area(K.arena, K.first_end)
        sq = area.take(TT, D)
        st = area.take(3, 3, TT)
        chain, w_loaded, ms_ready, var_ready = sem("chain"), sem("w_loaded"), sem("ms"), sem("var")
        sd_ready, yn_ready, yt_ready, y_out, o_ready = (sem("sd"), sem("yn"), sem("yt"), sem("y_out"),
                                                        sem("o_ready"))
        w = K.ring[:, 0:KD * D].rearrange("p (k n) -> p k n", k=KD)

        @block.sync
        def _(sp):
            sp.dma_start(w, i["w_out"][bass.ds(l, 1)].rearrange("a (k p) n -> p (a k) n", p=P)
                         ).then_inc(w_loaded, 16)

        @block.scalar
        def _(act):
            for b, (c0, c1) in enumerate(BRANCHES):
                for t in range(TT):
                    nc.scalar.activation(sq[:, t, c0:c1], K.y[:, t, c0:c1], ACT.Square,
                                         accum_out=st[:, 0, b, t:t + 1]).then_inc(ms_ready, 1)
            act.wait_ge(var_ready, 1)
            nc.scalar.activation(st[:, 2], st[:, 1], ACT.Sqrt).then_inc(sd_ready, 1)

        @block.tensor
        def _(pe):
            pe.wait_ge(yn_ready, 1)
            for k in range(KD):
                for t in range(TT):
                    last = nc.tensor.transpose(K.ps_low[:, k, t * P:(t + 1) * P],
                                               K.y[:, t, k * P:(k + 1) * P], K.ident[:])
                last.then_inc(yt_ready, 1)
            pe.wait_ge(w_loaded, 16)
            pe.wait_ge(y_out, KD)
            for t in range(TT):
                for half in range(2):
                    last = matmul_rows(nc, K.ps[:, 4 + 2 * t + half], K.h_t,
                                       w[:, :, half * 512:(half + 1) * 512], t, KD)
                last.then_inc(o_ready, 1)

        @block.vector
        def _(dve):
            link = Link(dve, chain)
            dve.wait_ge(ms_ready, 6)
            for b, (c0, c1) in enumerate(BRANCHES):
                link(nc.vector.tensor_scalar(st[:, 1, b], st[:, 0, b], 1.0 / (c1 - c0), EPS, ALU.mult,
                                             ALU.add))
            dve.sem_inc(var_ready, 1)
            dve.wait_ge(sd_ready, 1)
            link(nc.vector.reciprocal(st[:, 0], st[:, 2]))
            for b, (c0, c1) in enumerate(BRANCHES):
                for t in range(TT):
                    link(nc.vector.tensor_scalar(K.y[:, t, c0:c1], K.y[:, t, c0:c1],
                                                 st[:, 0, b, t:t + 1], None, ALU.mult))
            dve.sem_inc(yn_ready, 1)
            for k in range(KD):
                dve.wait_ge(yt_ready, 2 * (k // 2) + 2)
                nc.vector.tensor_scalar(K.h_t[:, k], K.ps_low[:, k], K.g_branch[:, k:k + 1], None,
                                        ALU.mult).then_inc(y_out, 1)
            for t in range(TT):
                dve.wait_ge(o_ready, t + 1)
                link(nc.vector.tensor_tensor(
                    K.x[:, t], K.x[:, t],
                    K.ps[:, 4 + 2 * t:6 + 2 * t].rearrange("p b n -> p (b n)"), ALU.add))


def first_block(K, S):
    with K.nc.Fori(0, DEPTH) as l:
        stage_in_projection(K, S, l)
        stage_conv(K, S, l)
        stage_mla_heads(K, S, l)
        stage_attention(K, S, l)
        stage_sgu(K, S, l)
        stage_out_projection(K, S, l)



D5 = 5 * D
HG = 8
HD = D // HG
CH = SEQ // P
PRE = P + 1
LEVELS = [64, 32, 16, 8, 4, 2, 1]
LRU_BLOCKS = 4
LRU_BW = D // LRU_BLOCKS
TAPS = 4
LEFT = 2
LRU_C = 8.0
PH = 8
NKEYS = 128
TOPK = 16
HP = 2 * PH
BIG = 3.0e38


def stage_modulation(K, S, l):
    nc, i = K.nc, K.i
    with S.open() as (block, sem):
        area = Area(K.arena)
        mod = area.take(6, D)
        diag = area.take(KD, P)
        cols = area.take(4, KD)
        cc = area.take(KD)
        cb = area.take(KD, P)
        gains = area.take(2, KD)
        chain, loaded, b_loaded, c_ready, cb_ready = (sem("chain"), sem("loaded"), sem("b_loaded"),
                                                      sem("c_ready"), sem("cb_ready"))
        w_loaded = [sem("w_loaded0"), sem("w_loaded1")]
        half_done, half_out = sem("half_done"), sem("half_out")

        @block.sync
        def _(sp):
            def load(n, half):
                src = i["w_ada_2"][l, :, bass.ds(n * D + half * 512, 512)]
                sp.dma_start(K.wslot[half], src.rearrange("(k p) n -> p k n", p=P)).then_inc(w_loaded[half], 16)

            for half in range(2):
                load(0, half)
            with sp.Fori(0, 5) as n:
                for half in range(2):
                    sp.wait_ge(half_done, 2 * n + half + 1)
                    load(n + 1, half)

        @block.scalar
        def _(act):
            load_cols(act.dma_start, cc, i["c_2"], KD).then_inc(loaded, 16)
            for n in range(2):
                load_cols(act.dma_start, gains[:, n], i["norm_g_2"][l, n:n + 1], KD).then_inc(loaded, 16)
            act.dma_start(mod.rearrange("p v d -> p (v d)"),
                          i["b_ada_2"][l:l + 1].broadcast_to([P, 6 * D])).then_inc(b_loaded, 16)
            act.wait_ge(loaded, 48)
            nc.scalar.activation(cc, cc, ACT.Silu).then_inc(c_ready, 1)

        @block.tensor
        def _(pe):
            pe.wait_ge(cb_ready, 1)

            def vector(n, wait_out):
                for half in range(2):
                    pe.wait_ge(w_loaded[half], 16 * (n + 1))
                    if wait_out is not None:
                        pe.wait_ge(half_out, wait_out + half)
                    for k in range(KD):
                        last = nc.tensor.matmul(K.ps[:, half], cb[:, k], K.wslot[half][:, k],
                                                start=(k == 0), stop=(k == KD - 1))
                    last.then_inc(half_done, 1)

            vector(0, None)
            with pe.Fori(1, 6) as n:
                vector(n, 2 * n - 1)

        @block.vector
        def _(dve):
            link = Link(dve, chain)
            dve.wait_ge(c_ready, 1)
            nc.vector.tensor_copy(cb, cc.unsqueeze(2).broadcast_to([P, KD, P])).then_inc(cb_ready, 1)
            dve.wait_ge(b_loaded, 16)
            flat = mod.rearrange("p v d -> p (v d)")
            with dve.Fori(0, 6) as n:
                for half in range(2):
                    dve.wait_ge(half_done, 2 * n + half + 1)
                    piece = flat[:, bass.ds(n * D + half * 512, 512)]
                    nc.vector.tensor_tensor(piece, piece, K.ps[:, half], ALU.add).then_inc(half_out, 1)
            dve.wait_ge(half_out, 12)
            for n, v in enumerate((2, 5)):
                nc.vector.tensor_copy(K.gate[:, n], mod[:, v])
            for n, v in enumerate((0, 1, 3, 4)):
                link(nc.vector.tensor_tensor(diag, mod[:, v].rearrange("p (k c) -> p k c", k=KD),
                                             K.ident[:].unsqueeze(1).broadcast_to([P, KD, P]), ALU.mult))
                link(nc.vector.tensor_reduce(cols[:, n], diag, AX.X, ALU.add))
            for n in range(2):
                nc.vector.tensor_copy(K.shift[:, n], cols[:, 2 * n])
                link(nc.vector.scalar_tensor_tensor(K.gain[:, n], cols[:, 2 * n + 1], 1.0, gains[:, n],
                                                    ALU.add, ALU.mult))


def stage_projection(K, S, gain, shift, source, blocks, area_at):
    nc = K.nc
    with S.open() as (block, sem):
        norm = NormTranspose(K, sem, Area(K.arena, area_at))
        chain, h_ready = sem("chain"), sem("h_ready")
        w_loaded = [sem("w_loaded0"), sem("w_loaded1")]
        proj_ready, proj_out = sem("proj_ready"), sem("proj_out")

        @block.sync
        def _(sp):
            for n, (_, c0, _) in enumerate(blocks):
                if n >= 2:
                    sp.wait_ge(proj_ready, n - 1)
                sp.dma_start(K.wslot[n % 2], source[:, c0:c0 + 512].rearrange("(k p) n -> p k n", p=P)
                             ).then_inc(w_loaded[n % 2], 16)

        @block.scalar
        def _(act):
            norm.act(act)

        @block.tensor
        def _(pe):
            norm.pe(pe)
            pe.wait_ge(h_ready, KD)
            for n, (kind, _, _) in enumerate(blocks):
                pe.wait_ge(w_loaded[n % 2], 16 * (n // 2 + 1))
                if n >= 2:
                    pe.wait_ge(proj_out, n - 1)
                w, ps = K.wslot[n % 2], K.ps_pair[n % 2]
                if kind == "cols":
                    for c in range(4):
                        last = matmul_cols(nc, ps[:, c // 2, (c % 2) * SEQ:(c % 2 + 1) * SEQ], w,
                                           K.h_t, c, KD)
                else:
                    for t in range(TT):
                        last = matmul_rows(nc, ps[:, t], K.h_t, w, t, KD)
                last.then_inc(proj_ready, 1)

        @block.vector
        def _(dve):
            link = Link(dve, chain)
            norm.dve_norm(dve, link)
            norm.dve_scale(dve, gain, shift, h_ready)
            for n, (kind, _, dst) in enumerate(blocks):
                dve.wait_ge(proj_ready, n + 1)
                ps = K.ps_pair[n % 2]
                if kind == "cols":
                    ps = ps.rearrange("p b (c t) -> p (b c) t", c=2)
                nc.vector.tensor_copy(dst, ps).then_inc(proj_out, 1)


def residual_out(K, dve, link, w_gate, o_ready, tmp):
    nc = K.nc
    for t in range(TT):
        dve.wait_ge(o_ready, t + 1)
        link(nc.vector.tensor_tensor(tmp, K.ps[:, 4 + 2 * t:6 + 2 * t].rearrange("p b n -> p (b n)"),
                                     w_gate, ALU.mult))
        link(nc.vector.tensor_tensor(K.x[:, t], K.x[:, t], tmp, ALU.add))


def product_out(K, pe, w, o_ready):
    for t in range(TT):
        for half in range(2):
            last = matmul_rows(K.nc, K.ps[:, 4 + 2 * t + half], K.h_t, w[:, :, half * 512:(half + 1) * 512],
                               t, KD)
        last.then_inc(o_ready, 1)



def hg_memory(K):
    area = Area(K.arena)
    H = Names()
    H.q = area.take(HG, CH, P)
    H.k = area.take(2, HG, CH, P)
    H.v = area.take(TT, D)
    H.g = area.take(TT, D)
    H.pre = area.take(2, HG * CH, PRE)
    H.at = area.take(HG, 4, P)
    H.masks = area.take(HG * P // 4).bitcast(U8).rearrange("p (l t) -> p l t", l=8)
    H.end = area.at
    return H


def stage_hg_gates(K, S, H):
    nc, i = K.nc, K.i
    with S.open() as (block, sem):
        area = Area(K.arena, H.end)
        lb = area.take(4, HG)
        carry = area.take(HG * CH, PRE)
        px = area.take(P).bitcast(I32)
        tx = area.take(P).bitcast(I32)
        m = area.take(P).bitcast(I32)
        chain, loaded, iotas, sig_ready = sem("chain"), sem("loaded"), sem("iotas"), sem("sig")
        lb_ready, exp_ready, f_ready, ln_ready = sem("lb"), sem("exp"), sem("f"), sem("ln")
        k_flat = H.k.rearrange("p d h c t -> p (d h c t)")

        @block.sync
        def _(sp):
            load_cols(sp.dma_start, lb[:, 0], i["hg_lb_2"], HG).then_inc(loaded, 16)

        @block.gpsimd
        def _(pool):
            nc.gpsimd.memset(carry, 1.0).then_inc(iotas, 1)
            nc.gpsimd.iota(px, pattern=[[0, P]], base=0, channel_multiplier=1).then_inc(iotas, 1)
            nc.gpsimd.iota(tx, pattern=[[1, P]], base=0, channel_multiplier=0).then_inc(iotas, 1)
            pool.wait_ge(iotas, 3)
            nc.gpsimd.memset(carry[:, :, 0:1], 0.0).then_inc(iotas, 1)

        @block.scalar
        def _(act):
            nc.scalar.activation(k_flat, k_flat, ACT.Sigmoid).then_inc(sig_ready, 1)
            act.wait_ge(lb_ready, 1)
            nc.scalar.activation(lb[:, 2], lb[:, 1], ACT.Exp).then_inc(exp_ready, 1)
            act.wait_ge(f_ready, 1)
            for d in range(2):
                nc.scalar.activation(H.pre[:, d, :, 1:], H.k[:, d].rearrange("p h c t -> p (h c) t"),
                                     ACT.Ln).then_inc(ln_ready, 1)

        @block.vector
        def _(dve):
            link = Link(dve, chain)
            dve.wait_ge(loaded, 16)
            nc.vector.tensor_tensor(lb[:, 1], lb[:, 0], lb[:, 0], ALU.subtract).then_inc(lb_ready, 1)
            dve.wait_ge(exp_ready, 1)
            link(nc.vector.reciprocal(lb[:, 3], lb[:, 2]))
            link(nc.vector.tensor_tensor(lb[:, 3], lb[:, 3], lb[:, 2], ALU.mult))
            link(nc.vector.tensor_tensor(lb[:, 0], lb[:, 3], lb[:, 3], ALU.subtract))
            link(nc.vector.tensor_scalar(lb[:, 1], lb[:, 0], -1.0, 1.0, ALU.mult, ALU.add))
            dve.wait_ge(sig_ready, 1)
            for d in range(2):
                for h in range(HG):
                    f = H.k[:, d, h].rearrange("p c t -> p (c t)")
                    ins = nc.vector.tensor_scalar(f, f, lb[:, 1, h:h + 1], lb[:, 0, h:h + 1], ALU.mult,
                                                  ALU.add)
            ins.then_inc(f_ready, 1)
            dve.wait_ge(iotas, 4)
            link(nc.vector.tensor_tensor(m, px, tx, ALU.bitwise_xor))
            link(nc.vector.memset(H.pre[:, :, :, 0:1], 0.0))
            dve.wait_ge(ln_ready, 2)
            for d in range(2):
                flat = H.pre[:, d].rearrange("p n t -> p (n t)")
                nc.vector.tensor_tensor_scan(flat, carry.rearrange("p n t -> p (n t)"), flat, 0.0,
                                             ALU.mult, ALU.add)
            link(nc.vector.tensor_scalar(k_flat, k_flat, -1.0, 1.0, ALU.mult, ALU.add))
            for n, L in enumerate(LEVELS):
                link(nc.vector.tensor_scalar(px, m, float(L), None, ALU.is_ge))
                link(nc.vector.scalar_tensor_tensor(H.masks[:, n], m, float(2 * L), px, ALU.is_lt, ALU.mult))
            link(nc.vector.tensor_scalar(H.masks[:, 7], m, 0.0, None, ALU.is_equal))


def stage_hg_attention(K, S, H):
    nc = K.nc
    NL = len(LEVELS)
    with S.open() as (block, sem):
        area = Area(K.arena, H.end)
        kq = area.take(2, 2, HG * CH * P)
        chain, exps, exp_done, pair_ready = sem("chain"), sem("exps"), sem("exp_done"), sem("pair_ready")
        a_ready, a_out = sem("a_ready"), sem("a_out")
        pool_chain = sem("pool_chain")
        q = H.q.rearrange("p h c t -> p (h c) t")
        kf, kb = (H.k[:, d].rearrange("p h c t -> p (h c) t") for d in range(2))
        kk = H.k
        pf, pb = H.pre[:, 0], H.pre[:, 1]

        def halves(a, L):
            return a.rearrange("p n (b s j) -> p n b s j", s=2, j=L)

        def middle(pre, L):
            m = pre[:, :, 0:P].rearrange("p n (b s j) -> p n b s j", s=2, j=L)[:, :, :, 1, 0:1]
            return m.broadcast_to([P, HG * CH, P // (2 * L), L])

        @block.vector
        def _(dve):
            link = Link(dve, chain)

            def exponents(n):
                if n >= 2:
                    dve.wait_ge(a_ready, n - 1)
                L = LEVELS[n]
                ek, eq = (kq[:, n % 2, w].rearrange("p (n t) -> p n t", t=P) for w in range(2))
                ek, eq = halves(ek, L), halves(eq, L)
                inc = lambda pre: pre[:, :, 1:].rearrange("p n (b s j) -> p n b s j", s=2, j=L)
                exc = lambda pre: pre[:, :, 0:P].rearrange("p n (b s j) -> p n b s j", s=2, j=L)
                nc.vector.tensor_tensor(ek[:, :, :, 0], middle(pf, L), inc(pf)[:, :, :, 0], ALU.subtract)
                nc.vector.tensor_tensor(ek[:, :, :, 1], exc(pb)[:, :, :, 1], middle(pb, L), ALU.subtract)
                nc.vector.tensor_tensor(eq[:, :, :, 1], inc(pf)[:, :, :, 1], middle(pf, L), ALU.subtract)
                nc.vector.tensor_tensor(eq[:, :, :, 0], middle(pb, L), exc(pb)[:, :, :, 0],
                                        ALU.subtract).then_inc(exps, 1)

            def factors(n):
                L = LEVELS[n]
                dve.wait_ge(exp_done, n + 1)
                ek, eq = (kq[:, n % 2, w].rearrange("p (n t) -> p n t", t=P) for w in range(2))
                ekh = halves(ek, L)
                nc.vector.tensor_tensor(ekh[:, :, :, 0], ekh[:, :, :, 0], halves(kf, L)[:, :, :, 0], ALU.mult)
                nc.vector.tensor_tensor(ekh[:, :, :, 1], ekh[:, :, :, 1], halves(kb, L)[:, :, :, 1], ALU.mult)
                nc.vector.tensor_tensor(eq, eq, q, ALU.mult).then_inc(pair_ready, 1)

            def take(n):
                dve.wait_ge(a_ready, n + 1)
                if n >= 1:
                    dve.wait_ge(a_out, n)
                for b in range(4):
                    src = K.ps[:, 4 * (n % 2) + b].rearrange("p (h c t) -> p h c t", h=2, c=CH)
                    mask = H.masks[:, n].unsqueeze(1).broadcast_to([P, CH, P])
                    for h in range(2):
                        ins = nc.vector.copy_predicated(H.at[:, 2 * b + h, 0:4:3], mask, src[:, h])
                ins.then_inc(a_out, 1)

            exponents(0)
            for n in range(NL):
                if n + 1 < NL:
                    exponents(n + 1)
                factors(n)
                if n >= 1:
                    take(n - 1)
            dve.wait_ge(a_ready, NL - 1)
            nc.vector.tensor_tensor(kq[:, NL % 2, 0].rearrange("p (n t) -> p n t", t=P), kf, kb,
                                    ALU.add).then_inc(pair_ready, 1)
            take(NL - 1)
            e = kq[:, (NL + 1) % 2].rearrange("p w (h c t) -> p w h c t", h=HG, c=CH)
            pre = H.pre.rearrange("p d (h c) t -> p d h c t", c=CH)
            end_f = pre[:, 0, :, 0, P:].broadcast_to([P, HG, P])
            end_b = pre[:, 1, :, 0, P:].broadcast_to([P, HG, P])
            nc.vector.tensor_tensor(e[:, 0, :, 0], end_f, pre[:, 0, :, 0, 1:], ALU.subtract)
            nc.vector.tensor_copy(e[:, 0, :, 1], pre[:, 1, :, 1, 0:P])
            nc.vector.tensor_copy(e[:, 1, :, 1], pre[:, 0, :, 1, 1:])
            nc.vector.tensor_tensor(e[:, 1, :, 0], end_b, pre[:, 1, :, 0, 0:P], ALU.subtract).then_inc(exps, 1)
            take(NL)
            dve.wait_ge(exp_done, NL + 1)
            nc.vector.tensor_tensor(e[:, 0, :, 0], e[:, 0, :, 0], kk[:, 0, :, 0], ALU.mult)
            nc.vector.tensor_tensor(e[:, 0, :, 1], e[:, 0, :, 1], kk[:, 1, :, 1], ALU.mult)
            nc.vector.tensor_tensor(e[:, 1], e[:, 1], H.q, ALU.mult).then_inc(pair_ready, 1)
            dve.wait_ge(a_ready, NL + 2)
            b0 = 4 * ((NL + 1) % 2)
            src = K.ps[:, b0:b0 + 4].rearrange("p b (h c t) -> p (b h) c t", h=2, c=CH)
            for h in range(HG):
                ins = nc.vector.tensor_copy(H.at[:, h, 1:3], src[:, h])
            link(ins)

        @block.scalar
        def _(act):
            for n in range(NL + 1):
                act.wait_ge(exps, n + 1)
                b = n % 2 if n < NL else (NL + 1) % 2
                flat = kq[:, b].rearrange("p w n -> p (w n)")
                nc.scalar.activation(flat, flat, ACT.Exp).then_inc(exp_done, 1)

        @block.tensor
        def _(pe):
            for n in range(NL + 2):
                pe.wait_ge(pair_ready, n + 1)
                if n >= 2:
                    pe.wait_ge(a_out, n - 1)
                b = n % 2
                keys = kq[:, b, 0].rearrange("p (h c t) -> p h c t", h=HG, c=CH)
                queries = (kq[:, b, 1].rearrange("p (h c t) -> p h c t", h=HG, c=CH) if n != NL else H.q)
                for h in range(HG):
                    for c in range(CH):
                        cq = c if n <= NL else 1 - c
                        o = K.ps[:, 4 * (n % 2) + h // 2, ((h % 2) * 2 + c) * P:((h % 2) * 2 + c + 1) * P]
                        last = nc.tensor.matmul(o, keys[:, h, c], queries[:, h, cq], start=True, stop=True)
                last.then_inc(a_ready, 1)


def stage_hg_out(K, S, H):
    nc, i = K.nc, K.i
    with S.open() as (block, sem):
        area = Area(K.arena, H.end)
        o = area.take(TT, D)
        sq = area.take(TT, D)
        gain = area.take(D)
        st = area.take(3, TT, HG)
        chain, w_loaded, g_loaded, silu_ready = sem("chain"), sem("w_loaded"), sem("g_loaded"), sem("silu")
        o_ready, sq_ready, v_ready, sd_ready = sem("o_ready"), sem("sq"), sem("veps"), sem("sd")
        oc_ready, y_ready, yt_ready, yt_out, p_ready = (sem("oc"), sem("y"), sem("yt"), sem("yt_out"),
                                                        sem("p_ready"))
        w = K.ring[:].rearrange("p (k n) -> p k n", k=KD)

        @block.sync
        def _(sp):
            sp.dma_start(gain, i["hg_norm_g_2"].broadcast_to([P, D])).then_inc(g_loaded, 16)
            sp.dma_start(w, i["hg_w_out_2"][0].rearrange("(k p) n -> p k n", p=P)).then_inc(w_loaded, 16)

        @block.tensor
        def _(pe):
            for t in range(TT):
                for h in range(HG):
                    for s in range(TT):
                        last = nc.tensor.matmul(K.ps[:, 2 * t + h // 4, (h % 4) * P:(h % 4 + 1) * P],
                                                H.at[:, h, 2 * s + t], H.v[:, s, h * P:(h + 1) * P],
                                                start=(s == 0), stop=(s == 1))
                last.then_inc(o_ready, 1)
            for t in range(TT):
                pe.wait_ge(y_ready, t + 1)
                for k in range(KD):
                    last = nc.tensor.transpose(K.ps_low[:, k, t * P:(t + 1) * P],
                                               o[:, t, k * P:(k + 1) * P], K.ident[:])
            last.then_inc(yt_ready, 1)
            pe.wait_ge(w_loaded, 16)
            pe.wait_ge(yt_out, 1)
            product_out(K, pe, w, p_ready)

        @block.scalar
        def _(act):
            nc.scalar.activation(H.g, H.g, ACT.Silu).then_inc(silu_ready, 1)
            for t in range(TT):
                act.wait_ge(oc_ready, t + 1)
                nc.scalar.activation(sq[:, t], o[:, t], ACT.Square).then_inc(sq_ready, 1)
            act.wait_ge(v_ready, 1)
            nc.scalar.activation(st[:, 2], st[:, 1], ACT.Sqrt).then_inc(sd_ready, 1)

        @block.vector
        def _(dve):
            link = Link(dve, chain)
            for t in range(TT):
                dve.wait_ge(o_ready, t + 1)
                nc.vector.tensor_copy(o[:, t], K.ps[:, 2 * t:2 * t + 2].rearrange("p b n -> p (b n)")
                                      ).then_inc(oc_ready, 1)
            for t in range(TT):
                dve.wait_ge(sq_ready, t + 1)
                link(nc.vector.tensor_reduce(st[:, 0, t], sq[:, t].rearrange("p (h d) -> p h d", h=HG), AX.X,
                                             ALU.add))
            nc.vector.tensor_scalar(st[:, 1], st[:, 0], 1.0 / HD, EPS, ALU.mult, ALU.add).then_inc(v_ready, 1)
            dve.wait_ge(silu_ready, 1)
            dve.wait_ge(g_loaded, 16)
            for t in range(TT):
                link(nc.vector.tensor_tensor(H.g[:, t], H.g[:, t], gain, ALU.mult))
            dve.wait_ge(sd_ready, 1)
            link(nc.vector.reciprocal(st[:, 0], st[:, 2]))
            for t in range(TT):
                link(nc.vector.tensor_tensor(
                    o[:, t].rearrange("p (h d) -> p h d", h=HG), o[:, t].rearrange("p (h d) -> p h d", h=HG),
                    st[:, 0, t].unsqueeze(2).broadcast_to([P, HG, HD]), ALU.mult))
                nc.vector.tensor_tensor(o[:, t], o[:, t], H.g[:, t], ALU.mult).then_inc(y_ready, 1)
            dve.wait_ge(yt_ready, 1)
            nc.vector.tensor_copy(K.h_t[:].rearrange("p k t -> p (k t)"),
                                  K.ps_low.rearrange("p k t -> p (k t)")).then_inc(yt_out, 1)
            residual_out(K, dve, link, K.gate[:, 0], p_ready, sq[:, 0])


def hg_mixer(K, S):
    H = hg_memory(K)
    src = K.i["hg_w_in_2"][0]
    blocks = []
    for half in range(2):
        hs = slice(4 * half, 4 * half + 4)
        blocks.append(("cols", half * 512, H.q[:, hs].rearrange("p h c t -> p h (c t)")))
        for d in range(2):
            blocks.append(("cols", (1 + d) * D + half * 512, H.k[:, d, hs].rearrange("p h c t -> p h (c t)")))
        blocks.append(("rows", 3 * D + half * 512, H.v[:, :, half * 512:(half + 1) * 512]))
        blocks.append(("rows", 4 * D + half * 512, H.g[:, :, half * 512:(half + 1) * 512]))
    stage_projection(K, S, K.gain[:, 0], K.shift[:, 0], src, blocks, H.end)
    stage_hg_gates(K, S, H)
    stage_hg_attention(K, S, H)
    stage_hg_out(K, S, H)



def stage_lru(K, S, xb, yb, at):
    nc, i = K.nc, K.i
    with S.open() as (block, sem):
        area = Area(K.arena, at)
        padded = area.take(KD, SEQ + TAPS - 1)
        xc, r, th, ig, bb, aa = (area.take(KD, SEQ) for _ in range(6))
        hs = area.take(2, KD, SEQ)
        w = area.take(KD, D)
        cw = area.take(TAPS, KD)
        cb = area.take(KD)
        bias = area.take(4, KD)
        lam, ex, u, u2, poly = (area.take(2, KD) for _ in range(5))
        tmp = r.rearrange("p k t -> p (k t)")[:, 0:D]
        chain, loaded, wg_loaded, w_loaded = sem("chain"), sem("loaded"), sem("wg_loaded"), sem("w_loaded")
        z_ready, e_ready, xc_ready, g_ready = sem("z"), sem("e"), sem("xc"), sem("g")
        sig_done, nsp_ready, at_done = sem("sig"), sem("nsp"), sem("at")
        m_ready, sq_done, gelu_done, y_ready, o_ready = (sem("m"), sem("sq"), sem("gelu"), sem("y"),
                                                         sem("o"))
        th_used = sem("th_used")
        wg = K.ring[:].rearrange("p (w n j) -> p w n j", w=2, n=16)

        @block.sync
        def _(sp):
            for n, gate_w in enumerate((i["lru_w_a_2"], i["lru_w_x_2"])):
                src = gate_w[0].rearrange("d b (k p) j -> p (d b k) j", p=P)
                sp.dma_start(wg[:, n], src).then_inc(wg_loaded, 16)
            sp.dma_start(w, i["lru_w_out_2"][0].rearrange("(k p) n -> p k n", p=P)).then_inc(w_loaded, 16)

        @block.scalar
        def _(act):
            for j in range(TAPS):
                load_cols(act.dma_start, cw[:, j], i["lru_conv_w_2"][0, j:j + 1], KD).then_inc(loaded, 16)
            load_cols(act.dma_start, cb, i["lru_conv_b_2"], KD).then_inc(loaded, 16)
            for d in range(2):
                load_cols(act.dma_start, bias[:, 2 * d], i["lru_b_a_2"][0, d:d + 1], KD).then_inc(loaded, 16)
                load_cols(act.dma_start, bias[:, 2 * d + 1], i["lru_b_x_2"][0, d:d + 1], KD).then_inc(loaded, 16)
                load_cols(act.dma_start, lam[:, d], i["lru_lam_2"][0, d:d + 1], KD).then_inc(loaded, 16)
            act.wait_ge(z_ready, 1)
            nc.scalar.activation(ex, u, ACT.Exp).then_inc(e_ready, 1)
            for d in range(2):
                for which, dst in enumerate((r, ig)):
                    act.wait_ge(g_ready, 2 * d + which + 1)
                    if d == 1 and which == 0:
                        act.wait_ge(at_done, 1)
                    if d == 1 and which == 1:
                        act.wait_ge(th_used, 1)
                    for c in range(KD):
                        src = K.ps[:, 4 * which + c // 2, (c % 2) * SEQ:(c % 2 + 1) * SEQ]
                        ins = nc.scalar.activation(dst[:, c], src, ACT.Sigmoid,
                                                   bias=bias[:, 2 * d + which, c:c + 1])
                ins.then_inc(sig_done, 1)
                act.wait_ge(sig_done, d + 1)
                act.wait_ge(nsp_ready, 1)
                if d == 1:
                    act.wait_ge(th_used, 1)
                for c in range(KD):
                    nc.scalar.activation(th[:, c], r[:, c], ACT.Tanh, scale=lam[:, d, c:c + 1])
                    ins = nc.scalar.activation(aa[:, c], r[:, c], ACT.Exp, scale=lam[:, d, c:c + 1])
                ins.then_inc(at_done, 1)
                act.wait_ge(m_ready, d + 1)
                nc.scalar.activation(th, th, ACT.Sqrt).then_inc(sq_done, 1)
            nc.scalar.activation(yb, yb, ACT.Gelu_apprx_tanh).then_inc(gelu_done, 1)

        @block.tensor
        def _(pe):
            pe.wait_ge(wg_loaded, 32)
            pe.wait_ge(xc_ready, 1)
            for d in range(2):
                for which in range(2):
                    if d == 1:
                        pe.wait_ge(sig_done, 1)
                    for c in range(KD):
                        for kk in range(2):
                            n = (d * LRU_BLOCKS + c // 2) * 2 + kk
                            last = nc.tensor.matmul(
                                K.ps[:, 4 * which + c // 2, (c % 2) * SEQ:(c % 2 + 1) * SEQ],
                                wg[:, which, n, (c % 2) * P:(c % 2 + 1) * P], xc[:, (c // 2) * 2 + kk],
                                start=(kk == 0), stop=(kk == 1))
                    last.then_inc(g_ready, 1)
            pe.wait_ge(w_loaded, 16)
            pe.wait_ge(y_ready, 1)
            product_out(K, pe, w, o_ready)

        @block.vector
        def _(dve):
            link = Link(dve, chain)
            nc.vector.memset(padded, 0.0)
            dve.wait_ge(loaded, 16 * (TAPS + 1 + 6))
            link(nc.vector.scalar_tensor_tensor(u, lam, -1.0, lam, ALU.mult, ALU.min))
            dve.sem_inc(z_ready, 1)
            link(nc.vector.tensor_copy(padded[:, :, LEFT:LEFT + SEQ], xb))
            for c in range(KD):
                for j in range(TAPS):
                    src = padded[:, c, j:j + SEQ]
                    if j == 0:
                        ins = nc.vector.tensor_scalar(xc[:, c], src, cw[:, 0, c:c + 1], cb[:, c:c + 1],
                                                      ALU.mult, ALU.add)
                    else:
                        ins = nc.vector.scalar_tensor_tensor(xc[:, c], src, cw[:, j, c:c + 1], xc[:, c],
                                                             ALU.mult, ALU.add)
                    link(ins)
            dve.sem_inc(xc_ready, 1)
            dve.wait_ge(e_ready, 1)
            link(nc.vector.tensor_scalar(u2, ex, 2.0, None, ALU.add))
            link(nc.vector.reciprocal(u, u2))
            link(nc.vector.tensor_tensor(u, u, ex, ALU.mult))
            link(nc.vector.tensor_tensor(u2, u, u, ALU.mult))
            link(nc.vector.tensor_scalar(poly, u2, 1.0 / 17, 1.0 / 15, ALU.mult, ALU.add))
            for k in (13, 11, 9, 7, 5, 3, 1):
                link(nc.vector.tensor_tensor(poly, poly, u2, ALU.mult))
                link(nc.vector.tensor_scalar(poly, poly, 1.0 / k, None, ALU.add))
            link(nc.vector.tensor_tensor(poly, poly, u, ALU.mult))
            link(nc.vector.tensor_scalar(ex, lam, -1.0, 0.0, ALU.mult, ALU.max))
            link(nc.vector.scalar_tensor_tensor(lam, poly, 2.0, ex, ALU.mult, ALU.add))
            link(nc.vector.tensor_scalar(lam, lam, -LRU_C, None, ALU.mult))
            dve.sem_inc(nsp_ready, 1)
            for d in range(2):
                dve.wait_ge(at_done, d + 1)
                link(nc.vector.tensor_scalar(bb, th, -1.0, 1.0, ALU.mult, ALU.add))
                link(nc.vector.reciprocal(bb, bb))
                link(nc.vector.scalar_tensor_tensor(th, th, -2.0, bb, ALU.mult, ALU.mult))
                dve.sem_inc(m_ready, 1)
                link(nc.vector.tensor_tensor(bb, ig, xc, ALU.mult))
                dve.wait_ge(sq_done, d + 1)
                link(nc.vector.tensor_tensor(bb, bb, th, ALU.mult))
                for c in range(KD):
                    if d == 0:
                        ins = nc.vector.tensor_tensor_scan(hs[:, d, c], aa[:, c], bb[:, c], 0.0, ALU.mult,
                                                           ALU.add)
                    else:
                        ins = nc.vector.tensor_tensor_scan(hs[:, d, c][:, ::-1], aa[:, c][:, ::-1],
                                                           bb[:, c][:, ::-1], 0.0, ALU.mult, ALU.add)
                link(ins)
                dve.sem_inc(th_used, 1)
            link(nc.vector.tensor_tensor(hs[:, 0], hs[:, 0], hs[:, 1], ALU.add))
            dve.wait_ge(gelu_done, 1)
            nc.vector.tensor_tensor(K.h_t[:], hs[:, 0], yb, ALU.mult).then_inc(y_ready, 1)
            residual_out(K, dve, link, K.gate[:, 0], o_ready, tmp)


def lru_mixer(K, S):
    area = Area(K.arena)
    xb = area.take(KD, SEQ)
    yb = area.take(KD, SEQ)
    blocks = [("cols", n * 512, (xb, yb)[n // 2][:, 4 * (n % 2):4 * (n % 2) + 4]) for n in range(4)]
    stage_projection(K, S, K.gain[:, 0], K.shift[:, 0], K.i["lru_w_in_2"][0], blocks, area.at)
    stage_lru(K, S, xb, yb, area.at)



def stage_scores(K, S, l, q, s, keys, keys_t):
    nc = K.nc
    with S.open() as (block, sem):
        loaded, kt_ready, kt_out, s_ready, s_out = (sem("loaded"), sem("kt_ready"), sem("kt_out"),
                                                    sem("s_ready"), sem("s_out"))

        @block.sync
        def _(sp):
            sp.dma_start(keys, K.i["peer_keys_2"][l].rearrange("h w k d -> k (h w) d")).then_inc(loaded, 16)

        @block.tensor
        def _(pe):
            pe.wait_ge(loaded, 16)
            for n in range(HP):
                last = nc.tensor.transpose(K.ps[:, n // 4, (n % 4) * P:(n % 4 + 1) * P], keys[:, n], K.ident[:])
            last.then_inc(kt_ready, 1)
            pe.wait_ge(kt_out, 1)
            for t in range(TT):
                for n in range(HP):
                    last = nc.tensor.matmul(K.ps[:, 4 * (1 - t) + n // 4, (n % 4) * P:(n % 4 + 1) * P],
                                            q[:, n, t * P:(t + 1) * P], keys_t[:, n], start=True, stop=True)
                last.then_inc(s_ready, 1)

        @block.vector
        def _(dve):
            dve.wait_ge(kt_ready, 1)
            nc.vector.tensor_copy(keys_t.rearrange("p n k -> p (n k)"),
                                  K.ps[:, 0:4].rearrange("p b n -> p (b n)")).then_inc(kt_out, 1)
            for t in range(TT):
                dve.wait_ge(s_ready, t + 1)
                b0 = 4 * (1 - t)
                nc.vector.tensor_copy(s[:, t].rearrange("p n k -> p (n k)"),
                                      K.ps[:, b0:b0 + 4].rearrange("p b n -> p (b n)")).then_inc(s_out, 1)
            dve.wait_ge(s_out, 2)


def stage_routing(K, S, s, at):
    nc = K.nc
    G = TT * PH
    with S.open() as (block, sem):
        area = Area(K.arena, at)
        val = area.take(TT * HP, TOPK)
        idx = area.take(TT * HP, TOPK).bitcast(U32)
        idf = area.take(TT * HP, TOPK)
        cand = area.take(G, TOPK, TOPK)
        top = area.take(G, TOPK)
        pos = area.take(G, TOPK).bitcast(U32)
        part = area.take(G, TOPK).bitcast(U32)
        partf = area.take(G, TOPK)
        picked = area.take(2, G, TOPK)
        gates = area.take(G, TOPK)
        sums = area.take(G)
        onehot = area.take(G, TOPK, TOPK)
        ramp = area.take(TOPK)
        chain, ramp_ready, gl_ready, e_ready, sel_ready, t_ready = (
            sem("chain"), sem("ramp"), sem("gl"), sem("e"), sem("sel"), sem("t"))
        sf = s.rearrange("p t n k -> p (t n) k")

        @block.gpsimd
        def _(pool):
            nc.gpsimd.iota(ramp, pattern=[[1, TOPK]], base=0, channel_multiplier=0,
                           allow_small_or_imprecise_dtypes=True).then_inc(ramp_ready, 1)

        @block.scalar
        def _(act):
            act.wait_ge(gl_ready, 1)
            nc.scalar.activation(gates, gates, ACT.Exp).then_inc(e_ready, 1)

        @block.tensor
        def _(pe):
            pe.wait_ge(sel_ready, 1)
            for n, src in enumerate((picked[:, 0], picked[:, 1], gates)):
                src = src.rearrange("p (t h) k -> p t (h k)", t=TT)
                for t in range(TT):
                    last = nc.tensor.transpose(K.ps[:, n, t * P:(t + 1) * P], src[:, t], K.ident[:])
            last.then_inc(t_ready, 1)

        @block.vector
        def _(dve):
            link = Link(dve, chain)

            def top16(values, out, places, n):
                for half in range(2):
                    cut = slice(8 * half, 8 * half + 8)
                    for g in range(n):
                        ins = nc.vector.max(out[:, g, cut], values[:, g])
                    link(ins)
                    for g in range(n):
                        ins = nc.vector.max_index(places[:, g, cut], out[:, g, cut], values[:, g])
                    link(ins)
                    if half == 0:
                        for g in range(n):
                            ins = nc.vector.match_replace(values[:, g], out[:, g, cut], values[:, g], -BIG)
                        link(ins)

            top16(sf, val, idx, TT * HP)
            link(nc.vector.tensor_copy(idf, idx))
            v4 = val.rearrange("p (g w) k -> p g w k", w=2)
            for g in range(G):
                ins = nc.vector.tensor_tensor(cand[:, g], v4[:, g, 0].unsqueeze(2).broadcast_to([P, TOPK, TOPK]),
                                              v4[:, g, 1].unsqueeze(1).broadcast_to([P, TOPK, TOPK]), ALU.add)
            link(ins)
            top16(cand.rearrange("p g a b -> p g (a b)"), top, pos, G)
            nc.vector.tensor_tensor(gates, top, top[:, :, 0:1].broadcast_to([P, G, TOPK]),
                                    ALU.subtract).then_inc(gl_ready, 1)
            dve.wait_ge(ramp_ready, 1)
            i4 = idf.rearrange("p (g w) k -> p g w k", w=2)
            rampb = ramp.unsqueeze(1).broadcast_to([P, TOPK, TOPK])
            for w, (op, number) in enumerate(((ALU.logical_shift_right, 4), (ALU.bitwise_and, TOPK - 1))):
                link(nc.vector.tensor_scalar(part, pos, number, None, op))
                link(nc.vector.tensor_copy(partf, part))
                for g in range(G):
                    ins = nc.vector.tensor_tensor(onehot[:, g], partf[:, g].unsqueeze(2).broadcast_to([P, TOPK, TOPK]),
                                                  rampb, ALU.is_equal)
                link(ins)
                for g in range(G):
                    ins = nc.vector.tensor_tensor(onehot[:, g], onehot[:, g],
                                                  i4[:, g, w].unsqueeze(1).broadcast_to([P, TOPK, TOPK]), ALU.mult)
                link(ins)
                link(nc.vector.tensor_reduce(picked[:, w].rearrange("p g k -> p (g k)"),
                                             onehot.rearrange("p g k a -> p (g k) a"), AX.X, ALU.add))
            dve.wait_ge(e_ready, 1)
            link(nc.vector.tensor_reduce(sums, gates, AX.X, ALU.add))
            link(nc.vector.reciprocal(sums, sums))
            nc.vector.tensor_tensor(gates, gates, sums.unsqueeze(2).broadcast_to([P, G, TOPK]),
                                    ALU.mult).then_inc(sel_ready, 1)
            dve.wait_ge(t_ready, 1)
            for n in range(3):
                ins = nc.vector.tensor_copy(K.sel[:, n], K.ps[:, n, 0:SEQ])
            link(ins)


def pipeline(engine, total, unroll, body):
    for u in range(unroll):
        body(u, u, True)
    with engine.Fori(1, total // unroll - 1) as i:
        for u in range(unroll):
            body(i * unroll + u, u, False)
    for u in range(unroll):
        body(total - unroll + u, u, False)


USLOTS = 4


def stage_expert_inputs(K, S, l):
    nc = K.nc
    table = K.i["peer_u_2"][l].rearrange("(i j) d -> j i d", j=NKEYS)
    with S.open() as (block, sem):
        u_loaded = [sem(f"u_loaded{s}") for s in range(USLOTS)]
        ut_ready, ut_out_act, ut_out_dve = sem("ut_ready"), sem("ut_out_act"), sem("ut_out_dve")
        a_ready, gelu_done = sem("a_ready"), sem("gelu_done")
        u = K.ring[:, 0:USLOTS * D].rearrange("p (s k d) -> p s k d", s=USLOTS, k=KD)
        u_t = K.ring[:, USLOTS * D:(USLOTS + 2) * D].rearrange("p (s k e) -> p s k e", s=2, k=KD)

        @block.sync
        def _(sp):
            def load(n, s, first):
                if not first:
                    sp.wait_ge(ut_ready, n - (USLOTS - 1))
                sp.dma_start(u[:, s].rearrange("p k d -> p (k d)"),
                             table[bass.ds(n, 1)].rearrange("a i d -> i (a d)")).then_inc(u_loaded[s], 16)

            pipeline(sp, NKEYS, USLOTS, load)

        @block.tensor
        def _(pe):
            def products(n, b, early):
                pe.wait_ge(ut_out_act, n + 1)
                pe.wait_ge(ut_out_dve, n + 1)
                if not early:
                    pe.wait_ge(gelu_done, n - 1)
                for k in range(KD):
                    last = nc.tensor.matmul(K.ps[:, 4 + b, 0:SEQ], u_t[:, b, k], K.h_t[:, k],
                                            start=(k == 0), stop=(k == KD - 1))
                last.then_inc(a_ready, 1)

            def chunk(n, s, first):
                b = s % 2
                if first:
                    pe.wait_ge(u_loaded[s], 16)
                else:
                    pe.wait_ge(u_loaded[s], chunk_loads(n, s))
                if not first or n >= 2:
                    pe.wait_ge(ut_out_act, n - 1)
                    pe.wait_ge(ut_out_dve, n - 1)
                for k in range(KD):
                    last = nc.tensor.transpose(K.ps[:, 2 * b + k // 4, (k % 4) * P:(k % 4 + 1) * P],
                                               u[:, s, k], K.ident[:])
                last.then_inc(ut_ready, 1)
                if not first or n >= 1:
                    products(n - 1, 1 - b, first and n < 3)

            def chunk_loads(n, s):
                return (n - s) * (16 // USLOTS) + 16

            pipeline(pe, NKEYS, USLOTS, chunk)
            products(NKEYS - 1, (NKEYS - 1) % 2, False)

        def copy_out(engine, op, half, done):
            def copy(n, s, first):
                b = s % 2
                engine.wait_ge(ut_ready, n + 1)
                if not first or n >= 2:
                    engine.wait_ge(a_ready, n - 1)
                op(u_t[:, b, 4 * half:4 * half + 4].rearrange("p k e -> p (k e)"),
                   K.ps[:, 2 * b + half]).then_inc(done, 1)
            return copy

        @block.scalar
        def _(act):
            copy = copy_out(act, nc.scalar.copy, 0, ut_out_act)

            def gelu(n, b):
                act.wait_ge(a_ready, n + 1)
                nc.scalar.activation(K.arena[:, bass.ds(n * SEQ, SEQ)], K.ps[:, 4 + b, 0:SEQ],
                                     ACT.Gelu_apprx_tanh).then_inc(gelu_done, 1)

            def chunk(n, s, first):
                copy(n, s, first)
                if not first or n >= 1:
                    gelu(n - 1, (s + 1) % 2)

            pipeline(act, NKEYS, USLOTS, chunk)
            gelu(NKEYS - 1, (NKEYS - 1) % 2)
            act.wait_ge(gelu_done, NKEYS)

        @block.vector
        def _(dve):
            pipeline(dve, NKEYS, USLOTS, copy_out(dve, nc.vector.tensor_copy, 1, ut_out_dve))


TG = 4


def stage_expert_gates(K, S):
    nc = K.nc
    groups = SEQ // TG
    with S.open() as (block, sem):
        left = K.ring[:, 0:2 * TG * P].rearrange("p (b t i) -> p b t i", b=2, t=TG)
        right = K.ring[:, 2 * TG * P:4 * TG * P].rearrange("p (b t i) -> p b t i", b=2, t=TG)
        ramp = K.ring[:, 4 * TG * P:4 * TG * P + P]
        number = K.ring[:, 4 * TG * P + P:4 * TG * P + P + 2 * TG].rearrange("p (b t) -> p b t", b=2)
        fetched, fetch_seen = sem("fetched"), sem("fetch_seen")
        ramp_ready, left_ready, right_ready, w_ready, w_out = (
            sem("ramp"), sem("left_ready"), sem("right_ready"), sem("w_ready"), sem("w_out"))
        act_buf = K.arena[:].rearrange("p (j t) -> p t j", t=SEQ)

        @block.gpsimd
        def _(pool):
            nc.gpsimd.iota(ramp, pattern=[[1, P]], base=0, channel_multiplier=0,
                           allow_small_or_imprecise_dtypes=True).then_inc(ramp_ready, 1)
            pool.wait_ge(ramp_ready, 1)

            def group(n, b, first):
                if not first:
                    pool.wait_ge(w_ready, n - 1)
                nc.gpsimd.tensor_copy(number[:, b], K.sel[:, 0, bass.ds(n * TG, TG)]).then_inc(fetched, 1)
                pool.wait_ge(fetched, n + 1)
                pool.sem_inc(fetch_seen, 1)
                for t in range(TG):
                    ins = nc.gpsimd.tensor_scalar(left[:, b, t], ramp, number[:, b, t:t + 1],
                                                  None, ALU.is_equal)
                ins.then_inc(left_ready, 1)

            pipeline(pool, groups, 2, group)

        @block.tensor
        def _(pe):
            def group(n, b, first):
                pe.wait_ge(left_ready, n + 1)
                pe.wait_ge(right_ready, n + 1)
                if not first:
                    pe.wait_ge(w_out, n - 1)
                for t in range(TG):
                    last = nc.tensor.matmul(K.ps[:, b, t * P:(t + 1) * P], left[:, b, t], right[:, b, t],
                                            start=True, stop=True)
                last.then_inc(w_ready, 1)

            pipeline(pe, groups, 2, group)

        @block.vector
        def _(dve):
            dve.wait_ge(ramp_ready, 1)

            def build(n, b, first):
                if not first:
                    dve.wait_ge(w_ready, n - 1)
                for t in range(TG):
                    ins = nc.vector.tensor_scalar(right[:, b, t], ramp, K.sel[:, 1, bass.ds(n * TG + t, 1)],
                                                  K.sel[:, 2, bass.ds(n * TG + t, 1)], ALU.is_equal, ALU.mult)
                ins.then_inc(right_ready, 1)

            def weigh(n, b):
                dve.wait_ge(w_ready, n + 1)
                piece = act_buf[:, bass.ds(n * TG, TG)]
                nc.vector.tensor_tensor(piece, piece, K.ps[:, b].rearrange("p (t j) -> p t j", t=TG),
                                        ALU.mult).then_inc(w_out, 1)

            def group(n, b, first):
                build(n, b, first)
                if not first or n >= 1:
                    weigh(n - 1, 1 - b)

            pipeline(dve, groups, 2, group)
            weigh(groups - 1, (groups - 1) % 2)
            dve.wait_ge(w_out, groups)


def stage_expert_outputs(K, S, l):
    nc = K.nc
    table = K.i["peer_v_2"][l].rearrange("(i j) d -> j i d", j=NKEYS)
    with S.open() as (block, sem):
        v_loaded = [sem(f"v_loaded{s}") for s in range(USLOTS)]
        g_ready, p_done, chain = sem("g_ready"), sem("p_done"), sem("chain")
        v = K.ring[:, 0:USLOTS * D].rearrange("p (s d) -> p s d", s=USLOTS)
        g = K.ring[:, USLOTS * D:USLOTS * D + 2 * SEQ].rearrange("p (s t) -> p s t", s=2)
        tmp = K.ring[:, (USLOTS + 1) * D:(USLOTS + 2) * D]

        @block.sync
        def _(sp):
            def load(n, s, first):
                if not first:
                    sp.wait_ge(p_done, n - (USLOTS - 1))
                sp.dma_start(v[:, s], table[bass.ds(n, 1)].rearrange("a i d -> i (a d)")
                             ).then_inc(v_loaded[s], 16)

            pipeline(sp, NKEYS, USLOTS, load)

        @block.tensor
        def _(pe):
            def chunk(n, s, first, start=False, stop=False):
                pe.wait_ge(v_loaded[s], (n - s) * (16 // USLOTS) + 16)
                pe.wait_ge(g_ready, n + 1)
                for t in range(TT):
                    for half in range(2):
                        last = nc.tensor.matmul(K.ps[:, 4 + 2 * t + half], g[:, s % 2, t * P:(t + 1) * P],
                                                v[:, s, half * 512:(half + 1) * 512],
                                                start=(first and s == 0), stop=stop)
                last.then_inc(p_done, 1)

            for s in range(USLOTS):
                chunk(s, s, True)
            with pe.Fori(1, NKEYS // USLOTS - 1) as i:
                for s in range(USLOTS):
                    chunk(i * USLOTS + s, s, False)
            for s in range(USLOTS):
                chunk(NKEYS - USLOTS + s, s, False, stop=(s == USLOTS - 1))

        @block.vector
        def _(dve):
            link = Link(dve, chain)

            def fetch(n, s, first):
                if not first or n >= 2:
                    dve.wait_ge(p_done, n - 1)
                nc.vector.tensor_copy(g[:, s % 2], K.arena[:, bass.ds(n * SEQ, SEQ)]).then_inc(g_ready, 1)

            pipeline(dve, NKEYS, USLOTS, fetch)
            dve.wait_ge(p_done, NKEYS)
            for t in range(TT):
                link(nc.vector.tensor_tensor(tmp, K.ps[:, 4 + 2 * t:6 + 2 * t].rearrange("p b n -> p (b n)"),
                                             K.gate[:, 1], ALU.mult))
                link(nc.vector.tensor_tensor(K.x[:, t], K.x[:, t], tmp, ALU.add))


def retrieval(K, S, l):
    area = Area(K.arena)
    q = area.take(HP, SEQ)
    s = area.take(TT, HP, NKEYS)
    keys = area.take(HP, P)
    keys_t = area.take(HP, P)
    blocks = [("cols", n * 512, q[:, 4 * n:4 * n + 4]) for n in range(4)]
    stage_projection(K, S, K.gain[:, 1], K.shift[:, 1], K.i["peer_w_q_2"][l], blocks, area.at)
    stage_scores(K, S, l, q, s, keys, keys_t)
    stage_routing(K, S, s, area.at)
    stage_expert_inputs(K, S, l)
    stage_expert_gates(K, S)
    stage_expert_outputs(K, S, l)


def stage_final(K, S):
    nc = K.nc
    with S.open() as (block, sem):
        area = Area(K.arena)
        gain = area.take(D)
        sq = area.take(D)
        st = area.take(3, TT)
        chain, loaded, ms, var, sd, y, stored = (sem("chain"), sem("loaded"), sem("ms"), sem("var"), sem("sd"),
                                                 sem("y"), sem("stored"))

        @block.sync
        def _(sp):
            sp.dma_start(gain, K.i["final_g_2"].rearrange("(a d) -> a d", a=1).broadcast_to([P, D])
                         ).then_inc(loaded, 16)
            for t in range(TT):
                sp.wait_ge(y, t + 1)
                sp.dma_start(K.out[0, t * P:(t + 1) * P], K.x[:, t]).then_inc(stored, 16)
            sp.wait_ge(stored, 16 * TT)

        @block.scalar
        def _(act):
            for t in range(TT):
                nc.scalar.activation(sq, K.x[:, t], ACT.Square, accum_out=st[:, 0, t:t + 1]).then_inc(ms, 1)
                act.wait_ge(ms, t + 1)
            act.wait_ge(var, 1)
            nc.scalar.activation(st[:, 2], st[:, 1], ACT.Sqrt).then_inc(sd, 1)

        @block.vector
        def _(dve):
            link = Link(dve, chain)
            dve.wait_ge(ms, TT)
            nc.vector.tensor_scalar(st[:, 1], st[:, 0], 1.0 / D, EPS, ALU.mult, ALU.add).then_inc(var, 1)
            dve.wait_ge(sd, 1)
            link(nc.vector.reciprocal(st[:, 0], st[:, 2]))
            dve.wait_ge(loaded, 16)
            for t in range(TT):
                nc.vector.scalar_tensor_tensor(K.x[:, t], K.x[:, t], st[:, 0, t:t + 1], gain, ALU.mult,
                                               ALU.mult).then_inc(y, 1)


def second_block(K, S):
    for l in range(DEPTH):
        stage_modulation(K, S, l)
        if l % 2 == 0:
            hg_mixer(K, S)
        else:
            lru_mixer(K, S)
        retrieval(K, S, l)
    stage_final(K, S)


def memory(nc, K):
    def sb(name, dims, dt=F32):
        return nc.alloc_sbuf_tensor(name, [P, *dims], dt)

    K.x = sb("x_rows", [TT, D])
    K.h_t = sb("h_cols", [KD, SEQ])
    K.ident = sb("identity", [P])
    K.ones = sb("ones", [P])
    K.causal = sb("causal", [P])
    K.pos = sb("position", [TT])
    K.invf = sb("inverse_frequency", [HALF])
    K.cos = sb("cosine", [TT, HALF])
    K.sin = sb("sine", [TT, HALF])
    K.g_norm = sb("norm_gain", [KD])
    K.gain = sb("mixer_gains", [2, KD])
    K.shift = sb("mixer_shifts", [2, KD])
    K.gate = sb("residual_gates", [2, D])
    K.sel = sb("chosen_experts", [3, SEQ])
    K.arena = sb("arena", [32768])
    K.ring = sb("weights_ring", [8192])
    K.wslot = [K.ring[:, n * 4096:(n + 1) * 4096].rearrange("p (k n) -> p k n", k=KD) for n in range(2)]
    K.ps = nc.alloc_psum_tensor("psum", [P, 8, 512], F32)
    K.ps_low = K.ps[:, 0:4].rearrange("p b (c t) -> p (b c) t", c=2)
    K.ps_pair = [K.ps[:, 4:6], K.ps[:, 6:8]]

    area = Area(K.arena)
    K.glu = area.take(4, SEQ)
    K.low = area.take((Q_LORA + KV_LORA) // P, SEQ)
    K.zconv = area.take(TT, CONV_W)
    K.rows = area.take(TT, N_ROWS)
    K.y = area.take(TT, D)
    K.v = area.take(TT, HEADS, VD)
    K.q_t = area.take(HEADS, SEQ)
    K.k_t = area.take(HEADS, SEQ)
    K.g_q = area.take(Q_LORA // P)
    K.g_kv = area.take(KV_LORA // P)
    K.g_branch = area.take(KD)
    K.cb = area.take(3, 2)
    K.cw = area.take(2, CONV_K)
    K.sgb = area.take(SG_HEADS)
    K.sgw = area.take(SG_HEADS, P)
    K.pwb = area.take(CONV_W)
    K.gqk = area.take(2, QK)
    K.sgln = area.take(2, SG_W)
    K.first_end = area.at


def build(nc, ins, out):
    K = Names()
    K.nc, K.i, K.out = nc, ins, out
    K.layer = lambda name, l: ins[name][bass.ds(l, 1), :]
    memory(nc, K)
    S = Stages(nc)
    with nc.allow_non_contiguous_dma("parameters by channel, a few KB"):
        stage_setup(K, S)
        stage_rope_tables(K, S)
        first_block(K, S)
        second_block(K, S)


def kernel(**inputs):
    import numpy as _np
    import concourse.bacc as _bacc
    from concourse import mybir as _mybir
    from concourse.bass_utils import run_bass_kernel_spmd as _run

    half = ROPE // 2
    inputs = dict(inputs)
    inputs["inv_freq"] = (_np.float32(10000.0) ** (-_np.arange(half, dtype=_np.float32) / _np.float32(half))
                          ).astype(_np.float32)[None]
    nc = _bacc.Bacc("TRN2", target_bir_lowering=False, num_devices=1)
    arrays, aps = {}, {}
    for name, value in inputs.items():
        a = _np.ascontiguousarray(value)
        arrays[f"in_{name}_dram"] = a
        aps[name] = nc.dram_tensor(f"in_{name}_dram", a.shape, _mybir.dt.from_np(a.dtype),
                                   kind="ExternalInput").ap()
    out = nc.dram_tensor("out_0_dram", (1, SEQ, D), F32, kind="ExternalOutput").ap()
    build(nc, aps, out)
    r = _run(nc, [arrays], core_ids=[0])
    return r.results[0]["out_0_dram"]
```

```python
from contextlib import ExitStack, contextmanager

import numpy as np

import concourse.bass as bass
from concourse import mybir

F32 = mybir.dt.float32
U32 = mybir.dt.uint32
I32 = mybir.dt.int32
U8 = mybir.dt.uint8
ALU = mybir.AluOpType
ACT = mybir.ActivationFunctionType
AX = mybir.AxisListType

P = 128
SEQ = 256
TT = SEQ // P
D = 1024
KD = D // P
DEPTH = 2
EPS = 1e-6
NEG = -1e30

CONV_W = 256
CONV_K = 31
HEADS = 8
NOPE = 64
ROPE = 32
HALF = ROPE // 2
QK = NOPE + ROPE
VD = 64
MLA_W = HEADS * VD
Q_LORA = 768
KV_LORA = 256
SG_W = 256
SG_HEADS = 4
SG_D = SG_W // SG_HEADS

C_ZCONV = 2 * CONV_W
C_CQ = 3 * CONV_W
C_ROWS = C_CQ + Q_LORA + KV_LORA
IN_COLS = C_ROWS + ROPE + MLA_W + 3 * SG_W
N_ROWS = IN_COLS - C_ROWS
R_ROPE, R_ZMLA, R_U = 0, ROPE, ROPE + MLA_W
R_V, R_ZSG = R_U + SG_W, R_U + 2 * SG_W

STAGE_SEMS = 28


class Names:
    pass


class Link:

    def __init__(self, engine, sem, base=0):
        self.engine, self.sem, self.base, self.n = engine, sem, base, 0

    def __call__(self, instruction):
        instruction.then_inc(self.sem, 1)
        self.n += 1
        self.engine.wait_ge(self.sem, self.base + self.n)
        return instruction


class Area:

    def __init__(self, arena, at=0):
        self.arena, self.at = arena, at

    def take(self, *dims, parts=P):
        n = int(np.prod(dims))
        piece = self.arena[0:parts, self.at:self.at + n]
        self.at += n + n % 2
        if len(dims) == 1:
            return piece
        names = "abcd"[:len(dims)]
        sizes = {c: d for c, d in zip(names, dims)}
        return piece.rearrange(f"p ({' '.join(names)}) -> p {' '.join(names)}", **sizes)


class Stages:

    def __init__(self, nc):
        self.nc, self.turn = nc, 0
        self.banks = []
        for b in range(2):
            handles = [nc.alloc_semaphore(f"stage_bank{b}_{i}") for i in range(STAGE_SEMS)]
            self.banks.append(handles)

    @contextmanager
    def open(self):
        nc = self.nc
        idle, mine = self.banks[1 - self.turn], list(self.banks[self.turn])
        nums = sorted(s.num for s in idle)
        assert nums == list(range(nums[0], nums[0] + STAGE_SEMS))
        nc.gpsimd.sem_clear(range(nums[0], nums[-1] + 1))
        with nc.Block(no_gpsimd_drain=True) as block:
            yield block, (lambda name: mine.pop(0))
        self.turn = 1 - self.turn


def load_cols(dma, out, src, chunks):
    return dma(out, src.rearrange("a (k p) -> p (a k)", k=chunks))


def cast_rows(src):
    return src.broadcast_to([P, src.shape[1]])



class NormTranspose:

    def __init__(self, K, sem, area):
        self.K = K
        self.xn = area.take(TT, D)
        self.sq = area.take(D)
        self.stat = area.take(3, TT)
        self.ms_ready = sem("ms_ready")
        self.var_ready = sem("var_ready")
        self.sd_ready = sem("sd_ready")
        self.xn_ready = sem("xn_ready")
        self.xt_ready = sem("xt_ready")

    def act(self, act):
        K, nc = self.K, self.K.nc
        for t in range(TT):
            nc.scalar.activation(self.xn[:, t], K.x[:, t], ACT.Square,
                                 accum_out=self.stat[:, 0, t:t + 1]).then_inc(self.ms_ready, 1)
        act.wait_ge(self.var_ready, 1)
        nc.scalar.activation(self.stat[:, 2], self.stat[:, 1], ACT.Sqrt).then_inc(self.sd_ready, 1)

    def dve_norm(self, dve, link):
        K, nc = self.K, self.K.nc
        dve.wait_ge(self.ms_ready, TT)
        nc.vector.tensor_scalar(self.stat[:, 1], self.stat[:, 0], 1.0 / D, EPS, ALU.mult,
                                ALU.add).then_inc(self.var_ready, 1)
        dve.wait_ge(self.sd_ready, 1)
        link(nc.vector.reciprocal(self.stat[:, 0], self.stat[:, 2]))
        for t in range(TT):
            nc.vector.tensor_scalar(self.xn[:, t], K.x[:, t], self.stat[:, 0, t:t + 1], None,
                                    ALU.mult).then_inc(self.xn_ready, 1)

    def pe(self, pe):
        K, nc = self.K, self.K.nc
        for t in range(TT):
            pe.wait_ge(self.xn_ready, t + 1)
            for k in range(KD):
                last = nc.tensor.transpose(K.ps_low[:, k, t * P:(t + 1) * P],
                                           self.xn[:, t, k * P:(k + 1) * P], K.ident[:])
            last.then_inc(self.xt_ready, 1)

    def dve_scale(self, dve, gain, shift, h_ready):
        K, nc = self.K, self.K.nc
        dve.wait_ge(self.xt_ready, TT)
        for k in range(KD):
            if shift is None:
                ins = nc.vector.tensor_scalar(K.h_t[:, k], K.ps_low[:, k], gain[:, k:k + 1], None,
                                              ALU.mult)
            else:
                ins = nc.vector.tensor_scalar(K.h_t[:, k], K.ps_low[:, k], gain[:, k:k + 1],
                                              shift[:, k:k + 1], ALU.mult, ALU.add)
            ins.then_inc(h_ready, 1)


def matmul_rows(nc, out, lhs_t, w, t, chunks):
    for k in range(chunks):
        last = nc.tensor.matmul(out, lhs_t[:, k, t * P:(t + 1) * P], w[:, k],
                                start=(k == 0), stop=(k == chunks - 1))
    return last


def matmul_cols(nc, out, w, rhs_t, c, chunks):
    for k in range(chunks):
        last = nc.tensor.matmul(out, w[:, k, c * P:(c + 1) * P], rhs_t[:, k],
                                start=(k == 0), stop=(k == chunks - 1))
    return last



def stage_setup(K, S):
    nc = K.nc
    with S.open() as (block, sem):
        loaded, zeroed, made = sem("loaded"), sem("zeroed"), sem("made")

        @block.sync
        def _(sp):
            sp.dma_start(K.x[:], K.i["x"].rearrange("b (t p) d -> p (b t) d", p=P)).then_inc(loaded, 16)
            sp.dma_start(K.invf[:], K.i["inv_freq"].broadcast_to([P, HALF])).then_inc(loaded, 16)
            sp.wait_ge(loaded, 32)

        @block.gpsimd
        def _(pool):
            nc.gpsimd.memset(K.ident[:], 0.0)
            nc.gpsimd.memset(K.ones[:], 1.0)
            nc.gpsimd.memset(K.causal[:], 0.0)
            nc.gpsimd.iota(K.pos[:], pattern=[[P, TT]], base=0, channel_multiplier=1,
                           allow_small_or_imprecise_dtypes=True).then_inc(zeroed, 1)
            pool.wait_ge(zeroed, 1)
            nc.gpsimd.affine_select(out=K.ident[:], in_=K.ident[:], compare_op=ALU.not_equal,
                                    fill=1.0, base=0, pattern=[[-1, P]], channel_multiplier=1)
            nc.gpsimd.affine_select(out=K.causal[:], in_=K.causal[:], compare_op=ALU.is_ge,
                                    fill=NEG, base=0, pattern=[[-1, P]],
                                    channel_multiplier=1).then_inc(made, 1)
            pool.wait_ge(made, 1)


def stage_rope_tables(K, S):
    nc = K.nc
    two_pi = 2 * np.pi
    hi = float(np.float32(6.28125))
    mid = float(np.float32(np.round((two_pi - hi) * 2**20) / 2**20))
    low = float(np.float32(two_pi - hi - mid))
    with S.open() as (block, sem):
        chain, angle_ready, sin_done = sem("chain"), sem("angle_ready"), sem("sin_done")
        area = Area(K.arena)
        ang, turns, red, whole = (area.take(TT, HALF) for _ in range(4))
        whole_i = whole.bitcast(I32)

        @block.vector
        def _(dve):
            link = Link(dve, chain)
            for t in range(TT):
                link(nc.vector.tensor_scalar(ang[:, t], K.invf[:], K.pos[:, t:t + 1], None, ALU.mult))
            for n, (table, shift) in enumerate(((K.sin, 0.0), (K.cos, 0.25))):
                link(nc.vector.tensor_scalar(turns, ang, 1.0 / two_pi, shift, ALU.mult, ALU.add))
                link(nc.vector.tensor_copy(whole_i, turns))
                link(nc.vector.tensor_copy(turns, whole_i))
                link(nc.vector.scalar_tensor_tensor(red, turns, -hi, ang, ALU.mult, ALU.add))
                link(nc.vector.scalar_tensor_tensor(red, turns, -mid, red, ALU.mult, ALU.add))
                link(nc.vector.scalar_tensor_tensor(red, turns, -low, red, ALU.mult, ALU.add))
                if shift:
                    link(nc.vector.tensor_scalar(red, red, float(np.pi / 2), None, ALU.add))
                link(nc.vector.tensor_scalar(table[:], red, float(-np.pi), float(np.pi), ALU.max, ALU.min))
            dve.sem_inc(angle_ready, 1)

        @block.scalar
        def _(act):
            act.wait_ge(angle_ready, 1)
            nc.scalar.activation(K.sin[:], K.sin[:], ACT.Sin)
            nc.scalar.activation(K.cos[:], K.cos[:], ACT.Sin).then_inc(sin_done, 1)
            act.wait_ge(sin_done, 1)



IN_BLOCKS = [("cols", 0, 512), ("rows", C_ZCONV, 256), ("cols", C_CQ, 512),
             ("cols", C_CQ + 512, 512), ("rows", C_ROWS, 512), ("rows", C_ROWS + 512, 512),
             ("rows", C_ROWS + 1024, N_ROWS - 1024)]


def stage_in_projection(K, S, l):
    nc, i = K.nc, K.i
    with S.open() as (block, sem):
        area = Area(K.arena, K.first_end)
        norm = NormTranspose(K, sem, area)
        chain, params, h_ready = sem("chain"), sem("params"), sem("h_ready")
        w_loaded = [sem("w_loaded0"), sem("w_loaded1")]
        proj_ready, proj_out = sem("proj_ready"), sem("proj_out")

        @block.sync
        def _(sp):
            at = {}
            for n, (_, c0, width) in enumerate(IN_BLOCKS):
                if n >= 2:
                    sp.wait_ge(proj_ready, n - 1)
                src = i["w_in"][bass.ds(l, 1), :, c0:c0 + width].rearrange("a (k p) n -> p (a k) n", p=P)
                sp.dma_start(K.wslot[n % 2][:, :, 0:width], src).then_inc(w_loaded[n % 2], 16)

        @block.scalar
        def _(act):
            norm.act(act)
            load = lambda out, name, chunks: load_cols(
                act.dma_start, out, K.layer(name, l), chunks).then_inc(params, 16)
            load(K.g_norm[:], "norm_g", KD)
            load(K.g_q[:], "q_norm_g", Q_LORA // P)
            load(K.g_kv[:], "kv_norm_g", KV_LORA // P)
            load(K.cb[:, 0], "conv_b", 2)
            load(K.cb[:, 1], "conv_ln_g", 2)
            load(K.cb[:, 2], "conv_ln_b", 2)
            load(K.g_branch[:], "branch_norm_g", KD)
            for c in range(2):
                act.dma_start(K.cw[:, c], i["conv_w"][bass.ds(l, 1), :, c * P:(c + 1) * P].rearrange(
                    "a k p -> p (a k)")).then_inc(params, 16)
            act.dma_start(K.sgb[:], i["sg_b"][bass.ds(l, 1)].rearrange("a g t -> t (a g)")).then_inc(params, 16)
            act.dma_start(K.sgw[:], i["sg_w"][bass.ds(l, 1)].rearrange("a g t s -> t (a g) s")).then_inc(params, 16)
            for out, name in ((K.pwb, "conv_pw_b"), (K.gqk[:, 0], "qk_q_g"), (K.gqk[:, 1], "qk_k_g"),
                              (K.sgln[:, 0], "sg_ln_g"), (K.sgln[:, 1], "sg_ln_b")):
                act.dma_start(out,
                               cast_rows(K.layer(name, l))).then_inc(params, 16)

        @block.tensor
        def _(pe):
            norm.pe(pe)
            for n, (kind, c0, width) in enumerate(IN_BLOCKS):
                pe.wait_ge(w_loaded[n % 2], 16 * (n // 2 + 1))
                if n == 0:
                    pe.wait_ge(h_ready, KD)
                if n >= 2:
                    pe.wait_ge(proj_out, n - 1)
                w, ps = K.wslot[n % 2], K.ps_pair[n % 2]
                if kind == "cols":
                    for c in range(width // P):
                        last = matmul_cols(nc, ps[:, c // 2, (c % 2) * SEQ:(c % 2 + 1) * SEQ], w,
                                           K.h_t, c, KD)
                else:
                    for t in range(TT):
                        last = matmul_rows(nc, ps[:, t, 0:width], K.h_t, w[:, :, 0:width], t, KD)
                last.then_inc(proj_ready, 1)

        @block.vector
        def _(dve):
            link = Link(dve, chain)
            norm.dve_norm(dve, link)
            dve.wait_ge(params, 16 * 16)
            norm.dve_scale(dve, K.g_norm, None, h_ready)
            for n, (kind, c0, width) in enumerate(IN_BLOCKS):
                dve.wait_ge(proj_ready, n + 1)
                ps = K.ps_pair[n % 2]
                if kind == "cols":
                    dst = K.glu if c0 == 0 else K.low[:, (c0 - C_CQ) // P:(c0 - C_CQ) // P + 4]
                    ins = nc.vector.tensor_copy(dst.rearrange("p c t -> p (c t)"),
                                                ps.rearrange("p b n -> p (b n)"))
                elif c0 == C_ZCONV:
                    ins = nc.vector.tensor_copy(K.zconv, ps[:, :, 0:width])
                else:
                    ins = nc.vector.tensor_copy(K.rows[:, :, c0 - C_ROWS:c0 - C_ROWS + width],
                                                ps[:, :, 0:width])
                ins.then_inc(proj_out, 1)


def stage_conv(K, S, l):
    nc, i = K.nc, K.i
    with S.open() as (block, sem):
        area = Area(K.arena, K.first_end)
        padded = area.take(2, SEQ + CONV_K - 1)
        gate, acc, xc, sq, rstd = (area.take(2, SEQ) for _ in range(5))
        sz = area.take(TT, CONV_W)
        chain, pw_loaded, gate_ready, acc_ready = sem("chain"), sem("pw_loaded"), sem("gate"), sem("acc")
        mean_ready, xc_ready, sq_ready, var_ready = sem("mean"), sem("xc"), sem("sq"), sem("var")
        veps_ready, sd_ready, ln_ready, silu_ready = sem("veps"), sem("sd"), sem("ln"), sem("silu")
        pw_ready = sem("pw_ready")
        pw = K.ring[:, 0:2 * CONV_W].rearrange("p (k n) -> p k n", k=2)
        mean_ps, var_ps = K.ps[:, 0, 0:SEQ], K.ps[:, 1, 0:SEQ]
        out_ps = K.ps[:, 2:4, 0:CONV_W]

        @block.sync
        def _(sp):
            sp.dma_start(pw, i["conv_pw_w"][bass.ds(l, 1)].rearrange("a (k p) n -> p (a k) n", p=P)
                         ).then_inc(pw_loaded, 16)

        @block.scalar
        def _(act):
            nc.scalar.activation(gate, K.glu[:, 2:4], ACT.Sigmoid).then_inc(gate_ready, 1)
            act.wait_ge(xc_ready, 1)
            nc.scalar.activation(sq, xc, ACT.Square).then_inc(sq_ready, 1)
            act.wait_ge(veps_ready, 1)
            nc.scalar.activation(rstd[:, 1], rstd[:, 0], ACT.Sqrt).then_inc(sd_ready, 1)
            act.wait_ge(ln_ready, 1)
            for c in range(2):
                nc.scalar.activation(acc[:, c], xc[:, c], ACT.Silu, bias=K.cb[:, 2, c:c + 1],
                                     scale=K.cb[:, 1, c:c + 1]).then_inc(silu_ready, 1)
            nc.scalar.activation(sz, K.zconv, ACT.Silu).then_inc(silu_ready, 1)

        @block.tensor
        def _(pe):
            pe.wait_ge(acc_ready, 1)
            for c in range(2):
                last = nc.tensor.matmul(mean_ps, K.ones[:], acc[:, c], start=(c == 0), stop=(c == 1))
            last.then_inc(mean_ready, 1)
            pe.wait_ge(sq_ready, 1)
            for c in range(2):
                last = nc.tensor.matmul(var_ps, K.ones[:], sq[:, c], start=(c == 0), stop=(c == 1))
            last.then_inc(var_ready, 1)
            pe.wait_ge(pw_loaded, 16)
            pe.wait_ge(silu_ready, 2)
            for t in range(TT):
                last = matmul_rows(nc, out_ps[:, t], acc, pw, t, 2)
            last.then_inc(pw_ready, 1)

        @block.vector
        def _(dve):
            link = Link(dve, chain)
            nc.vector.memset(padded[:, :, 0:CONV_K - 1], 0.0)
            dve.wait_ge(gate_ready, 1)
            link(nc.vector.tensor_tensor(padded[:, :, CONV_K - 1:], K.glu[:, 0:2], gate, ALU.mult))
            for j in range(CONV_K):
                for c in range(2):
                    w = K.cw[:, c, j:j + 1]
                    if j == 0:
                        ins = nc.vector.tensor_scalar(acc[:, c], padded[:, c, 0:SEQ], w,
                                                      K.cb[:, 0, c:c + 1], ALU.mult, ALU.add)
                    else:
                        ins = nc.vector.scalar_tensor_tensor(acc[:, c], padded[:, c, j:j + SEQ], w,
                                                             acc[:, c], ALU.mult, ALU.add)
                    if c == 1 and j < CONV_K - 1:
                        link(ins)
            ins.then_inc(acc_ready, 1)
            dve.wait_ge(mean_ready, 1)
            for c in range(2):
                ins = nc.vector.scalar_tensor_tensor(xc[:, c], mean_ps, -1.0 / CONV_W, acc[:, c],
                                                     ALU.mult, ALU.add)
            ins.then_inc(xc_ready, 1)
            dve.wait_ge(var_ready, 1)
            nc.vector.tensor_scalar(rstd[:, 0], var_ps, 1.0 / CONV_W, EPS, ALU.mult,
                                    ALU.add).then_inc(veps_ready, 1)
            dve.wait_ge(sd_ready, 1)
            link(nc.vector.reciprocal(rstd[:, 0], rstd[:, 1]))
            for c in range(2):
                ins = nc.vector.tensor_tensor(xc[:, c], xc[:, c], rstd[:, 0], ALU.mult)
            ins.then_inc(ln_ready, 1)
            dve.wait_ge(silu_ready, 3)
            dve.wait_ge(pw_ready, 1)
            for t in range(TT):
                link(nc.vector.tensor_tensor(K.y[:, t, 0:CONV_W], out_ps[:, t], K.pwb[:], ALU.add))
            link(nc.vector.tensor_tensor(K.y[:, :, 0:CONV_W], K.y[:, :, 0:CONV_W], sz, ALU.mult))


def rms_rstd_dve(nc, link, out, sums, n):
    return nc.vector.tensor_scalar(out, sums, 1.0 / n, EPS, ALU.mult, ALU.add)


def stage_mla_heads(K, S, l):
    nc, i = K.nc, K.i
    NQ, NKV = Q_LORA // P, KV_LORA // P
    with S.open() as (block, sem):
        area = Area(K.arena, K.first_end)
        sq = area.take(NQ + NKV, SEQ)
        q = area.take(TT, HEADS, QK)
        k = area.take(TT, HEADS, QK)
        hsq = area.take(TT, HEADS, QK)
        rot = area.take(4, TT, HEADS, HALF)
        st = area.take(3, 2, TT)
        hst = area.take(3, 2, TT * HEADS)
        chain, w_loaded, sq_ready, st_ready = sem("chain"), sem("w_loaded"), sem("sq"), sem("st")
        scaled, vst_ready, sd_ready, up_ready = sem("scaled"), sem("vst"), sem("sd"), sem("up")
        hv_ready, hsd_ready, qk_ready, tr_ready = sem("hv"), sem("hsd"), sem("qk"), sem("tr")
        tr_out, act_chain = sem("tr_out"), sem("act_chain")
        w_uq = K.big[:, 0:NQ * HEADS * QK].rearrange("p (k n) -> p k n", k=NQ)
        w_ukv = K.big[:, NQ * HEADS * QK:NQ * HEADS * QK + NKV * 1024].rearrange("p (k n) -> p k n", k=NKV)
        st_ps = K.ps[:, 7]

        @block.sync
        def _(sp):
            sp.dma_start(w_uq, i["w_uq"][bass.ds(l, 1)].rearrange("a (k p) n -> p (a k) n", p=P)
                         ).then_inc(w_loaded, 16)
            sp.dma_start(w_ukv, i["w_ukv"][bass.ds(l, 1)].rearrange("a (k p) n -> p (a k) n", p=P)
                         ).then_inc(w_loaded, 16)

        @block.scalar
        def _(act):
            nc.scalar.activation(sq, K.low, ACT.Square).then_inc(sq_ready, 1)
            act.wait_ge(sq_ready, 1)
            for c in range(NQ + NKV):
                g = K.g_q[:, c:c + 1] if c < NQ else K.g_kv[:, c - NQ:c - NQ + 1]
                nc.scalar.activation(K.low[:, c], K.low[:, c], ACT.Copy, scale=g).then_inc(scaled, 1)
            act.wait_ge(vst_ready, 1)
            nc.scalar.activation(st[:, 2], st[:, 1], ACT.Sqrt).then_inc(sd_ready, 1)
            act.wait_ge(hv_ready, 1)
            nc.scalar.activation(hst[:, 2], hst[:, 1], ACT.Sqrt).then_inc(hsd_ready, 1)

        @block.tensor
        def _(pe):
            pe.wait_ge(sq_ready, 1)
            for n, (c0, c1) in enumerate(((0, NQ), (NQ, NQ + NKV))):
                for t in range(TT):
                    for c in range(c0, c1):
                        last = nc.tensor.matmul(st_ps[:, n * TT + t:n * TT + t + 1],
                                                sq[:, c, t * P:(t + 1) * P], K.ones[:, 0:1],
                                                start=(c == c0), stop=(c == c1 - 1))
            last.then_inc(st_ready, 1)
            pe.wait_ge(w_loaded, 32)
            pe.wait_ge(scaled, NQ + NKV)
            pe.wait_ge(vst_ready, 1)
            for t in range(TT):
                for half in range(2):
                    matmul_rows(nc, K.ps[:, 4 * t + half, 0:4 * QK], K.low[:, 0:NQ],
                                w_uq[:, :, half * 4 * QK:(half + 1) * 4 * QK], t, NQ)
                for half in range(2):
                    last = matmul_rows(nc, K.ps[:, 4 * t + 2 + half], K.low[:, NQ:],
                                       w_ukv[:, :, half * 512:(half + 1) * 512], t, NKV)
                last.then_inc(up_ready, 1)
            for n, src in enumerate((q, k)):
                pe.wait_ge(qk_ready, n + 1)
                for h in range(HEADS):
                    b = (n * 4 + h // 2)
                    for t in range(TT):
                        last = nc.tensor.transpose(
                            K.ps[0:QK, b, (h % 2) * SEQ + t * P:(h % 2) * SEQ + (t + 1) * P],
                            src[:, t, h], K.ident[:])
                    if h % 2:
                        last.then_inc(tr_ready, 1)

        @block.vector
        def _(dve):
            link = Link(dve, chain)
            dve.wait_ge(st_ready, 1)
            for n, width in enumerate((Q_LORA, KV_LORA)):
                ins = nc.vector.tensor_scalar(st[:, 1, n], st_ps[:, n * TT:(n + 1) * TT], 1.0 / width,
                                              EPS, ALU.mult, ALU.add)
                if n == 0:
                    link(ins)
            ins.then_inc(vst_ready, 1)
            dve.wait_ge(sd_ready, 1)
            link(nc.vector.reciprocal(st[:, 0], st[:, 2]))
            for t in range(TT):
                dve.wait_ge(up_ready, t + 1)
                for half in range(2):
                    hs = slice(4 * half, 4 * half + 4)
                    nc.vector.tensor_scalar(
                        q[:, t, hs].rearrange("p h d -> p (h d)"), K.ps[:, 4 * t + half, 0:4 * QK],
                        st[:, 0, 0, t:t + 1], None, ALU.mult)
                    kv = K.ps[:, 4 * t + 2 + half].rearrange("p (h d) -> p h d", h=4)
                    nc.vector.tensor_scalar(k[:, t, hs, 0:NOPE], kv[:, :, 0:NOPE],
                                            st[:, 0, 1, t:t + 1], None, ALU.mult)
                    nc.vector.tensor_scalar(K.v[:, t, hs], kv[:, :, NOPE:], st[:, 0, 1, t:t + 1],
                                            None, ALU.mult)
                link(nc.vector.tensor_copy(
                    k[:, t, :, NOPE:],
                    K.rows[:, t, R_ROPE:R_ROPE + ROPE].unsqueeze(1).broadcast_to([P, HEADS, ROPE])))
            flat = lambda a: a.rearrange("p t h d -> p (t h) d")
            for n, src in enumerate((q, k)):
                link(nc.vector.tensor_tensor(hsq, src, src, ALU.mult))
                link(nc.vector.tensor_reduce(hst[:, 0, n], flat(hsq), AX.X, ALU.add))
            nc.vector.tensor_scalar(hst[:, 1], hst[:, 0], 1.0 / QK, EPS, ALU.mult,
                                    ALU.add).then_inc(hv_ready, 1)
            dve.wait_ge(hsd_ready, 1)
            link(nc.vector.reciprocal(hst[:, 0], hst[:, 2]))
            for n, src in enumerate((q, k)):
                link(nc.vector.tensor_tensor(
                    flat(src), flat(src),
                    hst[:, 0, n].unsqueeze(2).broadcast_to([P, TT * HEADS, QK]), ALU.mult))
                link(nc.vector.tensor_tensor(
                    flat(src), flat(src),
                    K.gqk[:, n].unsqueeze(1).broadcast_to([P, TT * HEADS, QK]), ALU.mult))
                for t in range(TT):
                    x1, x2 = src[:, t, :, NOPE:NOPE + HALF], src[:, t, :, NOPE + HALF:]
                    cos = K.cos[:, t].unsqueeze(1).broadcast_to([P, HEADS, HALF])
                    sin = K.sin[:, t].unsqueeze(1).broadcast_to([P, HEADS, HALF])
                    nc.vector.tensor_tensor(rot[:, 0, t], x1, cos, ALU.mult)
                    nc.vector.tensor_tensor(rot[:, 1, t], x2, sin, ALU.mult)
                    nc.vector.tensor_tensor(rot[:, 2, t], x1, sin, ALU.mult)
                    link(nc.vector.tensor_tensor(rot[:, 3, t], x2, cos, ALU.mult))
                    nc.vector.tensor_tensor(x1, rot[:, 0, t], rot[:, 1, t], ALU.subtract)
                    ins = nc.vector.tensor_tensor(x2, rot[:, 2, t], rot[:, 3, t], ALU.add)
                    if t == 0:
                        link(ins)
                link(ins)
                dve.sem_inc(qk_ready, 1)
            for n, dst in enumerate((K.q_t, K.k_t)):
                for b in range(4):
                    dve.wait_ge(tr_ready, n * 4 + b + 1)
                    nc.vector.tensor_copy(dst[0:QK, 2 * b:2 * b + 2].rearrange("p h t -> p (h t)"),
                                          K.ps[0:QK, n * 4 + b]).then_inc(tr_out, 1)
            dve.wait_ge(tr_out, 8)


def stage_attention(K, S, l):
    nc = K.nc
    scale = float(QK) ** -0.5
    with S.open() as (block, sem):
        area = Area(K.arena, K.first_end)
        s = area.take(2, 4, SEQ)
        mx = area.take(2, 4)
        sums = area.take(TT, HEADS)
        p_t = area.take(2, 4, TT, P)
        sz = area.take(TT, MLA_W)
        chain, s_ready, s_out = sem("chain"), sem("s_ready"), sem("s_out")
        e_ready, pt_ready, pt_out, o_ready = sem("e_ready"), sem("pt_ready"), sem("pt_out"), sem("o_ready")
        silu_ready, max_ready = sem("silu_ready"), sem("max_ready")
        groups = [(t, g) for t in range(TT) for g in range(2)]

        def s_ps(n, keys):
            return K.ps[:, 2 * (n % 2):2 * (n % 2) + 2].rearrange("p b (h c) -> p (b h) c", h=2)[:, :, 0:keys]

        @block.tensor
        def _(pe):
            def scores(n):
                t, g = groups[n]
                if n >= 2:
                    pe.wait_ge(s_out, n - 1)
                for h in range(4):
                    last = nc.tensor.matmul(s_ps(n, (t + 1) * P)[:, h],
                                            K.q_t[0:QK, 4 * g + h, t * P:(t + 1) * P],
                                            K.k_t[0:QK, 4 * g + h, 0:(t + 1) * P], start=True, stop=True)
                last.then_inc(s_ready, 1)

            scores(0)
            for n, (t, g) in enumerate(groups):
                if n + 1 < len(groups):
                    scores(n + 1)
                pe.wait_ge(e_ready, 4 * (n + 1))
                if n >= 1:
                    pe.wait_ge(pt_out, n)
                for h in range(4):
                    for kt in range(t + 1):
                        last = nc.tensor.transpose(
                            K.ps[:, 4 + h // 2, (h % 2) * SEQ + kt * P:(h % 2) * SEQ + (kt + 1) * P],
                            s[:, n % 2, h, kt * P:(kt + 1) * P], K.ident[:])
                last.then_inc(pt_ready, 1)
                pe.wait_ge(pt_out, n + 1)
                for h in range(4):
                    for kt in range(t + 1):
                        last = nc.tensor.matmul(K.ps[:, 6 + t, (4 * g + h) * VD:(4 * g + h + 1) * VD],
                                                p_t[:, n % 2, h, kt], K.v[:, kt, 4 * g + h],
                                                start=(kt == 0), stop=(kt == t))
                last.then_inc(o_ready, 1)

        @block.scalar
        def _(act):
            nc.scalar.activation(sz, K.rows[:, :, R_ZMLA:R_ZMLA + MLA_W], ACT.Silu).then_inc(silu_ready, 1)
            for n, (t, g) in enumerate(groups):
                keys = (t + 1) * P
                act.wait_ge(max_ready, n + 1)
                for h in range(4):
                    nc.scalar.activation(s[:, n % 2, h, 0:keys], s[:, n % 2, h, 0:keys], ACT.Exp,
                                         bias=mx[:, n % 2, h:h + 1],
                                         accum_out=sums[:, t, 4 * g + h:4 * g + h + 1]
                                         ).then_inc(e_ready, 1)

        @block.vector
        def _(dve):
            link = Link(dve, chain)

            def probabilities_out(n):
                t, g = groups[n]
                dve.wait_ge(pt_ready, n + 1)
                if n >= 2:
                    dve.wait_ge(o_ready, n - 1)
                src = K.ps[:, 4:6].rearrange("p b (h c) -> p (b h) c", h=2)[:, :, 0:(t + 1) * P]
                nc.vector.tensor_copy(p_t[:, n % 2].rearrange("p h a b -> p h (a b)")[:, :, 0:(t + 1) * P],
                                      src).then_inc(pt_out, 1)

            for n, (t, g) in enumerate(groups):
                keys = (t + 1) * P
                dve.wait_ge(s_ready, n + 1)
                if n >= 2:
                    dve.wait_ge(pt_ready, n - 1)
                if t:
                    nc.vector.tensor_scalar(s[:, n % 2, :, 0:t * P], s_ps(n, keys)[:, :, 0:t * P], scale,
                                            None, ALU.mult)
                link(nc.vector.scalar_tensor_tensor(
                    s[:, n % 2, :, t * P:keys], s_ps(n, keys)[:, :, t * P:keys], scale,
                    K.causal[:].unsqueeze(1).broadcast_to([P, 4, P]), ALU.mult, ALU.add))
                dve.sem_inc(s_out, 1)
                if n >= 2:
                    dve.wait_ge(e_ready, 4 * (n - 1))
                link(nc.vector.tensor_reduce(mx[:, n % 2], s[:, n % 2, :, 0:keys], AX.X, ALU.max))
                nc.vector.tensor_scalar(mx[:, n % 2], mx[:, n % 2], -1.0, None,
                                        ALU.mult).then_inc(max_ready, 1)
                if n >= 1:
                    probabilities_out(n - 1)
            probabilities_out(len(groups) - 1)
            dve.wait_ge(o_ready, 4)
            dve.wait_ge(silu_ready, 1)
            link(nc.vector.reciprocal(sums, sums))
            for t in range(TT):
                y = K.y[:, t, CONV_W:CONV_W + MLA_W]
                link(nc.vector.tensor_tensor(
                    y.rearrange("p (h d) -> p h d", h=HEADS),
                    K.ps[:, 6 + t].rearrange("p (h d) -> p h d", h=HEADS),
                    sums[:, t].unsqueeze(2).broadcast_to([P, HEADS, VD]), ALU.mult))
                link(nc.vector.tensor_tensor(y, y, sz[:, t], ALU.mult))


def stage_sgu(K, S, l):
    nc = K.nc
    with S.open() as (block, sem):
        area = Area(K.arena, K.first_end)
        u, v, sz, mixed = (area.take(TT, SG_W) for _ in range(4))
        w_t = area.take(SG_HEADS, P)
        bn = area.take(TT, 6)
        mv = area.take(TT, 2)
        sd = area.take(TT, 2)
        chain, act_done, veps, sd_ready = sem("chain"), sem("act_done"), sem("veps"), sem("sd")
        w_ready, w_out, w_kept, v_ready, mix_ready = (sem("w_ready"), sem("w_out"), sem("w_kept"),
                                                      sem("v_ready"), sem("mix_ready"))

        @block.scalar
        def _(act):
            nc.scalar.activation(v, K.rows[:, :, R_V:R_V + SG_W], ACT.Gelu_apprx_tanh).then_inc(act_done, 1)
            nc.scalar.activation(u, K.rows[:, :, R_U:R_U + SG_W], ACT.Gelu_apprx_tanh).then_inc(act_done, 1)
            act.wait_ge(veps, 1)
            nc.scalar.activation(sd[:, :, 1], sd[:, :, 0], ACT.Sqrt).then_inc(sd_ready, 1)
            nc.scalar.activation(sz, K.rows[:, :, R_ZSG:R_ZSG + SG_W], ACT.Silu).then_inc(act_done, 1)

        @block.gpsimd
        def _(pool):
            pool.wait_ge(w_out, 1)
            nc.gpsimd.affine_select(out=w_t, in_=w_t, compare_op=ALU.is_ge, fill=0.0, base=0,
                                    pattern=[[0, SG_HEADS], [1, P]], channel_multiplier=-1).then_inc(w_kept, 1)

        @block.tensor
        def _(pe):
            for g in range(SG_HEADS):
                last = nc.tensor.transpose(K.ps[:, 0, g * P:(g + 1) * P], K.sgw[:, g], K.ident[:])
            last.then_inc(w_ready, 1)
            pe.wait_ge(w_kept, 1)
            pe.wait_ge(v_ready, 1)
            for t in range(TT):
                for g in range(SG_HEADS):
                    last = nc.tensor.matmul(K.ps[:, 1 + t, g * SG_D:(g + 1) * SG_D], w_t[:, g],
                                            v[:, t, g * SG_D:(g + 1) * SG_D], start=True, stop=True)
            last.then_inc(mix_ready, 1)

        @block.vector
        def _(dve):
            link = Link(dve, chain)
            dve.wait_ge(w_ready, 1)
            nc.vector.tensor_copy(w_t.rearrange("p g s -> p (g s)"), K.ps[:, 0]).then_inc(w_out, 1)
            dve.wait_ge(act_done, 1)
            for t in range(TT):
                link(nc.vector.bn_stats(bn[:, t], v[:, t]))
                link(nc.vector.bn_aggr(mv[:, t], bn[:, t]))
            nc.vector.tensor_scalar(sd[:, :, 0], mv[:, :, 1], EPS, None, ALU.add).then_inc(veps, 1)
            dve.wait_ge(sd_ready, 1)
            link(nc.vector.reciprocal(sd[:, :, 0], sd[:, :, 1]))
            for t in range(TT):
                link(nc.vector.tensor_scalar(v[:, t], v[:, t], mv[:, t, 0:1], sd[:, t, 0:1],
                                             ALU.subtract, ALU.mult))
                link(nc.vector.tensor_tensor(v[:, t], v[:, t], K.sgln[:, 0], ALU.mult))
                link(nc.vector.tensor_tensor(v[:, t], v[:, t], K.sgln[:, 1], ALU.add))
            dve.sem_inc(v_ready, 1)
            dve.wait_ge(act_done, 3)
            link(nc.vector.tensor_tensor(u, u, sz, ALU.mult))
            dve.wait_ge(mix_ready, 1)
            for t in range(TT):
                link(nc.vector.tensor_tensor(
                    mixed[:, t].rearrange("p (g d) -> p g d", g=SG_HEADS),
                    K.ps[:, 1 + t, 0:SG_W].rearrange("p (g d) -> p g d", g=SG_HEADS),
                    K.sgb[:].unsqueeze(2).broadcast_to([P, SG_HEADS, SG_D]), ALU.add))
                link(nc.vector.tensor_tensor(K.y[:, t, CONV_W + MLA_W:], mixed[:, t], u[:, t], ALU.mult))


BRANCHES = ((0, CONV_W), (CONV_W, CONV_W + MLA_W), (CONV_W + MLA_W, D))


def stage_out_projection(K, S, l):
    nc, i = K.nc, K.i
    with S.open() as (block, sem):
        area = Area(K.arena, K.first_end)
        sq = area.take(TT, D)
        st = area.take(3, 3, TT)
        chain, w_loaded, ms_ready, var_ready = sem("chain"), sem("w_loaded"), sem("ms"), sem("var")
        sd_ready, yn_ready, yt_ready, y_out, o_ready = (sem("sd"), sem("yn"), sem("yt"), sem("y_out"),
                                                        sem("o_ready"))
        w = K.big.rearrange("p (k n) -> p k n", k=KD)

        @block.sync
        def _(sp):
            sp.dma_start(w, i["w_out"][bass.ds(l, 1)].rearrange("a (k p) n -> p (a k) n", p=P)
                         ).then_inc(w_loaded, 16)

        @block.scalar
        def _(act):
            for b, (c0, c1) in enumerate(BRANCHES):
                for t in range(TT):
                    nc.scalar.activation(sq[:, t, c0:c1], K.y[:, t, c0:c1], ACT.Square,
                                         accum_out=st[:, 0, b, t:t + 1]).then_inc(ms_ready, 1)
            act.wait_ge(var_ready, 1)
            nc.scalar.activation(st[:, 2], st[:, 1], ACT.Sqrt).then_inc(sd_ready, 1)

        @block.tensor
        def _(pe):
            pe.wait_ge(yn_ready, 1)
            for k in range(KD):
                for t in range(TT):
                    last = nc.tensor.transpose(K.ps_low[:, k, t * P:(t + 1) * P],
                                               K.y[:, t, k * P:(k + 1) * P], K.ident[:])
                last.then_inc(yt_ready, 1)
            pe.wait_ge(w_loaded, 16)
            pe.wait_ge(y_out, KD)
            for t in range(TT):
                for half in range(2):
                    last = matmul_rows(nc, K.ps[:, 4 + 2 * t + half], K.h_t,
                                       w[:, :, half * 512:(half + 1) * 512], t, KD)
                last.then_inc(o_ready, 1)

        @block.vector
        def _(dve):
            link = Link(dve, chain)
            dve.wait_ge(ms_ready, 6)
            for b, (c0, c1) in enumerate(BRANCHES):
                link(nc.vector.tensor_scalar(st[:, 1, b], st[:, 0, b], 1.0 / (c1 - c0), EPS, ALU.mult,
                                             ALU.add))
            dve.sem_inc(var_ready, 1)
            dve.wait_ge(sd_ready, 1)
            link(nc.vector.reciprocal(st[:, 0], st[:, 2]))
            for b, (c0, c1) in enumerate(BRANCHES):
                for t in range(TT):
                    link(nc.vector.tensor_scalar(K.y[:, t, c0:c1], K.y[:, t, c0:c1],
                                                 st[:, 0, b, t:t + 1], None, ALU.mult))
            dve.sem_inc(yn_ready, 1)
            for k in range(KD):
                dve.wait_ge(yt_ready, 2 * (k // 2) + 2)
                nc.vector.tensor_scalar(K.h_t[:, k], K.ps_low[:, k], K.g_branch[:, k:k + 1], None,
                                        ALU.mult).then_inc(y_out, 1)
            for t in range(TT):
                dve.wait_ge(o_ready, t + 1)
                link(nc.vector.tensor_tensor(
                    K.x[:, t], K.x[:, t],
                    K.ps[:, 4 + 2 * t:6 + 2 * t].rearrange("p b n -> p (b n)"), ALU.add))


def first_block(K, S):
    with K.nc.Fori(0, DEPTH) as l:
        stage_in_projection(K, S, l)
        stage_conv(K, S, l)
        stage_mla_heads(K, S, l)
        stage_attention(K, S, l)
        stage_sgu(K, S, l)
        stage_out_projection(K, S, l)



D5 = 5 * D
HG = 8
HD = D // HG
CH = SEQ // P
PRE = P + 1
LEVELS = [64, 32, 16, 8, 4, 2, 1]
LRU_BLOCKS = 4
LRU_BW = D // LRU_BLOCKS
TAPS = 4
LEFT = 2
LRU_C = 8.0
PH = 8
NKEYS = 128
TOPK = 16
HP = 2 * PH
BIG = 3.0e38


def stage_modulation(K, S, l):
    nc, i = K.nc, K.i
    with S.open() as (block, sem):
        area = Area(K.arena)
        mod = area.take(6, D)
        diag = area.take(KD, P)
        cols = area.take(4, KD)
        cc = area.take(KD)
        cb = area.take(KD, P)
        gains = area.take(2, KD)
        chain, loaded, b_loaded, c_ready, cb_ready = (sem("chain"), sem("loaded"), sem("b_loaded"),
                                                      sem("c_ready"), sem("cb_ready"))
        w_loaded = [sem("w_loaded0"), sem("w_loaded1")]
        half_done, half_out = sem("half_done"), sem("half_out")

        @block.sync
        def _(sp):
            def load(n, half):
                src = i["w_ada_2"][l, :, bass.ds(n * D + half * 512, 512)]
                sp.dma_start(K.wslot[half], src.rearrange("(k p) n -> p k n", p=P)).then_inc(w_loaded[half], 16)

            for half in range(2):
                load(0, half)
            with sp.Fori(0, 5) as n:
                for half in range(2):
                    sp.wait_ge(half_done, 2 * n + half + 1)
                    load(n + 1, half)

        @block.scalar
        def _(act):
            load_cols(act.dma_start, cc, i["c_2"], KD).then_inc(loaded, 16)
            for n in range(2):
                load_cols(act.dma_start, gains[:, n], i["norm_g_2"][l, n:n + 1], KD).then_inc(loaded, 16)
            act.dma_start(mod.rearrange("p v d -> p (v d)"),
                          i["b_ada_2"][l:l + 1].broadcast_to([P, 6 * D])).then_inc(b_loaded, 16)
            act.wait_ge(loaded, 48)
            nc.scalar.activation(cc, cc, ACT.Silu).then_inc(c_ready, 1)

        @block.tensor
        def _(pe):
            pe.wait_ge(cb_ready, 1)

            def vector(n, wait_out):
                for half in range(2):
                    pe.wait_ge(w_loaded[half], 16 * (n + 1))
                    if wait_out is not None:
                        pe.wait_ge(half_out, wait_out + half)
                    for k in range(KD):
                        last = nc.tensor.matmul(K.ps[:, half], cb[:, k], K.wslot[half][:, k],
                                                start=(k == 0), stop=(k == KD - 1))
                    last.then_inc(half_done, 1)

            vector(0, None)
            with pe.Fori(1, 6) as n:
                vector(n, 2 * n - 1)

        @block.vector
        def _(dve):
            link = Link(dve, chain)
            dve.wait_ge(c_ready, 1)
            nc.vector.tensor_copy(cb, cc.unsqueeze(2).broadcast_to([P, KD, P])).then_inc(cb_ready, 1)
            dve.wait_ge(b_loaded, 16)
            flat = mod.rearrange("p v d -> p (v d)")
            with dve.Fori(0, 6) as n:
                for half in range(2):
                    dve.wait_ge(half_done, 2 * n + half + 1)
                    piece = flat[:, bass.ds(n * D + half * 512, 512)]
                    nc.vector.tensor_tensor(piece, piece, K.ps[:, half], ALU.add).then_inc(half_out, 1)
            dve.wait_ge(half_out, 12)
            for n, v in enumerate((2, 5)):
                nc.vector.tensor_copy(K.gate[:, n], mod[:, v])
            for n, v in enumerate((0, 1, 3, 4)):
                link(nc.vector.tensor_tensor(diag, mod[:, v].rearrange("p (k c) -> p k c", k=KD),
                                             K.ident[:].unsqueeze(1).broadcast_to([P, KD, P]), ALU.mult))
                link(nc.vector.tensor_reduce(cols[:, n], diag, AX.X, ALU.add))
            for n in range(2):
                nc.vector.tensor_copy(K.shift[:, n], cols[:, 2 * n])
                link(nc.vector.scalar_tensor_tensor(K.gain[:, n], cols[:, 2 * n + 1], 1.0, gains[:, n],
                                                    ALU.add, ALU.mult))


def stage_projection(K, S, gain, shift, source, blocks, area_at):
    nc = K.nc
    with S.open() as (block, sem):
        norm = NormTranspose(K, sem, Area(K.arena, area_at))
        chain, h_ready = sem("chain"), sem("h_ready")
        w_loaded = [sem("w_loaded0"), sem("w_loaded1")]
        proj_ready, proj_out = sem("proj_ready"), sem("proj_out")

        @block.sync
        def _(sp):
            for n, (_, c0, _) in enumerate(blocks):
                if n >= 2:
                    sp.wait_ge(proj_ready, n - 1)
                sp.dma_start(K.wslot[n % 2], source[:, c0:c0 + 512].rearrange("(k p) n -> p k n", p=P)
                             ).then_inc(w_loaded[n % 2], 16)

        @block.scalar
        def _(act):
            norm.act(act)

        @block.tensor
        def _(pe):
            norm.pe(pe)
            pe.wait_ge(h_ready, KD)
            for n, (kind, _, _) in enumerate(blocks):
                pe.wait_ge(w_loaded[n % 2], 16 * (n // 2 + 1))
                if n >= 2:
                    pe.wait_ge(proj_out, n - 1)
                w, ps = K.wslot[n % 2], K.ps_pair[n % 2]
                if kind == "cols":
                    for c in range(4):
                        last = matmul_cols(nc, ps[:, c // 2, (c % 2) * SEQ:(c % 2 + 1) * SEQ], w,
                                           K.h_t, c, KD)
                else:
                    for t in range(TT):
                        last = matmul_rows(nc, ps[:, t], K.h_t, w, t, KD)
                last.then_inc(proj_ready, 1)

        @block.vector
        def _(dve):
            link = Link(dve, chain)
            norm.dve_norm(dve, link)
            norm.dve_scale(dve, gain, shift, h_ready)
            for n, (kind, _, dst) in enumerate(blocks):
                dve.wait_ge(proj_ready, n + 1)
                ps = K.ps_pair[n % 2]
                if kind == "cols":
                    ps = ps.rearrange("p b (c t) -> p (b c) t", c=2)
                nc.vector.tensor_copy(dst, ps).then_inc(proj_out, 1)


def residual_out(K, dve, link, w_gate, o_ready, tmp):
    nc = K.nc
    for t in range(TT):
        dve.wait_ge(o_ready, t + 1)
        link(nc.vector.tensor_tensor(tmp, K.ps[:, 4 + 2 * t:6 + 2 * t].rearrange("p b n -> p (b n)"),
                                     w_gate, ALU.mult))
        link(nc.vector.tensor_tensor(K.x[:, t], K.x[:, t], tmp, ALU.add))


def product_out(K, pe, w, o_ready):
    for t in range(TT):
        for half in range(2):
            last = matmul_rows(K.nc, K.ps[:, 4 + 2 * t + half], K.h_t, w[:, :, half * 512:(half + 1) * 512],
                               t, KD)
        last.then_inc(o_ready, 1)



def hg_memory(K):
    area = Area(K.arena)
    H = Names()
    H.q = area.take(HG, CH, P)
    H.k = area.take(2, HG, CH, P)
    H.v = area.take(TT, D)
    H.g = area.take(TT, D)
    H.pre = area.take(2, HG * CH, PRE)
    H.at = area.take(HG, 4, P)
    H.masks = area.take(HG * P // 4).bitcast(U8).rearrange("p (l t) -> p l t", l=8)
    H.end = area.at
    return H


def stage_hg_gates(K, S, H):
    nc, i = K.nc, K.i
    with S.open() as (block, sem):
        area = Area(K.arena, H.end)
        lb = area.take(4, HG)
        carry = area.take(HG * CH, PRE)
        px = area.take(P).bitcast(I32)
        tx = area.take(P).bitcast(I32)
        m = area.take(P).bitcast(I32)
        chain, loaded, iotas, sig_ready = sem("chain"), sem("loaded"), sem("iotas"), sem("sig")
        lb_ready, exp_ready, f_ready, ln_ready = sem("lb"), sem("exp"), sem("f"), sem("ln")
        k_flat = H.k.rearrange("p d h c t -> p (d h c t)")

        @block.sync
        def _(sp):
            load_cols(sp.dma_start, lb[:, 0], i["hg_lb_2"], HG).then_inc(loaded, 16)

        @block.gpsimd
        def _(pool):
            nc.gpsimd.memset(carry, 1.0).then_inc(iotas, 1)
            nc.gpsimd.iota(px, pattern=[[0, P]], base=0, channel_multiplier=1).then_inc(iotas, 1)
            nc.gpsimd.iota(tx, pattern=[[1, P]], base=0, channel_multiplier=0).then_inc(iotas, 1)
            pool.wait_ge(iotas, 3)
            nc.gpsimd.memset(carry[:, :, 0:1], 0.0).then_inc(iotas, 1)

        @block.scalar
        def _(act):
            nc.scalar.activation(k_flat, k_flat, ACT.Sigmoid).then_inc(sig_ready, 1)
            act.wait_ge(lb_ready, 1)
            nc.scalar.activation(lb[:, 2], lb[:, 1], ACT.Exp).then_inc(exp_ready, 1)
            act.wait_ge(f_ready, 1)
            for d in range(2):
                nc.scalar.activation(H.pre[:, d, :, 1:], H.k[:, d].rearrange("p h c t -> p (h c) t"),
                                     ACT.Ln).then_inc(ln_ready, 1)

        @block.vector
        def _(dve):
            link = Link(dve, chain)
            dve.wait_ge(loaded, 16)
            nc.vector.tensor_tensor(lb[:, 1], lb[:, 0], lb[:, 0], ALU.subtract).then_inc(lb_ready, 1)
            dve.wait_ge(exp_ready, 1)
            link(nc.vector.reciprocal(lb[:, 3], lb[:, 2]))
            link(nc.vector.tensor_tensor(lb[:, 3], lb[:, 3], lb[:, 2], ALU.mult))
            link(nc.vector.tensor_tensor(lb[:, 0], lb[:, 3], lb[:, 3], ALU.subtract))
            link(nc.vector.tensor_scalar(lb[:, 1], lb[:, 0], -1.0, 1.0, ALU.mult, ALU.add))
            dve.wait_ge(sig_ready, 1)
            for d in range(2):
                for h in range(HG):
                    f = H.k[:, d, h].rearrange("p c t -> p (c t)")
                    ins = nc.vector.tensor_scalar(f, f, lb[:, 1, h:h + 1], lb[:, 0, h:h + 1], ALU.mult,
                                                  ALU.add)
            ins.then_inc(f_ready, 1)
            dve.wait_ge(iotas, 4)
            link(nc.vector.tensor_tensor(m, px, tx, ALU.bitwise_xor))
            link(nc.vector.memset(H.pre[:, :, :, 0:1], 0.0))
            dve.wait_ge(ln_ready, 2)
            for d in range(2):
                flat = H.pre[:, d].rearrange("p n t -> p (n t)")
                nc.vector.tensor_tensor_scan(flat, carry.rearrange("p n t -> p (n t)"), flat, 0.0,
                                             ALU.mult, ALU.add)
            link(nc.vector.tensor_scalar(k_flat, k_flat, -1.0, 1.0, ALU.mult, ALU.add))
            for n, L in enumerate(LEVELS):
                link(nc.vector.tensor_scalar(px, m, float(L), None, ALU.is_ge))
                link(nc.vector.scalar_tensor_tensor(H.masks[:, n], m, float(2 * L), px, ALU.is_lt, ALU.mult))
            link(nc.vector.tensor_scalar(H.masks[:, 7], m, 0.0, None, ALU.is_equal))


def stage_hg_attention(K, S, H):
    nc = K.nc
    NL = len(LEVELS)
    with S.open() as (block, sem):
        area = Area(K.arena, H.end)
        kq = area.take(2, 2, HG * CH * P)
        chain, exps, exp_done, pair_ready = sem("chain"), sem("exps"), sem("exp_done"), sem("pair_ready")
        a_ready, a_out = sem("a_ready"), sem("a_out")
        pool_chain = sem("pool_chain")
        q = H.q.rearrange("p h c t -> p (h c) t")
        kf, kb = (H.k[:, d].rearrange("p h c t -> p (h c) t") for d in range(2))
        kk = H.k
        pf, pb = H.pre[:, 0], H.pre[:, 1]

        def halves(a, L):
            return a.rearrange("p n (b s j) -> p n b s j", s=2, j=L)

        def middle(pre, L):
            m = pre[:, :, 0:P].rearrange("p n (b s j) -> p n b s j", s=2, j=L)[:, :, :, 1, 0:1]
            return m.broadcast_to([P, HG * CH, P // (2 * L), L])

        @block.vector
        def _(dve):
            link = Link(dve, chain)

            def exponents(n):
                if n >= 2:
                    dve.wait_ge(a_ready, n - 1)
                L = LEVELS[n]
                ek, eq = (kq[:, n % 2, w].rearrange("p (n t) -> p n t", t=P) for w in range(2))
                ek, eq = halves(ek, L), halves(eq, L)
                inc = lambda pre: pre[:, :, 1:].rearrange("p n (b s j) -> p n b s j", s=2, j=L)
                exc = lambda pre: pre[:, :, 0:P].rearrange("p n (b s j) -> p n b s j", s=2, j=L)
                nc.vector.tensor_tensor(ek[:, :, :, 0], middle(pf, L), inc(pf)[:, :, :, 0], ALU.subtract)
                nc.vector.tensor_tensor(ek[:, :, :, 1], exc(pb)[:, :, :, 1], middle(pb, L), ALU.subtract)
                nc.vector.tensor_tensor(eq[:, :, :, 1], inc(pf)[:, :, :, 1], middle(pf, L), ALU.subtract)
                nc.vector.tensor_tensor(eq[:, :, :, 0], middle(pb, L), exc(pb)[:, :, :, 0],
                                        ALU.subtract).then_inc(exps, 1)

            def factors(n):
                L = LEVELS[n]
                dve.wait_ge(exp_done, n + 1)
                ek, eq = (kq[:, n % 2, w].rearrange("p (n t) -> p n t", t=P) for w in range(2))
                ekh = halves(ek, L)
                nc.vector.tensor_tensor(ekh[:, :, :, 0], ekh[:, :, :, 0], halves(kf, L)[:, :, :, 0], ALU.mult)
                nc.vector.tensor_tensor(ekh[:, :, :, 1], ekh[:, :, :, 1], halves(kb, L)[:, :, :, 1], ALU.mult)
                nc.vector.tensor_tensor(eq, eq, q, ALU.mult).then_inc(pair_ready, 1)

            def take(n):
                dve.wait_ge(a_ready, n + 1)
                if n >= 1:
                    dve.wait_ge(a_out, n)
                for b in range(4):
                    src = K.ps[:, 4 * (n % 2) + b].rearrange("p (h c t) -> p h c t", h=2, c=CH)
                    mask = H.masks[:, n].unsqueeze(1).broadcast_to([P, CH, P])
                    for h in range(2):
                        ins = nc.vector.copy_predicated(H.at[:, 2 * b + h, 0:4:3], mask, src[:, h])
                ins.then_inc(a_out, 1)

            exponents(0)
            for n in range(NL):
                if n + 1 < NL:
                    exponents(n + 1)
                factors(n)
                if n >= 1:
                    take(n - 1)
            dve.wait_ge(a_ready, NL - 1)
            nc.vector.tensor_tensor(kq[:, NL % 2, 0].rearrange("p (n t) -> p n t", t=P), kf, kb,
                                    ALU.add).then_inc(pair_ready, 1)
            take(NL - 1)
            e = kq[:, (NL + 1) % 2].rearrange("p w (h c t) -> p w h c t", h=HG, c=CH)
            pre = H.pre.rearrange("p d (h c) t -> p d h c t", c=CH)
            end_f = pre[:, 0, :, 0, P:].broadcast_to([P, HG, P])
            end_b = pre[:, 1, :, 0, P:].broadcast_to([P, HG, P])
            nc.vector.tensor_tensor(e[:, 0, :, 0], end_f, pre[:, 0, :, 0, 1:], ALU.subtract)
            nc.vector.tensor_copy(e[:, 0, :, 1], pre[:, 1, :, 1, 0:P])
            nc.vector.tensor_copy(e[:, 1, :, 1], pre[:, 0, :, 1, 1:])
            nc.vector.tensor_tensor(e[:, 1, :, 0], end_b, pre[:, 1, :, 0, 0:P], ALU.subtract).then_inc(exps, 1)
            take(NL)
            dve.wait_ge(exp_done, NL + 1)
            nc.vector.tensor_tensor(e[:, 0, :, 0], e[:, 0, :, 0], kk[:, 0, :, 0], ALU.mult)
            nc.vector.tensor_tensor(e[:, 0, :, 1], e[:, 0, :, 1], kk[:, 1, :, 1], ALU.mult)
            nc.vector.tensor_tensor(e[:, 1], e[:, 1], H.q, ALU.mult).then_inc(pair_ready, 1)
            dve.wait_ge(a_ready, NL + 2)
            b0 = 4 * ((NL + 1) % 2)
            src = K.ps[:, b0:b0 + 4].rearrange("p b (h c t) -> p (b h) c t", h=2, c=CH)
            for h in range(HG):
                ins = nc.vector.tensor_copy(H.at[:, h, 1:3], src[:, h])
            link(ins)

        @block.scalar
        def _(act):
            for n in range(NL + 1):
                act.wait_ge(exps, n + 1)
                b = n % 2 if n < NL else (NL + 1) % 2
                flat = kq[:, b].rearrange("p w n -> p (w n)")
                nc.scalar.activation(flat, flat, ACT.Exp).then_inc(exp_done, 1)

        @block.tensor
        def _(pe):
            for n in range(NL + 2):
                pe.wait_ge(pair_ready, n + 1)
                if n >= 2:
                    pe.wait_ge(a_out, n - 1)
                b = n % 2
                keys = kq[:, b, 0].rearrange("p (h c t) -> p h c t", h=HG, c=CH)
                queries = (kq[:, b, 1].rearrange("p (h c t) -> p h c t", h=HG, c=CH) if n != NL else H.q)
                for h in range(HG):
                    for c in range(CH):
                        cq = c if n <= NL else 1 - c
                        o = K.ps[:, 4 * (n % 2) + h // 2, ((h % 2) * 2 + c) * P:((h % 2) * 2 + c + 1) * P]
                        last = nc.tensor.matmul(o, keys[:, h, c], queries[:, h, cq], start=True, stop=True)
                last.then_inc(a_ready, 1)


def stage_hg_out(K, S, H):
    nc, i = K.nc, K.i
    with S.open() as (block, sem):
        area = Area(K.arena, H.end)
        o = area.take(TT, D)
        sq = area.take(TT, D)
        gain = area.take(D)
        st = area.take(3, TT, HG)
        chain, w_loaded, g_loaded, silu_ready = sem("chain"), sem("w_loaded"), sem("g_loaded"), sem("silu")
        o_ready, sq_ready, v_ready, sd_ready = sem("o_ready"), sem("sq"), sem("veps"), sem("sd")
        oc_ready, y_ready, yt_ready, yt_out, p_ready = (sem("oc"), sem("y"), sem("yt"), sem("yt_out"),
                                                        sem("p_ready"))
        w = K.big.rearrange("p (k n) -> p k n", k=KD)

        @block.sync
        def _(sp):
            sp.dma_start(gain, i["hg_norm_g_2"].broadcast_to([P, D])).then_inc(g_loaded, 16)
            sp.dma_start(w, i["hg_w_out_2"][0].rearrange("(k p) n -> p k n", p=P)).then_inc(w_loaded, 16)

        @block.tensor
        def _(pe):
            for t in range(TT):
                for h in range(HG):
                    for s in range(TT):
                        last = nc.tensor.matmul(K.ps[:, 2 * t + h // 4, (h % 4) * P:(h % 4 + 1) * P],
                                                H.at[:, h, 2 * s + t], H.v[:, s, h * P:(h + 1) * P],
                                                start=(s == 0), stop=(s == 1))
                last.then_inc(o_ready, 1)
            for t in range(TT):
                pe.wait_ge(y_ready, t + 1)
                for k in range(KD):
                    last = nc.tensor.transpose(K.ps_low[:, k, t * P:(t + 1) * P],
                                               o[:, t, k * P:(k + 1) * P], K.ident[:])
            last.then_inc(yt_ready, 1)
            pe.wait_ge(w_loaded, 16)
            pe.wait_ge(yt_out, 1)
            product_out(K, pe, w, p_ready)

        @block.scalar
        def _(act):
            nc.scalar.activation(H.g, H.g, ACT.Silu).then_inc(silu_ready, 1)
            for t in range(TT):
                act.wait_ge(oc_ready, t + 1)
                nc.scalar.activation(sq[:, t], o[:, t], ACT.Square).then_inc(sq_ready, 1)
            act.wait_ge(v_ready, 1)
            nc.scalar.activation(st[:, 2], st[:, 1], ACT.Sqrt).then_inc(sd_ready, 1)

        @block.vector
        def _(dve):
            link = Link(dve, chain)
            for t in range(TT):
                dve.wait_ge(o_ready, t + 1)
                nc.vector.tensor_copy(o[:, t], K.ps[:, 2 * t:2 * t + 2].rearrange("p b n -> p (b n)")
                                      ).then_inc(oc_ready, 1)
            for t in range(TT):
                dve.wait_ge(sq_ready, t + 1)
                link(nc.vector.tensor_reduce(st[:, 0, t], sq[:, t].rearrange("p (h d) -> p h d", h=HG), AX.X,
                                             ALU.add))
            nc.vector.tensor_scalar(st[:, 1], st[:, 0], 1.0 / HD, EPS, ALU.mult, ALU.add).then_inc(v_ready, 1)
            dve.wait_ge(silu_ready, 1)
            dve.wait_ge(g_loaded, 16)
            for t in range(TT):
                link(nc.vector.tensor_tensor(H.g[:, t], H.g[:, t], gain, ALU.mult))
            dve.wait_ge(sd_ready, 1)
            link(nc.vector.reciprocal(st[:, 0], st[:, 2]))
            for t in range(TT):
                link(nc.vector.tensor_tensor(
                    o[:, t].rearrange("p (h d) -> p h d", h=HG), o[:, t].rearrange("p (h d) -> p h d", h=HG),
                    st[:, 0, t].unsqueeze(2).broadcast_to([P, HG, HD]), ALU.mult))
                nc.vector.tensor_tensor(o[:, t], o[:, t], H.g[:, t], ALU.mult).then_inc(y_ready, 1)
            dve.wait_ge(yt_ready, 1)
            nc.vector.tensor_copy(K.h_t[:].rearrange("p k t -> p (k t)"),
                                  K.ps_low.rearrange("p k t -> p (k t)")).then_inc(yt_out, 1)
            residual_out(K, dve, link, K.gate[:, 0], p_ready, sq[:, 0])


def hg_mixer(K, S):
    H = hg_memory(K)
    src = K.i["hg_w_in_2"][0]
    blocks = []
    for half in range(2):
        hs = slice(4 * half, 4 * half + 4)
        blocks.append(("cols", half * 512, H.q[:, hs].rearrange("p h c t -> p h (c t)")))
        for d in range(2):
            blocks.append(("cols", (1 + d) * D + half * 512, H.k[:, d, hs].rearrange("p h c t -> p h (c t)")))
        blocks.append(("rows", 3 * D + half * 512, H.v[:, :, half * 512:(half + 1) * 512]))
        blocks.append(("rows", 4 * D + half * 512, H.g[:, :, half * 512:(half + 1) * 512]))
    stage_projection(K, S, K.gain[:, 0], K.shift[:, 0], src, blocks, H.end)
    stage_hg_gates(K, S, H)
    stage_hg_attention(K, S, H)
    stage_hg_out(K, S, H)



def stage_lru(K, S, xb, yb, at):
    nc, i = K.nc, K.i
    with S.open() as (block, sem):
        area = Area(K.arena, at)
        padded = area.take(KD, SEQ + TAPS - 1)
        xc, r, th, ig, bb, aa = (area.take(KD, SEQ) for _ in range(6))
        hs = [area.take(KD, SEQ), bb]
        w = K.big.rearrange("p (k n) -> p k n", k=KD)
        cw = area.take(TAPS, KD)
        cb = area.take(KD)
        bias = area.take(4, KD)
        lam, ex, u, u2, poly = (area.take(2, KD) for _ in range(5))
        tmp = r.rearrange("p k t -> p (k t)")[:, 0:D]
        chain, loaded, wg_loaded, w_loaded = sem("chain"), sem("loaded"), sem("wg_loaded"), sem("w_loaded")
        z_ready, e_ready, xc_ready, g_ready = sem("z"), sem("e"), sem("xc"), sem("g")
        sig_done, nsp_ready, at_done = sem("sig"), sem("nsp"), sem("at")
        m_ready, sq_done, gelu_done, y_ready, o_ready = (sem("m"), sem("sq"), sem("gelu"), sem("y"),
                                                         sem("o"))
        th_used = sem("th_used")
        wg = [a.rearrange("p (n j) -> p n j", n=16) for a in (K.ring[:], K.arena[:, 28672:32768])]
        assert area.at <= 24576

        @block.sync
        def _(sp):
            for n, gate_w in enumerate((i["lru_w_a_2"], i["lru_w_x_2"])):
                src = gate_w[0].rearrange("d b (k p) j -> p (d b k) j", p=P)
                sp.dma_start(wg[n], src).then_inc(wg_loaded, 16)
            w_out = i["lru_w_out_2"][0].rearrange("(k p) n -> p k n", p=P)
            sp.dma_start(w[:, 0:4], w_out[:, 0:4]).then_inc(w_loaded, 16)
            sp.wait_ge(g_ready, 4)
            sp.dma_start(w[:, 4:8], w_out[:, 4:8]).then_inc(w_loaded, 16)

        @block.scalar
        def _(act):
            for j in range(TAPS):
                load_cols(act.dma_start, cw[:, j], i["lru_conv_w_2"][0, j:j + 1], KD).then_inc(loaded, 16)
            load_cols(act.dma_start, cb, i["lru_conv_b_2"], KD).then_inc(loaded, 16)
            for d in range(2):
                load_cols(act.dma_start, bias[:, 2 * d], i["lru_b_a_2"][0, d:d + 1], KD).then_inc(loaded, 16)
                load_cols(act.dma_start, bias[:, 2 * d + 1], i["lru_b_x_2"][0, d:d + 1], KD).then_inc(loaded, 16)
                load_cols(act.dma_start, lam[:, d], i["lru_lam_2"][0, d:d + 1], KD).then_inc(loaded, 16)
            act.wait_ge(z_ready, 1)
            nc.scalar.activation(ex, u, ACT.Exp).then_inc(e_ready, 1)
            for d in range(2):
                for which, dst in enumerate((r, ig)):
                    act.wait_ge(g_ready, 2 * d + which + 1)
                    if d == 1 and which == 0:
                        act.wait_ge(at_done, 1)
                    if d == 1 and which == 1:
                        act.wait_ge(th_used, 1)
                    for c in range(KD):
                        src = K.ps[:, 4 * which + c // 2, (c % 2) * SEQ:(c % 2 + 1) * SEQ]
                        ins = nc.scalar.activation(dst[:, c], src, ACT.Sigmoid,
                                                   bias=bias[:, 2 * d + which, c:c + 1])
                ins.then_inc(sig_done, 1)
                act.wait_ge(sig_done, d + 1)
                act.wait_ge(nsp_ready, 1)
                if d == 1:
                    act.wait_ge(th_used, 1)
                for c in range(KD):
                    nc.scalar.activation(th[:, c], r[:, c], ACT.Tanh, scale=lam[:, d, c:c + 1])
                    ins = nc.scalar.activation(aa[:, c], r[:, c], ACT.Exp, scale=lam[:, d, c:c + 1])
                ins.then_inc(at_done, 1)
                act.wait_ge(m_ready, d + 1)
                nc.scalar.activation(th, th, ACT.Sqrt).then_inc(sq_done, 1)
            nc.scalar.activation(yb, yb, ACT.Gelu_apprx_tanh).then_inc(gelu_done, 1)

        @block.tensor
        def _(pe):
            pe.wait_ge(wg_loaded, 32)
            pe.wait_ge(xc_ready, 1)
            for d in range(2):
                for which in range(2):
                    if d == 1:
                        pe.wait_ge(sig_done, 1)
                    for c in range(KD):
                        for kk in range(2):
                            n = (d * LRU_BLOCKS + c // 2) * 2 + kk
                            last = nc.tensor.matmul(
                                K.ps[:, 4 * which + c // 2, (c % 2) * SEQ:(c % 2 + 1) * SEQ],
                                wg[which][:, n, (c % 2) * P:(c % 2 + 1) * P], xc[:, (c // 2) * 2 + kk],
                                start=(kk == 0), stop=(kk == 1))
                    last.then_inc(g_ready, 1)
            pe.wait_ge(w_loaded, 32)
            pe.wait_ge(y_ready, 1)
            product_out(K, pe, w, o_ready)

        @block.vector
        def _(dve):
            link = Link(dve, chain)
            nc.vector.memset(padded, 0.0)
            dve.wait_ge(loaded, 16 * (TAPS + 1 + 6))
            link(nc.vector.scalar_tensor_tensor(u, lam, -1.0, lam, ALU.mult, ALU.min))
            dve.sem_inc(z_ready, 1)
            link(nc.vector.tensor_copy(padded[:, :, LEFT:LEFT + SEQ], xb))
            for c in range(KD):
                for j in range(TAPS):
                    src = padded[:, c, j:j + SEQ]
                    if j == 0:
                        ins = nc.vector.tensor_scalar(xc[:, c], src, cw[:, 0, c:c + 1], cb[:, c:c + 1],
                                                      ALU.mult, ALU.add)
                    else:
                        ins = nc.vector.scalar_tensor_tensor(xc[:, c], src, cw[:, j, c:c + 1], xc[:, c],
                                                             ALU.mult, ALU.add)
                    link(ins)
            dve.sem_inc(xc_ready, 1)
            dve.wait_ge(e_ready, 1)
            link(nc.vector.tensor_scalar(u2, ex, 2.0, None, ALU.add))
            link(nc.vector.reciprocal(u, u2))
            link(nc.vector.tensor_tensor(u, u, ex, ALU.mult))
            link(nc.vector.tensor_tensor(u2, u, u, ALU.mult))
            link(nc.vector.tensor_scalar(poly, u2, 1.0 / 17, 1.0 / 15, ALU.mult, ALU.add))
            for k in (13, 11, 9, 7, 5, 3, 1):
                link(nc.vector.tensor_tensor(poly, poly, u2, ALU.mult))
                link(nc.vector.tensor_scalar(poly, poly, 1.0 / k, None, ALU.add))
            link(nc.vector.tensor_tensor(poly, poly, u, ALU.mult))
            link(nc.vector.tensor_scalar(ex, lam, -1.0, 0.0, ALU.mult, ALU.max))
            link(nc.vector.scalar_tensor_tensor(lam, poly, 2.0, ex, ALU.mult, ALU.add))
            link(nc.vector.tensor_scalar(lam, lam, -LRU_C, None, ALU.mult))
            dve.sem_inc(nsp_ready, 1)
            for d in range(2):
                dve.wait_ge(at_done, d + 1)
                link(nc.vector.tensor_scalar(bb, th, -1.0, 1.0, ALU.mult, ALU.add))
                link(nc.vector.reciprocal(bb, bb))
                link(nc.vector.scalar_tensor_tensor(th, th, -2.0, bb, ALU.mult, ALU.mult))
                dve.sem_inc(m_ready, 1)
                link(nc.vector.tensor_tensor(bb, ig, xc, ALU.mult))
                dve.wait_ge(sq_done, d + 1)
                link(nc.vector.tensor_tensor(bb, bb, th, ALU.mult))
                for c in range(KD):
                    if d == 0:
                        ins = nc.vector.tensor_tensor_scan(hs[d][:, c], aa[:, c], bb[:, c], 0.0, ALU.mult,
                                                           ALU.add)
                    else:
                        ins = nc.vector.tensor_tensor_scan(hs[d][:, c][:, ::-1], aa[:, c][:, ::-1],
                                                           bb[:, c][:, ::-1], 0.0, ALU.mult, ALU.add)
                link(ins)
                dve.sem_inc(th_used, 1)
            link(nc.vector.tensor_tensor(hs[0], hs[0], hs[1], ALU.add))
            dve.wait_ge(gelu_done, 1)
            nc.vector.tensor_tensor(K.h_t[:], hs[0], yb, ALU.mult).then_inc(y_ready, 1)
            residual_out(K, dve, link, K.gate[:, 0], o_ready, tmp)


def lru_mixer(K, S):
    area = Area(K.arena)
    xb = area.take(KD, SEQ)
    yb = area.take(KD, SEQ)
    blocks = [("cols", n * 512, (xb, yb)[n // 2][:, 4 * (n % 2):4 * (n % 2) + 4]) for n in range(4)]
    stage_projection(K, S, K.gain[:, 0], K.shift[:, 0], K.i["lru_w_in_2"][0], blocks, area.at)
    stage_lru(K, S, xb, yb, area.at)



def stage_scores(K, S, l, q, s, keys, keys_t):
    nc = K.nc
    with S.open() as (block, sem):
        loaded, kt_ready, kt_out, s_ready, s_out = (sem("loaded"), sem("kt_ready"), sem("kt_out"),
                                                    sem("s_ready"), sem("s_out"))

        @block.sync
        def _(sp):
            sp.dma_start(keys, K.i["peer_keys_2"][l].rearrange("h w k d -> k (h w) d")).then_inc(loaded, 16)

        @block.tensor
        def _(pe):
            pe.wait_ge(loaded, 16)
            for n in range(HP):
                last = nc.tensor.transpose(K.ps[:, n // 4, (n % 4) * P:(n % 4 + 1) * P], keys[:, n], K.ident[:])
            last.then_inc(kt_ready, 1)
            pe.wait_ge(kt_out, 1)
            for t in range(TT):
                for n in range(HP):
                    last = nc.tensor.matmul(K.ps[:, 4 * (1 - t) + n // 4, (n % 4) * P:(n % 4 + 1) * P],
                                            q[:, n, t * P:(t + 1) * P], keys_t[:, n], start=True, stop=True)
                last.then_inc(s_ready, 1)

        @block.vector
        def _(dve):
            dve.wait_ge(kt_ready, 1)
            nc.vector.tensor_copy(keys_t.rearrange("p n k -> p (n k)"),
                                  K.ps[:, 0:4].rearrange("p b n -> p (b n)")).then_inc(kt_out, 1)
            for t in range(TT):
                dve.wait_ge(s_ready, t + 1)
                b0 = 4 * (1 - t)
                nc.vector.tensor_copy(s[:, t].rearrange("p n k -> p (n k)"),
                                      K.ps[:, b0:b0 + 4].rearrange("p b n -> p (b n)")).then_inc(s_out, 1)
            dve.wait_ge(s_out, 2)


def pipeline(engine, first, last, unroll, body, straight=True):
    start = first // unroll
    if straight:
        for u in range(unroll):
            body(first + u, u, True)
        start += 1
    with engine.Fori(start, last // unroll) as i:
        for u in range(unroll):
            body(i * unroll + u, u, False)


SLOTS = 4
HALF_J = NKEYS // 2
TG = 4
GROUPS = SEQ // TG
SCRATCH = HALF_J * SEQ
EXP_AT = 52

assert GROUPS == HALF_J


class Gates:

    def __init__(self, K, sem, half, bank):
        self.K, self.half, self.bank = K, half, bank
        flat = K.h_t[:].rearrange("p k t -> p (k t)")
        self.left = flat[:, 0:2 * TG * P].rearrange("p (b t i) -> p b t i", b=2, t=TG)
        at = 2 * TG * P
        self.right = flat[:, at:at + TG * P].rearrange("p (b t j) -> p b t j", b=2, t=TG)
        at += TG * P
        self.ramp = flat[:, at:at + P]
        self.number = flat[:, at + P:at + P + 2 * TG].rearrange("p (b t) -> p b t", b=2)
        self.act = K.arena[:, half * SCRATCH:(half + 1) * SCRATCH].rearrange("p (j t) -> p t j", t=SEQ)
        self.fetched, self.seen = sem("numbers_fetched"), sem("numbers_seen")
        self.left_ready, self.right_ready = sem("left_ready"), sem("right_ready")
        self.w_ready, self.w_out = sem("weights_ready"), sem("weights_out")

    def pool(self, pool, g, b, early):
        nc, K = self.K.nc, self.K
        if not early:
            pool.wait_ge(self.w_ready, g - 1)
        nc.gpsimd.tensor_copy(self.number[:, b], K.sel[:, 0, bass.ds(g * TG, TG)]).then_inc(self.fetched, 1)
        pool.wait_ge(self.fetched, g + 1)
        pool.sem_inc(self.seen, 1)
        for t in range(TG):
            ins = nc.gpsimd.tensor_scalar(self.left[:, b, t], self.ramp, self.number[:, b, t:t + 1], None,
                                          ALU.is_equal)
        ins.then_inc(self.left_ready, 1)

    def pe(self, pe, g, b, early):
        pe.wait_ge(self.left_ready, g + 1)
        pe.wait_ge(self.right_ready, g + 1)
        if not early or g >= 2:
            pe.wait_ge(self.w_out, g - 1)
        for t in range(TG):
            last = self.K.nc.tensor.matmul(self.K.ps[:, self.bank + b, t * HALF_J:(t + 1) * HALF_J],
                                           self.left[:, b, t], self.right[:, b, t], start=True, stop=True)
        last.then_inc(self.w_ready, 1)

    def build(self, dve, g, b, early):
        nc, K = self.K.nc, self.K
        if not early or g >= 2:
            dve.wait_ge(self.w_ready, g - 1)
        ramp = self.ramp[:, self.half * HALF_J:(self.half + 1) * HALF_J]
        for t in range(TG):
            ins = nc.vector.tensor_scalar(self.right[:, b, t], ramp, K.sel[:, 1, bass.ds(g * TG + t, 1)],
                                          K.sel[:, 2, bass.ds(g * TG + t, 1)], ALU.is_equal, ALU.mult)
        ins.then_inc(self.right_ready, 1)

    def weigh(self, dve, g, b):
        dve.wait_ge(self.w_ready, g + 1)
        piece = self.act[:, bass.ds(g * TG, TG)]
        weights = self.K.ps[:, self.bank + b, 0:TG * HALF_J].rearrange("p (t j) -> p t j", t=TG)
        self.K.nc.vector.tensor_tensor(piece, piece, weights, ALU.mult).then_inc(self.w_out, 1)


def slot_loads(n, s):
    return (n - s) * (16 // SLOTS) + 16


def stage_expert_inputs(K, S, l, s):
    nc = K.nc
    G = TT * PH
    table = K.i["peer_u_2"][l].rearrange("(i j) d -> j i d", j=NKEYS)
    with S.open() as (block, sem):
        area = Area(K.arena, SCRATCH + TT * HP * NKEYS)
        val = area.take(TT * HP, TOPK)
        idx = area.take(TT * HP, TOPK).bitcast(U32)
        idf = area.take(TT * HP, TOPK)
        cand = area.take(G, TOPK, TOPK)
        top = area.take(G, TOPK)
        pos = area.take(G, TOPK).bitcast(U32)
        part = area.take(G, TOPK).bitcast(U32)
        partf = area.take(G, TOPK)
        picked = area.take(2, G, TOPK)
        gates = area.take(G, TOPK)
        sums = area.take(G)
        onehot = area.take(G, TOPK, TOPK)
        ramp16 = area.take(TOPK)
        assert area.at <= 32768
        sf = s.rearrange("p t n k -> p (t n) k")

        u = K.ring[:].rearrange("p (s k d) -> p s k d", s=SLOTS, k=KD)
        u_t = K.split[:, 0:4 * D].rearrange("p (b w k e) -> p b w k e", b=2, w=2, k=KD)
        h = K.split[:, 4 * D:].rearrange("p (w k t) -> p w k t", w=2, k=KD)
        u_loaded = [sem(f"u_loaded{n}") for n in range(SLOTS)]
        chain, h_high, h_ready = sem("chain"), sem("h_high"), sem("h_ready")
        ut_high, ut_low = sem("ut_high"), sem("ut_low")
        a_ready, gelu_done, ut_ready = sem("a_ready"), sem("gelu_done"), sem("ut_ready")
        ramp_ready, gl_ready, e_ready = sem("ramp_ready"), sem("gl_ready"), sem("e_ready")
        sel_ready, sel_t_ready, sel_out = sem("sel_ready"), sem("sel_t_ready"), sem("sel_out")
        weights = Gates(K, sem, 0, 6)

        @block.sync
        def _(sp):
            def load(n, s, early):
                if not early:
                    sp.wait_ge(ut_ready, 2 * n - 2 * (SLOTS - 1))
                sp.dma_start(u[:, s].rearrange("p k d -> p (k d)"),
                             table[bass.ds(n, 1)].rearrange("a i d -> i (a d)")).then_inc(u_loaded[s], 16)

            pipeline(sp, 0, NKEYS, SLOTS, load)

        @block.gpsimd
        def _(pool):
            nc.gpsimd.iota(ramp16, pattern=[[1, TOPK]], base=0, channel_multiplier=0,
                           allow_small_or_imprecise_dtypes=True).then_inc(ramp_ready, 1)
            pool.wait_ge(h_ready, 1)
            nc.gpsimd.iota(weights.ramp, pattern=[[1, P]], base=0, channel_multiplier=0,
                           allow_small_or_imprecise_dtypes=True).then_inc(ramp_ready, 1)
            pool.wait_ge(ramp_ready, 2)
            pool.wait_ge(sel_out, 1)
            pipeline(pool, 0, GROUPS, 2, lambda g, b, early: weights.pool(pool, g, b, early))

        @block.tensor
        def _(pe):
            def products(n, b, early):
                pe.wait_ge(ut_high, 2 * n + 2)
                pe.wait_ge(ut_low, 2 * n + 2)
                if not early:
                    pe.wait_ge(gelu_done, n - 1)
                for k in range(KD):
                    for w, wh in ((0, 0), (0, 1), (1, 0)):
                        last = nc.tensor.matmul(K.ps[:, 4 + b, 0:SEQ], u_t[:, b, w, k], h[:, wh, k],
                                                start=(k == 0 and w == wh), stop=(k == KD - 1 and w == 1))
                last.then_inc(a_ready, 1)

            def chunk(n, s, early):
                b = s % 2
                pe.wait_ge(u_loaded[s], slot_loads(n, s))
                if not early or n >= 2:
                    pe.wait_ge(ut_high, 2 * n - 2)
                    pe.wait_ge(ut_low, 2 * n - 2)
                for k in range(KD):
                    last = nc.tensor.transpose(K.ps[:, 2 * b + k // 4, (k % 4) * P:(k % 4 + 1) * P],
                                               u[:, s, k], K.ident[:])
                    if k % 4 == 3:
                        last.then_inc(ut_ready, 1)
                if not early or n >= 1:
                    products(n - 1, 1 - b, early and n < 3)

            def chunk_and_gates(n, s, early):
                chunk(n, s, False)
                weights.pe(pe, n - HALF_J, s % 2, early)

            pe.wait_ge(h_ready, 1)
            pipeline(pe, 0, HALF_J, SLOTS, chunk)
            pe.wait_ge(sel_ready, 1)
            for n, src in enumerate((picked[:, 0], picked[:, 1], gates)):
                src = src.rearrange("p (t h) k -> p t (h k)", t=TT)
                for t in range(TT):
                    last = nc.tensor.transpose(K.ps[:, 6 + n // 2, (n % 2) * SEQ + t * P:(n % 2) * SEQ + (t + 1) * P],
                                               src[:, t], K.ident[:])
            last.then_inc(sel_t_ready, 1)
            pe.wait_ge(sel_out, 1)
            pipeline(pe, HALF_J, NKEYS, SLOTS, chunk_and_gates)
            products(NKEYS - 1, (NKEYS - 1) % 2, False)

        @block.scalar
        def _(act):
            def high(n, s, early):
                b = s % 2
                if not early or n >= 2:
                    act.wait_ge(a_ready, n - 1)
                for half in range(2):
                    act.wait_ge(ut_ready, 2 * n + half + 1)
                    nc.scalar.copy(u_t[:, b, 0, 4 * half:4 * half + 4].rearrange("p k e -> p (k e)"),
                                   K.ps[:, 2 * b + half]).then_inc(ut_high, 1)

            def gelu(n, b):
                act.wait_ge(a_ready, n + 1)
                nc.scalar.activation(K.arena[:, bass.ds(n * SEQ, SEQ)], K.ps[:, 4 + b, 0:SEQ],
                                     ACT.Gelu_apprx_tanh).then_inc(gelu_done, 1)

            def chunk(n, s, early):
                high(n, s, early)
                if not early or n >= 1:
                    gelu(n - 1, (s + 1) % 2)

            nc.scalar.copy(h[:, 0], K.h_t[:]).then_inc(h_high, 1)
            pipeline(act, 0, EXP_AT, SLOTS, chunk)
            act.wait_ge(gl_ready, 1)
            nc.scalar.activation(gates, gates, ACT.Exp).then_inc(e_ready, 1)
            pipeline(act, EXP_AT, HALF_J, SLOTS, chunk, straight=False)
            act.wait_ge(sel_t_ready, 1)
            pipeline(act, HALF_J, NKEYS, SLOTS, chunk, straight=False)
            gelu(NKEYS - 1, (NKEYS - 1) % 2)
            act.wait_ge(gelu_done, NKEYS)

        @block.vector
        def _(dve):
            link = Link(dve, chain)

            def low(n, s, early):
                b = s % 2
                if not early or n >= 2:
                    dve.wait_ge(a_ready, n - 1)
                for half in range(2):
                    dve.wait_ge(ut_high, 2 * n + half + 1)
                    pair = [u_t[:, b, w, 4 * half:4 * half + 4].rearrange("p k e -> p (k e)") for w in range(2)]
                    nc.vector.tensor_tensor(pair[1], K.ps[:, 2 * b + half], pair[0].bitcast(F32),
                                            ALU.subtract).then_inc(ut_low, 1)

            chunks = [0]

            def keep_up(count=1):
                for _ in range(count):
                    low(chunks[0], chunks[0] % SLOTS, True)
                    chunks[0] += 1

            def top16(values, out, places, n, per_chunk):
                for half in range(2):
                    cut = slice(8 * half, 8 * half + 8)
                    for g in range(n):
                        ins = nc.vector.max(out[:, g, cut], values[:, g])
                        if g == n - 1:
                            link(ins)
                        elif g % per_chunk == per_chunk - 1:
                            keep_up()
                    for g in range(n):
                        ins = nc.vector.max_index(places[:, g, cut], out[:, g, cut], values[:, g])
                        if g == n - 1:
                            link(ins)
                        elif g % per_chunk == per_chunk - 1:
                            keep_up()
                    if half == 0:
                        for g in range(n):
                            ins = nc.vector.match_replace(values[:, g], out[:, g, cut], values[:, g], -BIG)
                            if g == n - 1:
                                link(ins)
                            elif g % per_chunk == per_chunk - 1:
                                keep_up()

            dve.wait_ge(h_high, 1)
            nc.vector.tensor_tensor(h[:, 1], K.h_t[:], h[:, 0].bitcast(F32), ALU.subtract).then_inc(h_ready, 1)
            top16(sf, val, idx, TT * HP, 8)
            link(nc.vector.tensor_copy(idf, idx))
            v4 = val.rearrange("p (g w) k -> p g w k", w=2)
            for g in range(G):
                ins = nc.vector.tensor_tensor(cand[:, g], v4[:, g, 0].unsqueeze(2).broadcast_to([P, TOPK, TOPK]),
                                              v4[:, g, 1].unsqueeze(1).broadcast_to([P, TOPK, TOPK]), ALU.add)
                if g == G - 1:
                    link(ins)
                elif g % 5 == 4:
                    keep_up()
            keep_up()
            top16(cand.rearrange("p g a b -> p g (a b)"), top, pos, G, 5)
            nc.vector.tensor_tensor(gates, top, top[:, :, 0:1].broadcast_to([P, G, TOPK]),
                                    ALU.subtract).then_inc(gl_ready, 1)
            assert chunks[0] < EXP_AT
            dve.wait_ge(ramp_ready, 1)
            i4 = idf.rearrange("p (g w) k -> p g w k", w=2)
            rampb = ramp16.unsqueeze(1).broadcast_to([P, TOPK, TOPK])
            for w, (op, number) in enumerate(((ALU.logical_shift_right, 4), (ALU.bitwise_and, TOPK - 1))):
                link(nc.vector.tensor_scalar(part, pos, number, None, op))
                link(nc.vector.tensor_copy(partf, part))
                for g in range(G):
                    ins = nc.vector.tensor_tensor(onehot[:, g], partf[:, g].unsqueeze(2).broadcast_to([P, TOPK, TOPK]),
                                                  rampb, ALU.is_equal)
                    if g % 5 == 4:
                        keep_up()
                link(ins)
                for g in range(G):
                    ins = nc.vector.tensor_tensor(onehot[:, g], onehot[:, g],
                                                  i4[:, g, w].unsqueeze(1).broadcast_to([P, TOPK, TOPK]), ALU.mult)
                    if g % 5 == 4:
                        keep_up()
                link(ins)
                for q in range(4):
                    gs = slice(q * G // 4, (q + 1) * G // 4)
                    link(nc.vector.tensor_reduce(picked[:, w, gs].rearrange("p g k -> p (g k)"),
                                                 onehot[:, gs].rearrange("p g k a -> p (g k) a"), AX.X, ALU.add))
                    if q % 2:
                        keep_up()
            assert chunks[0] <= HALF_J
            keep_up(max(0, EXP_AT + 1 - chunks[0]))
            dve.wait_ge(e_ready, 1)
            link(nc.vector.tensor_reduce(sums, gates, AX.X, ALU.add))
            link(nc.vector.reciprocal(sums, sums))
            nc.vector.tensor_tensor(gates, gates, sums.unsqueeze(2).broadcast_to([P, G, TOPK]),
                                    ALU.mult).then_inc(sel_ready, 1)
            keep_up(HALF_J - chunks[0])
            dve.wait_ge(sel_t_ready, 1)
            nc.vector.tensor_copy(K.sel[:, 0:2].rearrange("p n t -> p (n t)"), K.ps[:, 6])
            nc.vector.tensor_copy(K.sel[:, 2], K.ps[:, 7, 0:SEQ]).then_inc(sel_out, 1)
            dve.wait_ge(sel_out, 1)
            dve.wait_ge(ramp_ready, 2)
            dve.wait_ge(gelu_done, HALF_J - 1)

            def chunk(n, s, early):
                low(n, s, False)
                g = n - HALF_J
                weights.build(dve, g, s % 2, early)
                if early and g == 0:
                    dve.wait_ge(gelu_done, HALF_J)
                if not early or g >= 1:
                    weights.weigh(dve, g - 1, 1 - s % 2)

            pipeline(dve, HALF_J, NKEYS, SLOTS, chunk)
            weights.weigh(dve, GROUPS - 1, (GROUPS - 1) % 2)
            dve.wait_ge(weights.w_out, GROUPS)


def stage_expert_outputs(K, S, l):
    nc = K.nc
    table = K.i["peer_v_2"][l].rearrange("(i j) d -> j i d", j=NKEYS)
    with S.open() as (block, sem):
        v_loaded = [sem(f"v_loaded{s}") for s in range(SLOTS)]
        v_high, v_low, g_high, g_low, p_done, chain = (sem("v_high"), sem("v_low"), sem("g_high"),
                                                       sem("g_low"), sem("p_done"), sem("chain"))
        v = K.ring[:].rearrange("p (s d) -> p s d", s=SLOTS)
        vs = K.split[:, 0:4 * D].rearrange("p (b w d) -> p b w d", b=2, w=2)
        g = K.split[:, 4 * D:4 * D + 4 * SEQ].rearrange("p (b w t) -> p b w t", b=2, w=2)
        weights = Gates(K, sem, 1, 0)
        tmp = K.ring[:, 0:D]

        @block.sync
        def _(sp):
            def load(n, s, early):
                if not early:
                    sp.wait_ge(v_low, n - (SLOTS - 1))
                sp.dma_start(v[:, s], table[bass.ds(n, 1)].rearrange("a i d -> i (a d)")
                             ).then_inc(v_loaded[s], 16)

            pipeline(sp, 0, NKEYS, SLOTS, load)

        @block.gpsimd
        def _(pool):
            pipeline(pool, 0, GROUPS, 2, lambda g, b, early: weights.pool(pool, g, b, early))

        @block.scalar
        def _(act):
            def chunk(n, s, early):
                b = s % 2
                if not early or n >= 2:
                    act.wait_ge(p_done, n - 1)
                nc.scalar.copy(g[:, b, 0], K.arena[:, bass.ds(n * SEQ, SEQ)]).then_inc(g_high, 1)
                act.wait_ge(v_loaded[s], slot_loads(n, s))
                nc.scalar.copy(vs[:, b, 0], v[:, s]).then_inc(v_high, 1)

            pipeline(act, 0, HALF_J, SLOTS, chunk)
            act.wait_ge(weights.w_out, GROUPS)
            pipeline(act, HALF_J, NKEYS, SLOTS, chunk, straight=False)

        @block.vector
        def _(dve):
            link = Link(dve, chain)

            def low(n, s, early):
                b = s % 2
                dve.wait_ge(g_high, n + 1)
                nc.vector.tensor_tensor(g[:, b, 1], K.arena[:, bass.ds(n * SEQ, SEQ)], g[:, b, 0].bitcast(F32),
                                        ALU.subtract).then_inc(g_low, 1)
                dve.wait_ge(v_high, n + 1)
                nc.vector.tensor_tensor(vs[:, b, 1], v[:, s], vs[:, b, 0].bitcast(F32),
                                        ALU.subtract).then_inc(v_low, 1)

            def chunk(n, s, early):
                low(n, s, early)
                weights.build(dve, n, s % 2, early)
                if not early or n >= 1:
                    weights.weigh(dve, n - 1, 1 - s % 2)

            pipeline(dve, 0, HALF_J, SLOTS, chunk)
            weights.weigh(dve, GROUPS - 1, (GROUPS - 1) % 2)
            dve.wait_ge(weights.w_out, GROUPS)
            pipeline(dve, HALF_J, NKEYS, SLOTS, low, straight=False)
            dve.wait_ge(p_done, NKEYS)
            dve.wait_ge(v_low, NKEYS)
            for t in range(TT):
                link(nc.vector.tensor_tensor(tmp, K.ps[:, 4 + 2 * t:6 + 2 * t].rearrange("p b n -> p (b n)"),
                                             K.gate[:, 1], ALU.mult))
                link(nc.vector.tensor_tensor(K.x[:, t], K.x[:, t], tmp, ALU.add))

        @block.tensor
        def _(pe):
            def products(n, s, start, stop):
                b = s % 2
                pe.wait_ge(g_low, n + 1)
                pe.wait_ge(v_low, n + 1)
                for t in range(TT):
                    for w, wv in ((0, 0), (0, 1), (1, 0)):
                        for half in range(2):
                            last = nc.tensor.matmul(K.ps[:, 4 + 2 * t + half], g[:, b, w, t * P:(t + 1) * P],
                                                    vs[:, b, wv, half * 512:(half + 1) * 512],
                                                    start=(start and w == wv), stop=(stop and w == 1))
                last.then_inc(p_done, 1)

            def chunk_and_gates(n, s, early):
                products(n, s, early and s == 0, False)
                weights.pe(pe, n, s % 2, early)

            pipeline(pe, 0, HALF_J, SLOTS, chunk_and_gates)
            pipeline(pe, HALF_J, NKEYS - SLOTS, SLOTS, lambda n, s, early: products(n, s, False, False),
                     straight=False)
            for s in range(SLOTS):
                products(NKEYS - SLOTS + s, s, False, s == SLOTS - 1)


def retrieval(K, S, l):
    area = Area(K.arena)
    q = area.take(HP, SEQ)
    keys = area.take(HP, P)
    keys_t = area.take(HP, P)
    s = Area(K.arena, SCRATCH).take(TT, HP, NKEYS)
    blocks = [("cols", n * 512, q[:, 4 * n:4 * n + 4]) for n in range(4)]
    stage_projection(K, S, K.gain[:, 1], K.shift[:, 1], K.i["peer_w_q_2"][l], blocks, area.at)
    stage_scores(K, S, l, q, s, keys, keys_t)
    stage_expert_inputs(K, S, l, s)
    stage_expert_outputs(K, S, l)


def stage_final(K, S):
    nc = K.nc
    with S.open() as (block, sem):
        area = Area(K.arena)
        gain = area.take(D)
        sq = area.take(D)
        st = area.take(3, TT)
        chain, loaded, ms, var, sd, y, stored = (sem("chain"), sem("loaded"), sem("ms"), sem("var"), sem("sd"),
                                                 sem("y"), sem("stored"))

        @block.sync
        def _(sp):
            sp.dma_start(gain, K.i["final_g_2"].rearrange("(a d) -> a d", a=1).broadcast_to([P, D])
                         ).then_inc(loaded, 16)
            for t in range(TT):
                sp.wait_ge(y, t + 1)
                sp.dma_start(K.out[0, t * P:(t + 1) * P], K.x[:, t]).then_inc(stored, 16)
            sp.wait_ge(stored, 16 * TT)

        @block.scalar
        def _(act):
            for t in range(TT):
                nc.scalar.activation(sq, K.x[:, t], ACT.Square, accum_out=st[:, 0, t:t + 1]).then_inc(ms, 1)
                act.wait_ge(ms, t + 1)
            act.wait_ge(var, 1)
            nc.scalar.activation(st[:, 2], st[:, 1], ACT.Sqrt).then_inc(sd, 1)

        @block.vector
        def _(dve):
            link = Link(dve, chain)
            dve.wait_ge(ms, TT)
            nc.vector.tensor_scalar(st[:, 1], st[:, 0], 1.0 / D, EPS, ALU.mult, ALU.add).then_inc(var, 1)
            dve.wait_ge(sd, 1)
            link(nc.vector.reciprocal(st[:, 0], st[:, 2]))
            dve.wait_ge(loaded, 16)
            for t in range(TT):
                nc.vector.scalar_tensor_tensor(K.x[:, t], K.x[:, t], st[:, 0, t:t + 1], gain, ALU.mult,
                                               ALU.mult).then_inc(y, 1)


def second_block(K, S):
    for l in range(DEPTH):
        stage_modulation(K, S, l)
        if l % 2 == 0:
            hg_mixer(K, S)
        else:
            lru_mixer(K, S)
        retrieval(K, S, l)
    stage_final(K, S)


def memory(nc, K):
    def sb(name, dims, dt=F32):
        return nc.alloc_sbuf_tensor(name, [P, *dims], dt)

    K.x = sb("x_rows", [TT, D])
    K.h_t = sb("h_cols", [KD, SEQ])
    K.ident = sb("identity", [P])
    K.ones = sb("ones", [P])
    K.causal = sb("causal", [P])
    K.pos = sb("position", [TT])
    K.invf = sb("inverse_frequency", [HALF])
    K.cos = sb("cosine", [TT, HALF])
    K.sin = sb("sine", [TT, HALF])
    K.g_norm = sb("norm_gain", [KD])
    K.gain = sb("mixer_gains", [2, KD])
    K.shift = sb("mixer_shifts", [2, KD])
    K.gate = sb("residual_gates", [2, D])
    K.sel = sb("chosen_experts", [3, SEQ])
    K.arena = sb("arena", [32768])
    K.ring = sb("weights_ring", [4096])
    K.split = sb("split_operands", [8192], mybir.dt.float32r)
    K.big = K.arena[:, 24576:32768]
    K.wslot = [w.rearrange("p (k n) -> p k n", k=KD) for w in (K.ring[:], K.arena[:, 28672:32768])]
    K.ps = nc.alloc_psum_tensor("psum", [P, 8, 512], F32)
    K.ps_low = K.ps[:, 0:4].rearrange("p b (c t) -> p (b c) t", c=2)
    K.ps_pair = [K.ps[:, 4:6], K.ps[:, 6:8]]

    area = Area(K.arena)
    K.glu = area.take(4, SEQ)
    K.low = area.take((Q_LORA + KV_LORA) // P, SEQ)
    K.zconv = area.take(TT, CONV_W)
    K.rows = area.take(TT, N_ROWS)
    K.y = area.take(TT, D)
    K.v = area.take(TT, HEADS, VD)
    K.q_t = area.take(HEADS, SEQ)
    K.k_t = area.take(HEADS, SEQ)
    K.g_q = area.take(Q_LORA // P)
    K.g_kv = area.take(KV_LORA // P)
    K.g_branch = area.take(KD)
    K.cb = area.take(3, 2)
    K.cw = area.take(2, CONV_K)
    K.sgb = area.take(SG_HEADS)
    K.sgw = area.take(SG_HEADS, P)
    K.pwb = area.take(CONV_W)
    K.gqk = area.take(2, QK)
    K.sgln = area.take(2, SG_W)
    K.first_end = area.at


def build(nc, ins, out):
    K = Names()
    K.nc, K.i, K.out = nc, ins, out
    K.layer = lambda name, l: ins[name][bass.ds(l, 1), :]
    memory(nc, K)
    S = Stages(nc)
    with nc.allow_non_contiguous_dma("parameters by channel, a few KB"):
        stage_setup(K, S)
        stage_rope_tables(K, S)
        first_block(K, S)
        second_block(K, S)


def kernel(**inputs):
    import numpy as _np
    import concourse.bacc as _bacc
    from concourse import mybir as _mybir
    from concourse.bass_utils import run_bass_kernel_spmd as _run

    half = ROPE // 2
    inputs = dict(inputs)
    inputs["inv_freq"] = (_np.float32(10000.0) ** (-_np.arange(half, dtype=_np.float32) / _np.float32(half))
                          ).astype(_np.float32)[None]
    nc = _bacc.Bacc("TRN2", target_bir_lowering=False, num_devices=1)
    arrays, aps = {}, {}
    for name, value in inputs.items():
        a = _np.ascontiguousarray(value)
        arrays[f"in_{name}_dram"] = a
        aps[name] = nc.dram_tensor(f"in_{name}_dram", a.shape, _mybir.dt.from_np(a.dtype),
                                   kind="ExternalInput").ap()
    out = nc.dram_tensor("out_0_dram", (1, SEQ, D), F32, kind="ExternalOutput").ap()
    build(nc, aps, out)
    r = _run(nc, [arrays], core_ids=[0])
    return r.results[0]["out_0_dram"]
```

```python
from contextlib import ExitStack, contextmanager

import numpy as np

import concourse.bass as bass
from concourse import mybir

F32 = mybir.dt.float32
U32 = mybir.dt.uint32
I32 = mybir.dt.int32
U8 = mybir.dt.uint8
ALU = mybir.AluOpType
ACT = mybir.ActivationFunctionType
AX = mybir.AxisListType

P = 128
SEQ = 256
TT = SEQ // P
D = 1024
KD = D // P
DEPTH = 2
EPS = 1e-6
NEG = -1e30

CONV_W = 256
CONV_K = 31
HEADS = 8
NOPE = 64
ROPE = 32
HALF = ROPE // 2
QK = NOPE + ROPE
VD = 64
MLA_W = HEADS * VD
Q_LORA = 768
KV_LORA = 256
SG_W = 256
SG_HEADS = 4
SG_D = SG_W // SG_HEADS

C_ZCONV = 2 * CONV_W
C_CQ = 3 * CONV_W
C_ROWS = C_CQ + Q_LORA + KV_LORA
IN_COLS = C_ROWS + ROPE + MLA_W + 3 * SG_W
N_ROWS = IN_COLS - C_ROWS
R_ROPE, R_ZMLA, R_U = 0, ROPE, ROPE + MLA_W
R_V, R_ZSG = R_U + SG_W, R_U + 2 * SG_W

STAGE_SEMS = 62


class Names:
    pass


class Link:

    def __init__(self, engine, sem, base=0):
        self.engine, self.sem, self.base, self.n = engine, sem, base, 0

    def __call__(self, instruction):
        instruction.then_inc(self.sem, 1)
        self.n += 1
        self.engine.wait_ge(self.sem, self.base + self.n)
        return instruction


class Area:

    def __init__(self, arena, at=0):
        self.arena, self.at = arena, at

    def take(self, *dims, parts=P):
        n = int(np.prod(dims))
        piece = self.arena[0:parts, self.at:self.at + n]
        self.at += n + n % 2
        if len(dims) == 1:
            return piece
        names = "abcd"[:len(dims)]
        sizes = {c: d for c, d in zip(names, dims)}
        return piece.rearrange(f"p ({' '.join(names)}) -> p {' '.join(names)}", **sizes)


class Stages:

    def __init__(self, nc):
        self.nc, self.turn = nc, 0
        self.banks = []
        for b in range(2):
            handles = [nc.alloc_semaphore(f"stage_bank{b}_{i}") for i in range(STAGE_SEMS)]
            self.banks.append(handles)

    @contextmanager
    def open(self):
        nc = self.nc
        idle, mine = self.banks[1 - self.turn], list(self.banks[self.turn])
        nums = sorted(s.num for s in idle)
        assert nums == list(range(nums[0], nums[0] + STAGE_SEMS))
        nc.gpsimd.sem_clear(range(nums[0], nums[-1] + 1))
        with nc.Block(no_gpsimd_drain=True) as block:
            yield block, (lambda name: mine.pop(0))
        self.turn = 1 - self.turn


def load_cols(dma, out, src, chunks):
    return dma(out, src.rearrange("a (k p) -> p (a k)", k=chunks))


def cast_rows(src):
    return src.broadcast_to([P, src.shape[1]])



class NormTranspose:

    def __init__(self, K, sem, area):
        self.K = K
        self.xn = area.take(TT, D)
        self.sq = area.take(D)
        self.stat = area.take(3, TT)
        self.ms_ready = sem("ms_ready")
        self.var_ready = sem("var_ready")
        self.sd_ready = sem("sd_ready")
        self.xn_ready = sem("xn_ready")
        self.xt_ready = sem("xt_ready")

    def act(self, act):
        K, nc = self.K, self.K.nc
        for t in range(TT):
            nc.scalar.activation(self.xn[:, t], K.x[:, t], ACT.Square,
                                 accum_out=self.stat[:, 0, t:t + 1]).then_inc(self.ms_ready, 1)
        act.wait_ge(self.var_ready, 1)
        nc.scalar.activation(self.stat[:, 2], self.stat[:, 1], ACT.Sqrt).then_inc(self.sd_ready, 1)

    def dve_norm(self, dve, link):
        K, nc = self.K, self.K.nc
        dve.wait_ge(self.ms_ready, TT)
        nc.vector.tensor_scalar(self.stat[:, 1], self.stat[:, 0], 1.0 / D, EPS, ALU.mult,
                                ALU.add).then_inc(self.var_ready, 1)
        dve.wait_ge(self.sd_ready, 1)
        link(nc.vector.reciprocal(self.stat[:, 0], self.stat[:, 2]))
        for t in range(TT):
            nc.vector.tensor_scalar(self.xn[:, t], K.x[:, t], self.stat[:, 0, t:t + 1], None,
                                    ALU.mult).then_inc(self.xn_ready, 1)

    def pe(self, pe):
        K, nc = self.K, self.K.nc
        for t in range(TT):
            pe.wait_ge(self.xn_ready, t + 1)
            for k in range(KD):
                last = nc.tensor.transpose(K.ps_low[:, k, t * P:(t + 1) * P],
                                           self.xn[:, t, k * P:(k + 1) * P], K.ident[:])
            last.then_inc(self.xt_ready, 1)

    def dve_scale(self, dve, gain, shift, h_ready):
        K, nc = self.K, self.K.nc
        dve.wait_ge(self.xt_ready, TT)
        for k in range(KD):
            if shift is None:
                ins = nc.vector.tensor_scalar(K.h_t[:, k], K.ps_low[:, k], gain[:, k:k + 1], None,
                                              ALU.mult)
            else:
                ins = nc.vector.tensor_scalar(K.h_t[:, k], K.ps_low[:, k], gain[:, k:k + 1],
                                              shift[:, k:k + 1], ALU.mult, ALU.add)
            ins.then_inc(h_ready, 1)


def matmul_rows(nc, out, lhs_t, w, t, chunks):
    for k in range(chunks):
        last = nc.tensor.matmul(out, lhs_t[:, k, t * P:(t + 1) * P], w[:, k],
                                start=(k == 0), stop=(k == chunks - 1))
    return last


def matmul_cols(nc, out, w, rhs_t, c, chunks):
    for k in range(chunks):
        last = nc.tensor.matmul(out, w[:, k, c * P:(c + 1) * P], rhs_t[:, k],
                                start=(k == 0), stop=(k == chunks - 1))
    return last



def stage_setup(K, S):
    nc = K.nc
    with S.open() as (block, sem):
        loaded, zeroed, made = sem("loaded"), sem("zeroed"), sem("made")

        @block.sync
        def _(sp):
            sp.dma_start(K.x[:], K.i["x"].rearrange("b (t p) d -> p (b t) d", p=P)).then_inc(loaded, 16)
            sp.dma_start(K.invf[:], K.i["inv_freq"].broadcast_to([P, HALF])).then_inc(loaded, 16)
            sp.wait_ge(loaded, 32)

        @block.gpsimd
        def _(pool):
            nc.gpsimd.memset(K.ident[:], 0.0)
            nc.gpsimd.memset(K.ones[:], 1.0)
            nc.gpsimd.memset(K.causal[:], 0.0)
            nc.gpsimd.iota(K.pos[:], pattern=[[P, TT]], base=0, channel_multiplier=1,
                           allow_small_or_imprecise_dtypes=True).then_inc(zeroed, 1)
            pool.wait_ge(zeroed, 1)
            nc.gpsimd.affine_select(out=K.ident[:], in_=K.ident[:], compare_op=ALU.not_equal,
                                    fill=1.0, base=0, pattern=[[-1, P]], channel_multiplier=1)
            nc.gpsimd.affine_select(out=K.causal[:], in_=K.causal[:], compare_op=ALU.is_ge,
                                    fill=NEG, base=0, pattern=[[-1, P]],
                                    channel_multiplier=1).then_inc(made, 1)
            pool.wait_ge(made, 1)


def stage_rope_tables(K, S):
    nc = K.nc
    two_pi = 2 * np.pi
    hi = float(np.float32(6.28125))
    mid = float(np.float32(np.round((two_pi - hi) * 2**20) / 2**20))
    low = float(np.float32(two_pi - hi - mid))
    with S.open() as (block, sem):
        chain, angle_ready, sin_done = sem("chain"), sem("angle_ready"), sem("sin_done")
        area = Area(K.arena)
        ang, turns, red, whole = (area.take(TT, HALF) for _ in range(4))
        whole_i = whole.bitcast(I32)

        @block.vector
        def _(dve):
            link = Link(dve, chain)
            for t in range(TT):
                link(nc.vector.tensor_scalar(ang[:, t], K.invf[:], K.pos[:, t:t + 1], None, ALU.mult))
            for n, (table, shift) in enumerate(((K.sin, 0.0), (K.cos, 0.25))):
                link(nc.vector.tensor_scalar(turns, ang, 1.0 / two_pi, shift, ALU.mult, ALU.add))
                link(nc.vector.tensor_copy(whole_i, turns))
                link(nc.vector.tensor_copy(turns, whole_i))
                link(nc.vector.scalar_tensor_tensor(red, turns, -hi, ang, ALU.mult, ALU.add))
                link(nc.vector.scalar_tensor_tensor(red, turns, -mid, red, ALU.mult, ALU.add))
                link(nc.vector.scalar_tensor_tensor(red, turns, -low, red, ALU.mult, ALU.add))
                if shift:
                    link(nc.vector.tensor_scalar(red, red, float(np.pi / 2), None, ALU.add))
                link(nc.vector.tensor_scalar(table[:], red, float(-np.pi), float(np.pi), ALU.max, ALU.min))
            dve.sem_inc(angle_ready, 1)

        @block.scalar
        def _(act):
            act.wait_ge(angle_ready, 1)
            nc.scalar.activation(K.sin[:], K.sin[:], ACT.Sin)
            nc.scalar.activation(K.cos[:], K.cos[:], ACT.Sin).then_inc(sin_done, 1)
            act.wait_ge(sin_done, 1)



IN_BLOCKS = [("cols", 0, 512), ("rows", C_ZCONV, 256), ("cols", C_CQ, 512),
             ("cols", C_CQ + 512, 512), ("rows", C_ROWS, 512), ("rows", C_ROWS + 512, 512),
             ("rows", C_ROWS + 1024, N_ROWS - 1024)]


def stage_in_projection(K, S, l):
    nc, i = K.nc, K.i
    with S.open() as (block, sem):
        area = Area(K.arena, K.first_end)
        norm = NormTranspose(K, sem, area)
        chain, params, h_ready = sem("chain"), sem("params"), sem("h_ready")
        gain_loaded = sem("gain_loaded")
        w_loaded = [sem("w_loaded0"), sem("w_loaded1")]
        proj_ready, proj_out = sem("proj_ready"), sem("proj_out")

        def load_parameters(sp):
            load = lambda out, name, chunks: load_cols(
                sp.dma_start, out, K.layer(name, l), chunks).then_inc(params, 16)
            load(K.g_q[:], "q_norm_g", Q_LORA // P)
            load(K.g_kv[:], "kv_norm_g", KV_LORA // P)
            load(K.cb[:, 0], "conv_b", 2)
            load(K.cb[:, 1], "conv_ln_g", 2)
            load(K.cb[:, 2], "conv_ln_b", 2)
            load(K.g_branch[:], "branch_norm_g", KD)
            for c in range(2):
                sp.dma_start(K.cw[:, c], i["conv_w"][bass.ds(l, 1), :, c * P:(c + 1) * P].rearrange(
                    "a k p -> p (a k)")).then_inc(params, 16)
            sp.dma_start(K.sgb[:], i["sg_b"][bass.ds(l, 1)].rearrange("a g t -> t (a g)")).then_inc(params, 16)
            sp.dma_start(K.sgw[:], i["sg_w"][bass.ds(l, 1)].rearrange("a g t s -> t (a g) s")).then_inc(params, 16)
            for out, name in ((K.pwb, "conv_pw_b"), (K.gqk[:, 0], "qk_q_g"), (K.gqk[:, 1], "qk_k_g"),
                              (K.sgln[:, 0], "sg_ln_g"), (K.sgln[:, 1], "sg_ln_b")):
                sp.dma_start(out,
                               cast_rows(K.layer(name, l))).then_inc(params, 16)

        @block.sync
        def _(sp):
            load_cols(sp.dma_start, K.g_norm[:], K.layer("norm_g", l), KD).then_inc(gain_loaded, 16)
            for n, (_, c0, width) in enumerate(IN_BLOCKS):
                if n == 2:
                    load_parameters(sp)
                if n >= 2:
                    sp.wait_ge(proj_ready, n - 1)
                src = i["w_in"][bass.ds(l, 1), :, c0:c0 + width].rearrange("a (k p) n -> p (a k) n", p=P)
                sp.dma_start(K.wslot[n % 2][:, :, 0:width], src).then_inc(w_loaded[n % 2], 16)

        @block.scalar
        def _(act):
            norm.act(act)
        @block.tensor
        def _(pe):
            norm.pe(pe)
            for n, (kind, c0, width) in enumerate(IN_BLOCKS):
                pe.wait_ge(w_loaded[n % 2], 16 * (n // 2 + 1))
                if n == 0:
                    pe.wait_ge(h_ready, KD)
                if n >= 2:
                    pe.wait_ge(proj_out, n - 1)
                w, ps = K.wslot[n % 2], K.ps_pair[n % 2]
                if kind == "cols":
                    for c in range(width // P):
                        last = matmul_cols(nc, ps[:, c // 2, (c % 2) * SEQ:(c % 2 + 1) * SEQ], w,
                                           K.h_t, c, KD)
                else:
                    for t in range(TT):
                        last = matmul_rows(nc, ps[:, t, 0:width], K.h_t, w[:, :, 0:width], t, KD)
                last.then_inc(proj_ready, 1)

        @block.vector
        def _(dve):
            link = Link(dve, chain)
            norm.dve_norm(dve, link)
            dve.wait_ge(gain_loaded, 16)
            norm.dve_scale(dve, K.g_norm, None, h_ready)
            for n, (kind, c0, width) in enumerate(IN_BLOCKS):
                dve.wait_ge(proj_ready, n + 1)
                ps = K.ps_pair[n % 2]
                if kind == "cols":
                    dst = K.glu if c0 == 0 else K.low[:, (c0 - C_CQ) // P:(c0 - C_CQ) // P + 4]
                    ins = nc.vector.tensor_copy(dst.rearrange("p c t -> p (c t)"),
                                                ps.rearrange("p b n -> p (b n)"))
                elif c0 == C_ZCONV:
                    ins = nc.vector.tensor_copy(K.zconv, ps[:, :, 0:width])
                else:
                    ins = nc.vector.tensor_copy(K.rows[:, :, c0 - C_ROWS:c0 - C_ROWS + width],
                                                ps[:, :, 0:width])
                ins.then_inc(proj_out, 1)
            dve.wait_ge(params, 16 * 15)


class ModulationProducts:

    def __init__(self, K, sem, area, row_area, l, n0, blocks, banks):
        self.K, self.l, self.n0, self.blocks, self.banks = K, l, n0, blocks, banks
        self.c = area.take(KD)
        self.row = row_area.take(len(banks), 512)
        self.ring = K.ring[:].rearrange("p (s k n) -> p s k n", s=2, k=KD // 2)
        self.c_loaded, self.c_ready = sem("c_loaded"), sem("c_ready")
        self.w_loaded = [sem("ada_loaded0"), sem("ada_loaded1")]
        self.w_used, self.row_ready, self.stored = sem("ada_used"), sem("ada_row"), sem("ada_stored")

    def load_c(self, sp):
        load_cols(sp.dma_start, self.c, self.K.i["c_2"], KD).then_inc(self.c_loaded, 16)

    def load(self, sp, first, last):
        for m in range(first, last):
            if m >= 2:
                sp.wait_ge(self.w_used, m - 1)
            src = self.K.i["w_ada_2"][self.l, (m % 2) * 512:(m % 2 + 1) * 512,
                                      bass.ds(self.n0 * 512 + (m // 2) * 512, 512)]
            sp.dma_start(self.ring[:, m % 2], src.rearrange("(k p) n -> p k n", p=P)
                         ).then_inc(self.w_loaded[m % 2], 16)

    def silu(self, act):
        act.wait_ge(self.c_loaded, 16)
        self.K.nc.scalar.activation(self.c, self.c, ACT.Silu).then_inc(self.c_ready, 1)

    def out(self, q):
        part, bank = 32 * (q % 4), self.banks[q // 4]
        return self.K.ps[part:part + 1, bank]

    def pe(self, pe, first, last):
        if first == 0:
            pe.wait_ge(self.c_ready, 1)
        for m in range(first, last):
            pe.wait_ge(self.w_loaded[m % 2], 16 * (m // 2 + 1))
            for k in range(KD // 2):
                kk = (m % 2) * (KD // 2) + k
                ins = self.K.nc.tensor.matmul(self.out(m // 2), self.c[:, kk:kk + 1], self.ring[:, m % 2, k],
                                              start=(kk == 0), stop=(kk == KD - 1),
                                              tile_position=(0, 32 * (m // 2 % 4)))
            ins.then_inc(self.w_used, 1)

    def act_out(self, act):
        act.wait_ge(self.w_used, 2 * self.blocks)
        for q in range(self.blocks):
            part = 32 * (q % 4)
            ins = self.K.nc.scalar.copy(self.row[part:part + 1, q // 4], self.out(q))
        ins.then_inc(self.row_ready, 1)

    def store(self, sp):
        sp.wait_ge(self.row_ready, 1)
        for q in range(self.blocks):
            part = 32 * (q % 4)
            dst = self.K.mod_dram[self.l:self.l + 1, bass.ds(self.n0 * 512 + q * 512, 512)]
            sp.dma_start(dst, self.row[part:part + 1, q // 4]).then_inc(self.stored, 16)
        sp.wait_ge(self.stored, 16 * self.blocks)


def stage_mixers(K, S, l):
    nc, i = K.nc, K.i
    NQ, NKV = Q_LORA // P, KV_LORA // P
    scale = float(QK) ** -0.5
    with S.open() as (block, sem):
        area = Area(K.arena, K.first_end)
        padded = area.take(2, SEQ + CONV_K - 1)
        gate, acc, xc, rstd = (area.take(2, SEQ) for _ in range(4))
        csq = gate
        szc = area.take(TT, CONV_W)
        sq_at = area.at
        sq = area.take(NQ + NKV, SEQ)
        qk_at = area.at
        q = area.take(TT, HEADS, QK)
        k = area.take(TT, HEADS, QK)
        rot_at = area.at
        rot = area.take(4, TT, HEADS, HALF)
        hsq = Area(K.arena, sq_at).take(TT, HEADS, QK)
        s = Area(K.arena, sq_at).take(2, 4, SEQ)
        p_t = Area(K.arena, qk_at).take(2, 4, TT, P)
        szm = Area(K.arena, rot_at).take(TT, MLA_W)
        st = area.take(3, 2, TT)
        hst = area.take(3, 2, TT * HEADS)
        mx = area.take(2, 4)
        sums = area.take(TT, HEADS)
        bn, mv, sd = area.take(TT, 6), area.take(TT, 2), area.take(TT, 2)
        low_flat = K.low.rearrange("p c t -> p (c t)")
        u, v, szs, mixed = (low_flat[:, n * 512:(n + 1) * 512].rearrange("p (t n) -> p t n", t=TT)
                            for n in range(4))
        w_t = K.glu[:, 0:2].rearrange("p c t -> p (c t)").rearrange("p (g s) -> p g s", g=SG_HEADS)
        w_uq = K.big[:, 0:NQ * HEADS * QK].rearrange("p (k n) -> p k n", k=NQ)
        at = NQ * HEADS * QK
        w_ukv = K.big[:, at:at + NKV * 1024].rearrange("p (k n) -> p k n", k=NKV)
        at += NKV * 1024
        pw = K.big[:, at:at + 2 * CONV_W].rearrange("p (k n) -> p k n", k=2)
        rows_area = Area(K.arena, 24576 + at + 2 * CONV_W)
        mod = ModulationProducts(K, sem, area, rows_area, 0, l * 6, 6, [4, 5])
        assert area.at <= 24576

        dve_chain, w_loaded, pw_loaded = sem("dve_chain"), sem("w_loaded"), sem("pw_loaded")
        gate_ready, acc_ready, mean_ready, xc_ready = sem("gate"), sem("acc"), sem("mean"), sem("xc")
        csq_ready, var_ready, veps_ready, csd_ready = sem("csq"), sem("var"), sem("veps"), sem("csd")
        ln_ready, csilu_ready, szc_ready, pw_ready = sem("ln"), sem("csilu"), sem("szc"), sem("pw")
        pw_out, padded_ready = sem("pw_out"), sem("padded")
        sq_ready, scaled, st_ready, st_eps, st_sd, st_rstd = (sem("sq"), sem("scaled"), sem("st"),
                                                              sem("st_eps"), sem("st_sd"), sem("st_rstd"))
        up_ready, up_out, hv_ready, hsd_ready = sem("up"), sem("up_out"), sem("hv"), sem("hsd")
        qk_ready, tr_ready, tr_out = sem("qk"), sem("tr"), sem("tr_out")
        s_ready, s_out, max_ready, e_ready = sem("s"), sem("s_out"), sem("max"), sem("e")
        pt_ready, pt_out, o_ready, szm_ready = sem("pt"), sem("pt_out"), sem("o"), sem("szm")
        sw_ready, sw_out, sw_kept, uv_ready = sem("sw"), sem("sw_out"), sem("sw_kept"), sem("uv")
        sd_eps, sd_ready, v_ready, mix_ready = sem("sd_eps"), sem("sd"), sem("v"), sem("mix")
        st_ps = K.ps[:, 6]
        mean_ps, var_ps = K.ps[:, 6, 0:SEQ], K.ps[:, 6, SEQ:2 * SEQ]
        pw_ps = K.ps[:, 7].rearrange("p (t n) -> p t n", t=TT)
        mix_ps = K.ps[:, 0].rearrange("p (t n) -> p t n", t=TT)
        groups = [(t, g) for t in range(TT) for g in range(2)]

        def s_ps(n, keys):
            return K.ps[:, 2 * (n % 2):2 * (n % 2) + 2].rearrange("p b (h c) -> p (b h) c", h=2)[:, :, 0:keys]

        @block.sync
        def _(sp):
            mod.load_c(sp)
            sp.dma_start(w_uq, i["w_uq"][bass.ds(l, 1)].rearrange("a (k p) n -> p (a k) n", p=P)
                         ).then_inc(w_loaded, 16)
            sp.dma_start(w_ukv, i["w_ukv"][bass.ds(l, 1)].rearrange("a (k p) n -> p (a k) n", p=P)
                         ).then_inc(w_loaded, 16)
            mod.load(sp, 0, 2)
            sp.dma_start(pw, i["conv_pw_w"][bass.ds(l, 1)].rearrange("a (k p) n -> p (a k) n", p=P)
                         ).then_inc(pw_loaded, 16)
            mod.load(sp, 2, 12)
            mod.store(sp)

        @block.gpsimd
        def _(pool):
            pool.wait_ge(sw_out, 1)
            nc.gpsimd.affine_select(out=w_t, in_=w_t, compare_op=ALU.is_ge, fill=0.0, base=0,
                                    pattern=[[0, SG_HEADS], [1, P]], channel_multiplier=-1
                                    ).then_inc(sw_kept, 1)

        @block.scalar
        def _(act):
            nc.scalar.activation(sq, K.low, ACT.Square).then_inc(sq_ready, 1)
            act.wait_ge(sq_ready, 1)
            for c in range(NQ + NKV):
                g = K.g_q[:, c:c + 1] if c < NQ else K.g_kv[:, c - NQ:c - NQ + 1]
                nc.scalar.activation(K.low[:, c], K.low[:, c], ACT.Copy, scale=g).then_inc(scaled, 1)
            nc.scalar.activation(gate, K.glu[:, 2:4], ACT.Sigmoid).then_inc(gate_ready, 1)
            mod.silu(act)
            act.wait_ge(st_eps, 1)
            nc.scalar.activation(st[:, 2], st[:, 1], ACT.Sqrt).then_inc(st_sd, 1)
            act.wait_ge(st_rstd, 1)
            for t in range(TT):
                act.wait_ge(up_ready, t + 1)
                for half in range(2):
                    hs = slice(4 * half, 4 * half + 4)
                    nc.scalar.activation(q[:, t, hs].rearrange("p h d -> p (h d)"), K.ps[:, half, 0:4 * QK],
                                         ACT.Copy, scale=st[:, 0, 0, t:t + 1])
                    kv = K.ps[:, 2 + half].rearrange("p (h d) -> p h d", h=4)
                    nc.scalar.activation(k[:, t, hs, 0:NOPE], kv[:, :, 0:NOPE], ACT.Copy,
                                         scale=st[:, 0, 1, t:t + 1])
                    ins = nc.scalar.activation(K.v[:, t, hs], kv[:, :, NOPE:], ACT.Copy,
                                               scale=st[:, 0, 1, t:t + 1])
                ins.then_inc(up_out, 1)
            act.wait_ge(hv_ready, 1)
            nc.scalar.activation(hst[:, 2], hst[:, 1], ACT.Sqrt).then_inc(hsd_ready, 1)
            act.wait_ge(xc_ready, 1)
            nc.scalar.activation(csq, xc, ACT.Square).then_inc(csq_ready, 1)
            act.wait_ge(veps_ready, 1)
            nc.scalar.activation(rstd[:, 1], rstd[:, 0], ACT.Sqrt).then_inc(csd_ready, 1)
            nc.scalar.activation(szc, K.zconv, ACT.Silu).then_inc(szc_ready, 1)
            act.wait_ge(ln_ready, 1)
            for c in range(2):
                nc.scalar.activation(acc[:, c], xc[:, c], ACT.Silu, bias=K.cb[:, 2, c:c + 1],
                                     scale=K.cb[:, 1, c:c + 1]).then_inc(csilu_ready, 1)
            act.wait_ge(qk_ready, 2)
            nc.scalar.activation(szm, K.rows[:, :, R_ZMLA:R_ZMLA + MLA_W], ACT.Silu).then_inc(szm_ready, 1)
            nc.scalar.activation(szs, K.rows[:, :, R_ZSG:R_ZSG + SG_W], ACT.Silu)
            nc.scalar.activation(v, K.rows[:, :, R_V:R_V + SG_W], ACT.Gelu_apprx_tanh)
            nc.scalar.activation(u, K.rows[:, :, R_U:R_U + SG_W], ACT.Gelu_apprx_tanh).then_inc(uv_ready, 1)
            mod.act_out(act)
            for n, (t, g) in enumerate(groups):
                keys = (t + 1) * P
                act.wait_ge(max_ready, n + 1)
                for h in range(4):
                    nc.scalar.activation(s[:, n % 2, h, 0:keys], s[:, n % 2, h, 0:keys], ACT.Exp,
                                         bias=mx[:, n % 2, h:h + 1],
                                         accum_out=sums[:, t, 4 * g + h:4 * g + h + 1]
                                         ).then_inc(e_ready, 1)
            act.wait_ge(sd_eps, 1)
            nc.scalar.activation(sd[:, :, 1], sd[:, :, 0], ACT.Sqrt).then_inc(sd_ready, 1)

        @block.tensor
        def _(pe):
            pe.wait_ge(sq_ready, 1)
            for n, (c0, c1) in enumerate(((0, NQ), (NQ, NQ + NKV))):
                for t in range(TT):
                    for c in range(c0, c1):
                        last = nc.tensor.matmul(st_ps[:, n * TT + t:n * TT + t + 1],
                                                sq[:, c, t * P:(t + 1) * P], K.ones[:, 0:1],
                                                start=(c == c0), stop=(c == c1 - 1))
            last.then_inc(st_ready, 1)
            for g in range(SG_HEADS):
                last = nc.tensor.transpose(K.ps[:, 7, g * P:(g + 1) * P], K.sgw[:, g], K.ident[:])
            last.then_inc(sw_ready, 1)
            pe.wait_ge(w_loaded, 32)
            pe.wait_ge(scaled, NQ + NKV)
            for t in range(TT):
                if t:
                    pe.wait_ge(up_out, t)
                for half in range(2):
                    matmul_rows(nc, K.ps[:, half, 0:4 * QK], K.low[:, 0:NQ],
                                w_uq[:, :, half * 4 * QK:(half + 1) * 4 * QK], t, NQ)
                for half in range(2):
                    last = matmul_rows(nc, K.ps[:, 2 + half], K.low[:, NQ:],
                                       w_ukv[:, :, half * 512:(half + 1) * 512], t, NKV)
                last.then_inc(up_ready, 1)
            pe.wait_ge(st_eps, 1)
            pe.wait_ge(acc_ready, 1)
            for c in range(2):
                last = nc.tensor.matmul(mean_ps, K.ones[:], acc[:, c], start=(c == 0), stop=(c == 1))
            last.then_inc(mean_ready, 1)
            mod.pe(pe, 0, 4)
            pe.wait_ge(csq_ready, 1)
            for c in range(2):
                last = nc.tensor.matmul(var_ps, K.ones[:], csq[:, c], start=(c == 0), stop=(c == 1))
            last.then_inc(var_ready, 1)
            mod.pe(pe, 4, 12)
            pe.wait_ge(up_out, TT)
            for n, src in enumerate((q, k)):
                pe.wait_ge(qk_ready, n + 1)
                for h in range(HEADS):
                    if n and h % 2 == 0:
                        pe.wait_ge(tr_out, h // 2 + 1)
                    for t in range(TT):
                        last = nc.tensor.transpose(
                            K.ps[0:QK, h // 2, (h % 2) * SEQ + t * P:(h % 2) * SEQ + (t + 1) * P],
                            src[:, t, h], K.ident[:])
                    if h % 2:
                        last.then_inc(tr_ready, 1)
            pe.wait_ge(pw_loaded, 16)
            pe.wait_ge(csilu_ready, 2)
            pe.wait_ge(sw_out, 1)
            for t in range(TT):
                last = matmul_rows(nc, pw_ps[:, t], acc, pw, t, 2)
            last.then_inc(pw_ready, 1)

            def scores(n):
                t, g = groups[n]
                if n == 0:
                    pe.wait_ge(tr_out, 8)
                if n >= 2:
                    pe.wait_ge(s_out, n - 1)
                for h in range(4):
                    last = nc.tensor.matmul(s_ps(n, (t + 1) * P)[:, h],
                                            K.q_t[0:QK, 4 * g + h, t * P:(t + 1) * P],
                                            K.k_t[0:QK, 4 * g + h, 0:(t + 1) * P], start=True, stop=True)
                last.then_inc(s_ready, 1)

            scores(0)
            for n, (t, g) in enumerate(groups):
                if n + 1 < len(groups):
                    scores(n + 1)
                pe.wait_ge(e_ready, 4 * (n + 1))
                if n >= 1:
                    pe.wait_ge(pt_out, n)
                for h in range(4):
                    for kt in range(t + 1):
                        last = nc.tensor.transpose(
                            K.ps[:, 4 + h // 2, (h % 2) * SEQ + kt * P:(h % 2) * SEQ + (kt + 1) * P],
                            s[:, n % 2, h, kt * P:(kt + 1) * P], K.ident[:])
                last.then_inc(pt_ready, 1)
                pe.wait_ge(pt_out, n + 1)
                if n == 0:
                    pe.wait_ge(pw_out, 1)
                for h in range(4):
                    for kt in range(t + 1):
                        last = nc.tensor.matmul(K.ps[:, 6 + t, (4 * g + h) * VD:(4 * g + h + 1) * VD],
                                                p_t[:, n % 2, h, kt], K.v[:, kt, 4 * g + h],
                                                start=(kt == 0), stop=(kt == t))
                last.then_inc(o_ready, 1)
            pe.wait_ge(sw_kept, 1)
            pe.wait_ge(v_ready, 1)
            for t in range(TT):
                for g in range(SG_HEADS):
                    last = nc.tensor.matmul(mix_ps[:, t, g * SG_D:(g + 1) * SG_D], w_t[:, g],
                                            v[:, t, g * SG_D:(g + 1) * SG_D], start=True, stop=True)
            last.then_inc(mix_ready, 1)

        @block.vector
        def _(dve):
            link = Link(dve, dve_chain)
            nc.vector.memset(padded[:, :, 0:CONV_K - 1], 0.0)
            dve.wait_ge(st_ready, 1)
            for n, width in enumerate((Q_LORA, KV_LORA)):
                ins = nc.vector.tensor_scalar(st[:, 1, n], st_ps[:, n * TT:(n + 1) * TT], 1.0 / width,
                                              EPS, ALU.mult, ALU.add)
            ins.then_inc(st_eps, 1)
            dve.wait_ge(gate_ready, 1)
            link(nc.vector.tensor_tensor(padded[:, :, CONV_K - 1:], K.glu[:, 0:2], gate, ALU.mult))
            dve.wait_ge(sw_ready, 1)
            nc.vector.tensor_copy(w_t.rearrange("p g s -> p (g s)"), K.ps[:, 7]).then_inc(sw_out, 1)
            dve.wait_ge(st_sd, 1)
            nc.vector.reciprocal(st[:, 0], st[:, 2]).then_inc(st_rstd, 1)
            for j in range(CONV_K):
                for c in range(2):
                    w = K.cw[:, c, j:j + 1]
                    if j == 0:
                        ins = nc.vector.tensor_scalar(acc[:, c], padded[:, c, 0:SEQ], w,
                                                      K.cb[:, 0, c:c + 1], ALU.mult, ALU.add)
                    else:
                        ins = nc.vector.scalar_tensor_tensor(acc[:, c], padded[:, c, j:j + SEQ], w,
                                                             acc[:, c], ALU.mult, ALU.add)
                    if c == 1 and j < CONV_K - 1:
                        link(ins)
            ins.then_inc(acc_ready, 1)

            for t in range(TT):
                ins = nc.vector.tensor_copy(
                    k[:, t, :, NOPE:],
                    K.rows[:, t, R_ROPE:R_ROPE + ROPE].unsqueeze(1).broadcast_to([P, HEADS, ROPE]))
            link(ins)
            dve.wait_ge(up_out, TT)
            flat = lambda a: a.rearrange("p t h d -> p (t h) d")
            for n, src in enumerate((q, k)):
                link(nc.vector.tensor_tensor(hsq, src, src, ALU.mult))
                link(nc.vector.tensor_reduce(hst[:, 0, n], flat(hsq), AX.X, ALU.add))
            nc.vector.tensor_scalar(hst[:, 1], hst[:, 0], 1.0 / QK, EPS, ALU.mult,
                                    ALU.add).then_inc(hv_ready, 1)
            dve.wait_ge(mean_ready, 1)
            for c in range(2):
                ins = nc.vector.scalar_tensor_tensor(xc[:, c], mean_ps, -1.0 / CONV_W, acc[:, c],
                                                     ALU.mult, ALU.add)
            ins.then_inc(xc_ready, 1)
            dve.wait_ge(hsd_ready, 1)
            link(nc.vector.reciprocal(hst[:, 0], hst[:, 2]))
            for n, src in enumerate((q, k)):
                link(nc.vector.tensor_tensor(
                    flat(src), flat(src),
                    hst[:, 0, n].unsqueeze(2).broadcast_to([P, TT * HEADS, QK]), ALU.mult))
                link(nc.vector.tensor_tensor(
                    flat(src), flat(src),
                    K.gqk[:, n].unsqueeze(1).broadcast_to([P, TT * HEADS, QK]), ALU.mult))
                for t in range(TT):
                    x1, x2 = src[:, t, :, NOPE:NOPE + HALF], src[:, t, :, NOPE + HALF:]
                    cos = K.cos[:, t].unsqueeze(1).broadcast_to([P, HEADS, HALF])
                    sin = K.sin[:, t].unsqueeze(1).broadcast_to([P, HEADS, HALF])
                    nc.vector.tensor_tensor(rot[:, 0, t], x1, cos, ALU.mult)
                    nc.vector.tensor_tensor(rot[:, 1, t], x2, sin, ALU.mult)
                    nc.vector.tensor_tensor(rot[:, 2, t], x1, sin, ALU.mult)
                    link(nc.vector.tensor_tensor(rot[:, 3, t], x2, cos, ALU.mult))
                    nc.vector.tensor_tensor(x1, rot[:, 0, t], rot[:, 1, t], ALU.subtract)
                    ins = nc.vector.tensor_tensor(x2, rot[:, 2, t], rot[:, 3, t], ALU.add)
                    if t == 0:
                        link(ins)
                ins.then_inc(qk_ready, 1)
                dve.wait_ge(qk_ready, n + 1)
            dve.wait_ge(var_ready, 1)
            nc.vector.tensor_scalar(rstd[:, 0], var_ps, 1.0 / CONV_W, EPS, ALU.mult,
                                    ALU.add).then_inc(veps_ready, 1)
            for n, dst in enumerate((K.q_t, K.k_t)):
                for b in range(4):
                    dve.wait_ge(tr_ready, n * 4 + b + 1)
                    nc.vector.tensor_copy(dst[0:QK, 2 * b:2 * b + 2].rearrange("p h t -> p (h t)"),
                                          K.ps[0:QK, b]).then_inc(tr_out, 1)
                if n == 0:
                    dve.wait_ge(csd_ready, 1)
                    link(nc.vector.reciprocal(rstd[:, 0], rstd[:, 1]))
                    for c in range(2):
                        ins = nc.vector.tensor_tensor(xc[:, c], xc[:, c], rstd[:, 0], ALU.mult)
                    ins.then_inc(ln_ready, 1)
            dve.wait_ge(szc_ready, 1)
            dve.wait_ge(pw_ready, 1)
            for t in range(TT):
                ins = nc.vector.tensor_tensor(K.y[:, t, 0:CONV_W], pw_ps[:, t], K.pwb[:], ALU.add)
            ins.then_inc(pw_out, 1)
            dve.wait_ge(pw_out, 1)
            link(nc.vector.tensor_tensor(K.y[:, :, 0:CONV_W], K.y[:, :, 0:CONV_W], szc, ALU.mult))

            def probabilities_out(n):
                t, g = groups[n]
                dve.wait_ge(pt_ready, n + 1)
                if n >= 2:
                    dve.wait_ge(o_ready, n - 1)
                src = K.ps[:, 4:6].rearrange("p b (h c) -> p (b h) c", h=2)[:, :, 0:(t + 1) * P]
                nc.vector.tensor_copy(p_t[:, n % 2].rearrange("p h a b -> p h (a b)")[:, :, 0:(t + 1) * P],
                                      src).then_inc(pt_out, 1)

            for n, (t, g) in enumerate(groups):
                keys = (t + 1) * P
                dve.wait_ge(s_ready, n + 1)
                if n >= 2:
                    dve.wait_ge(pt_ready, n - 1)
                if t:
                    nc.vector.tensor_scalar(s[:, n % 2, :, 0:t * P], s_ps(n, keys)[:, :, 0:t * P], scale,
                                            None, ALU.mult)
                link(nc.vector.scalar_tensor_tensor(
                    s[:, n % 2, :, t * P:keys], s_ps(n, keys)[:, :, t * P:keys], scale,
                    K.causal[:].unsqueeze(1).broadcast_to([P, 4, P]), ALU.mult, ALU.add))
                dve.sem_inc(s_out, 1)
                if n >= 2:
                    dve.wait_ge(e_ready, 4 * (n - 1))
                link(nc.vector.tensor_reduce(mx[:, n % 2], s[:, n % 2, :, 0:keys], AX.X, ALU.max))
                nc.vector.tensor_scalar(mx[:, n % 2], mx[:, n % 2], -1.0, None,
                                        ALU.mult).then_inc(max_ready, 1)
                if n >= 1:
                    probabilities_out(n - 1)
            dve.wait_ge(uv_ready, 1)
            for t in range(TT):
                link(nc.vector.bn_stats(bn[:, t], v[:, t]))
                link(nc.vector.bn_aggr(mv[:, t], bn[:, t]))
            nc.vector.tensor_scalar(sd[:, :, 0], mv[:, :, 1], EPS, None, ALU.add).then_inc(sd_eps, 1)
            probabilities_out(len(groups) - 1)
            dve.wait_ge(sd_ready, 1)
            link(nc.vector.reciprocal(sd[:, :, 0], sd[:, :, 1]))
            for t in range(TT):
                ins = nc.vector.tensor_scalar(v[:, t], v[:, t], mv[:, t, 0:1], sd[:, t, 0:1],
                                              ALU.subtract, ALU.mult)
            link(ins)
            for w, op in enumerate((ALU.mult, ALU.add)):
                ins = nc.vector.tensor_tensor(v, v, K.sgln[:, w].unsqueeze(1).broadcast_to([P, TT, SG_W]), op)
                if w == 0:
                    link(ins)
            ins.then_inc(v_ready, 1)
            link(nc.vector.tensor_tensor(u, u, szs, ALU.mult))
            dve.wait_ge(o_ready, 4)
            dve.wait_ge(szm_ready, 1)
            link(nc.vector.reciprocal(sums, sums))
            for t in range(TT):
                y = K.y[:, t, CONV_W:CONV_W + MLA_W]
                ins = nc.vector.tensor_tensor(
                    y.rearrange("p (h d) -> p h d", h=HEADS),
                    K.ps[:, 6 + t].rearrange("p (h d) -> p h d", h=HEADS),
                    sums[:, t].unsqueeze(2).broadcast_to([P, HEADS, VD]), ALU.mult)
            link(ins)
            y = K.y[:, :, CONV_W:CONV_W + MLA_W]
            link(nc.vector.tensor_tensor(y, y, szm, ALU.mult))
            dve.wait_ge(mix_ready, 1)
            for t in range(TT):
                ins = nc.vector.tensor_tensor(
                    mixed[:, t].rearrange("p (g d) -> p g d", g=SG_HEADS),
                    mix_ps[:, t].rearrange("p (g d) -> p g d", g=SG_HEADS),
                    K.sgb[:].unsqueeze(2).broadcast_to([P, SG_HEADS, SG_D]), ALU.add)
            link(ins)
            link(nc.vector.tensor_tensor(K.y[:, :, CONV_W + MLA_W:], mixed, u, ALU.mult))


BRANCHES = ((0, CONV_W), (CONV_W, CONV_W + MLA_W), (CONV_W + MLA_W, D))


def stage_out_projection(K, S, l):
    nc, i = K.nc, K.i
    with S.open() as (block, sem):
        area = Area(K.arena, K.first_end)
        sq = area.take(TT, D)
        st = area.take(3, 3, TT)
        chain, w_loaded, ms_ready, var_ready = sem("chain"), sem("w_loaded"), sem("ms"), sem("var")
        sd_ready, yn_ready, yt_ready, y_out, o_ready = (sem("sd"), sem("yn"), sem("yt"), sem("y_out"),
                                                        sem("o_ready"))
        w = K.big.rearrange("p (k n) -> p k n", k=KD)

        @block.sync
        def _(sp):
            sp.dma_start(w, i["w_out"][bass.ds(l, 1)].rearrange("a (k p) n -> p (a k) n", p=P)
                         ).then_inc(w_loaded, 16)

        @block.scalar
        def _(act):
            for b, (c0, c1) in enumerate(BRANCHES):
                for t in range(TT):
                    nc.scalar.activation(sq[:, t, c0:c1], K.y[:, t, c0:c1], ACT.Square,
                                         accum_out=st[:, 0, b, t:t + 1]).then_inc(ms_ready, 1)
            act.wait_ge(var_ready, 1)
            nc.scalar.activation(st[:, 2], st[:, 1], ACT.Sqrt).then_inc(sd_ready, 1)

        @block.tensor
        def _(pe):
            pe.wait_ge(yn_ready, 1)
            for k in range(KD):
                for t in range(TT):
                    last = nc.tensor.transpose(K.ps_low[:, k, t * P:(t + 1) * P],
                                               K.y[:, t, k * P:(k + 1) * P], K.ident[:])
                last.then_inc(yt_ready, 1)
            pe.wait_ge(w_loaded, 16)
            pe.wait_ge(y_out, KD)
            for t in range(TT):
                for half in range(2):
                    last = matmul_rows(nc, K.ps[:, 4 + 2 * t + half], K.h_t,
                                       w[:, :, half * 512:(half + 1) * 512], t, KD)
                last.then_inc(o_ready, 1)

        @block.vector
        def _(dve):
            link = Link(dve, chain)
            dve.wait_ge(ms_ready, 6)
            for b, (c0, c1) in enumerate(BRANCHES):
                link(nc.vector.tensor_scalar(st[:, 1, b], st[:, 0, b], 1.0 / (c1 - c0), EPS, ALU.mult,
                                             ALU.add))
            dve.sem_inc(var_ready, 1)
            dve.wait_ge(sd_ready, 1)
            link(nc.vector.reciprocal(st[:, 0], st[:, 2]))
            for b, (c0, c1) in enumerate(BRANCHES):
                for t in range(TT):
                    link(nc.vector.tensor_scalar(K.y[:, t, c0:c1], K.y[:, t, c0:c1],
                                                 st[:, 0, b, t:t + 1], None, ALU.mult))
            dve.sem_inc(yn_ready, 1)
            for k in range(KD):
                dve.wait_ge(yt_ready, 2 * (k // 2) + 2)
                nc.vector.tensor_scalar(K.h_t[:, k], K.ps_low[:, k], K.g_branch[:, k:k + 1], None,
                                        ALU.mult).then_inc(y_out, 1)
            for t in range(TT):
                dve.wait_ge(o_ready, t + 1)
                link(nc.vector.tensor_tensor(
                    K.x[:, t], K.x[:, t],
                    K.ps[:, 4 + 2 * t:6 + 2 * t].rearrange("p b n -> p (b n)"), ALU.add))


def stage_rest(K, S):
    with S.open():
        pass


def first_block(K, S):
    with K.nc.Fori(0, DEPTH) as l:
        stage_in_projection(K, S, l)
        stage_mixers(K, S, l)
        stage_out_projection(K, S, l)
        stage_rest(K, S)



D5 = 5 * D
HG = 8
HD = D // HG
CH = SEQ // P
PRE = P + 1
LEVELS = [64, 32, 16, 8, 4, 2, 1]
LRU_BLOCKS = 4
LRU_BW = D // LRU_BLOCKS
TAPS = 4
LEFT = 2
LRU_C = 8.0
PH = 8
NKEYS = 128
TOPK = 16
HP = 2 * PH
BIG = 3.0e38


def stage_modulation(K, S, l):
    nc, i = K.nc, K.i
    with S.open() as (block, sem):
        area = Area(K.arena)
        bias_rows = area.take(2, D)
        cols, bias_cols = area.take(4, KD), area.take(4, KD)
        gains = area.take(2, KD)
        chain, cols_loaded, rows_loaded = sem("chain"), sem("cols_loaded"), sem("rows_loaded")
        shifts_scales, residual_gates = (0, 1, 3, 4), (2, 5)

        @block.sync
        def _(sp):
            for n, v in enumerate(shifts_scales):
                load_cols(sp.dma_start, cols[:, n], K.mod_dram[l:l + 1, v * D:(v + 1) * D], KD
                          ).then_inc(cols_loaded, 16)
            for n, v in enumerate(residual_gates):
                sp.dma_start(K.gate[:, n], K.mod_dram[l:l + 1, v * D:(v + 1) * D].broadcast_to([P, D])
                             ).then_inc(rows_loaded, 16)

        @block.scalar
        def _(act):
            for n, v in enumerate(shifts_scales):
                load_cols(act.dma_start, bias_cols[:, n], i["b_ada_2"][l:l + 1, v * D:(v + 1) * D], KD
                          ).then_inc(cols_loaded, 16)
            for n in range(2):
                load_cols(act.dma_start, gains[:, n], i["norm_g_2"][l, n:n + 1], KD).then_inc(cols_loaded, 16)
            for n, v in enumerate(residual_gates):
                act.dma_start(bias_rows[:, n], i["b_ada_2"][l:l + 1, v * D:(v + 1) * D].broadcast_to([P, D])
                              ).then_inc(rows_loaded, 16)

        @block.vector
        def _(dve):
            link = Link(dve, chain)
            dve.wait_ge(cols_loaded, 160)
            link(nc.vector.tensor_tensor(cols, cols, bias_cols, ALU.add))
            for n in range(2):
                nc.vector.tensor_copy(K.shift[:, n], cols[:, 2 * n])
                link(nc.vector.scalar_tensor_tensor(K.gain[:, n], cols[:, 2 * n + 1], 1.0, gains[:, n],
                                                    ALU.add, ALU.mult))
            dve.wait_ge(rows_loaded, 64)
            link(nc.vector.tensor_tensor(K.gate[:], K.gate[:], bias_rows, ALU.add))


def stage_projection(K, S, gain, shift, source, blocks, area_at):
    nc = K.nc
    with S.open() as (block, sem):
        norm = NormTranspose(K, sem, Area(K.arena, area_at))
        chain, h_ready = sem("chain"), sem("h_ready")
        w_loaded = [sem("w_loaded0"), sem("w_loaded1")]
        proj_ready, proj_out = sem("proj_ready"), sem("proj_out")

        @block.sync
        def _(sp):
            for n, (_, c0, _) in enumerate(blocks):
                if n >= 2:
                    sp.wait_ge(proj_ready, n - 1)
                sp.dma_start(K.wslot[n % 2], source[:, c0:c0 + 512].rearrange("(k p) n -> p k n", p=P)
                             ).then_inc(w_loaded[n % 2], 16)

        @block.scalar
        def _(act):
            norm.act(act)

        @block.tensor
        def _(pe):
            norm.pe(pe)
            pe.wait_ge(h_ready, KD)
            for n, (kind, _, _) in enumerate(blocks):
                pe.wait_ge(w_loaded[n % 2], 16 * (n // 2 + 1))
                if n >= 2:
                    pe.wait_ge(proj_out, n - 1)
                w, ps = K.wslot[n % 2], K.ps_pair[n % 2]
                if kind == "cols":
                    for c in range(4):
                        last = matmul_cols(nc, ps[:, c // 2, (c % 2) * SEQ:(c % 2 + 1) * SEQ], w,
                                           K.h_t, c, KD)
                else:
                    for t in range(TT):
                        last = matmul_rows(nc, ps[:, t], K.h_t, w, t, KD)
                last.then_inc(proj_ready, 1)

        @block.vector
        def _(dve):
            link = Link(dve, chain)
            norm.dve_norm(dve, link)
            norm.dve_scale(dve, gain, shift, h_ready)
            for n, (kind, _, dst) in enumerate(blocks):
                dve.wait_ge(proj_ready, n + 1)
                ps = K.ps_pair[n % 2]
                if kind == "cols":
                    ps = ps.rearrange("p b (c t) -> p (b c) t", c=2)
                nc.vector.tensor_copy(dst, ps).then_inc(proj_out, 1)


def residual_out(K, dve, link, w_gate, o_ready, tmp):
    nc = K.nc
    for t in range(TT):
        dve.wait_ge(o_ready, t + 1)
        link(nc.vector.tensor_tensor(tmp, K.ps[:, 4 + 2 * t:6 + 2 * t].rearrange("p b n -> p (b n)"),
                                     w_gate, ALU.mult))
        link(nc.vector.tensor_tensor(K.x[:, t], K.x[:, t], tmp, ALU.add))


def product_out(K, pe, w, o_ready):
    for t in range(TT):
        for half in range(2):
            last = matmul_rows(K.nc, K.ps[:, 4 + 2 * t + half], K.h_t, w[:, :, half * 512:(half + 1) * 512],
                               t, KD)
        last.then_inc(o_ready, 1)



def hg_memory(K):
    area = Area(K.arena)
    H = Names()
    H.q = area.take(HG, CH, P)
    H.k = area.take(2, HG, CH, P)
    H.v = area.take(TT, D)
    H.g = area.take(TT, D)
    H.pre = area.take(2, HG * CH, PRE)
    H.at = area.take(HG, 4, P)
    H.masks = area.take(HG * P // 4).bitcast(U8).rearrange("p (l t) -> p l t", l=8)
    H.end = area.at
    return H


def stage_hg_gates(K, S, H):
    nc, i = K.nc, K.i
    with S.open() as (block, sem):
        area = Area(K.arena, H.end)
        lb = area.take(4, HG)
        carry = area.take(HG * CH, PRE)
        px = area.take(P).bitcast(I32)
        tx = area.take(P).bitcast(I32)
        m = area.take(P).bitcast(I32)
        chain, loaded, iotas, sig_ready = sem("chain"), sem("loaded"), sem("iotas"), sem("sig")
        lb_ready, exp_ready, f_ready, ln_ready = sem("lb"), sem("exp"), sem("f"), sem("ln")
        k_flat = H.k.rearrange("p d h c t -> p (d h c t)")

        @block.sync
        def _(sp):
            load_cols(sp.dma_start, lb[:, 0], i["hg_lb_2"], HG).then_inc(loaded, 16)

        @block.gpsimd
        def _(pool):
            nc.gpsimd.memset(carry, 1.0).then_inc(iotas, 1)
            nc.gpsimd.iota(px, pattern=[[0, P]], base=0, channel_multiplier=1).then_inc(iotas, 1)
            nc.gpsimd.iota(tx, pattern=[[1, P]], base=0, channel_multiplier=0).then_inc(iotas, 1)
            pool.wait_ge(iotas, 3)
            nc.gpsimd.memset(carry[:, :, 0:1], 0.0).then_inc(iotas, 1)

        @block.scalar
        def _(act):
            nc.scalar.activation(k_flat, k_flat, ACT.Sigmoid).then_inc(sig_ready, 1)
            act.wait_ge(lb_ready, 1)
            nc.scalar.activation(lb[:, 2], lb[:, 1], ACT.Exp).then_inc(exp_ready, 1)
            act.wait_ge(f_ready, 1)
            for d in range(2):
                nc.scalar.activation(H.pre[:, d, :, 1:], H.k[:, d].rearrange("p h c t -> p (h c) t"),
                                     ACT.Ln).then_inc(ln_ready, 1)

        @block.vector
        def _(dve):
            link = Link(dve, chain)
            dve.wait_ge(loaded, 16)
            nc.vector.tensor_tensor(lb[:, 1], lb[:, 0], lb[:, 0], ALU.subtract).then_inc(lb_ready, 1)
            dve.wait_ge(exp_ready, 1)
            link(nc.vector.reciprocal(lb[:, 3], lb[:, 2]))
            link(nc.vector.tensor_tensor(lb[:, 3], lb[:, 3], lb[:, 2], ALU.mult))
            link(nc.vector.tensor_tensor(lb[:, 0], lb[:, 3], lb[:, 3], ALU.subtract))
            link(nc.vector.tensor_scalar(lb[:, 1], lb[:, 0], -1.0, 1.0, ALU.mult, ALU.add))
            dve.wait_ge(sig_ready, 1)
            for d in range(2):
                for h in range(HG):
                    f = H.k[:, d, h].rearrange("p c t -> p (c t)")
                    ins = nc.vector.tensor_scalar(f, f, lb[:, 1, h:h + 1], lb[:, 0, h:h + 1], ALU.mult,
                                                  ALU.add)
            ins.then_inc(f_ready, 1)
            dve.wait_ge(iotas, 4)
            link(nc.vector.tensor_tensor(m, px, tx, ALU.bitwise_xor))
            link(nc.vector.memset(H.pre[:, :, :, 0:1], 0.0))
            dve.wait_ge(ln_ready, 2)
            for d in range(2):
                flat = H.pre[:, d].rearrange("p n t -> p (n t)")
                nc.vector.tensor_tensor_scan(flat, carry.rearrange("p n t -> p (n t)"), flat, 0.0,
                                             ALU.mult, ALU.add)
            link(nc.vector.tensor_scalar(k_flat, k_flat, -1.0, 1.0, ALU.mult, ALU.add))
            for n, L in enumerate(LEVELS):
                link(nc.vector.tensor_scalar(px, m, float(L), None, ALU.is_ge))
                link(nc.vector.scalar_tensor_tensor(H.masks[:, n], m, float(2 * L), px, ALU.is_lt, ALU.mult))
            link(nc.vector.tensor_scalar(H.masks[:, 7], m, 0.0, None, ALU.is_equal))


def stage_hg_attention(K, S, H):
    nc = K.nc
    NL = len(LEVELS)
    with S.open() as (block, sem):
        area = Area(K.arena, H.end)
        kq = area.take(2, 2, HG * CH * P)
        chain, exps, exp_done, pair_ready = sem("chain"), sem("exps"), sem("exp_done"), sem("pair_ready")
        a_ready, a_out = sem("a_ready"), sem("a_out")
        mod = ModulationProducts(K, sem, area, area, 1, 0, 12, [4, 5, 6])
        q = H.q.rearrange("p h c t -> p (h c) t")
        kf, kb = (H.k[:, d].rearrange("p h c t -> p (h c) t") for d in range(2))
        kk = H.k
        pf, pb = H.pre[:, 0], H.pre[:, 1]

        def halves(a, L):
            return a.rearrange("p n (b s j) -> p n b s j", s=2, j=L)

        def middle(pre, L):
            m = pre[:, :, 0:P].rearrange("p n (b s j) -> p n b s j", s=2, j=L)[:, :, :, 1, 0:1]
            return m.broadcast_to([P, HG * CH, P // (2 * L), L])

        @block.vector
        def _(dve):
            link = Link(dve, chain)

            def exponents(n):
                if n >= 2:
                    dve.wait_ge(a_ready, 4 * (n - 1))
                L = LEVELS[n]
                ek, eq = (kq[:, n % 2, w].rearrange("p (n t) -> p n t", t=P) for w in range(2))
                ek, eq = halves(ek, L), halves(eq, L)
                inc = lambda pre: pre[:, :, 1:].rearrange("p n (b s j) -> p n b s j", s=2, j=L)
                exc = lambda pre: pre[:, :, 0:P].rearrange("p n (b s j) -> p n b s j", s=2, j=L)
                nc.vector.tensor_tensor(ek[:, :, :, 0], middle(pf, L), inc(pf)[:, :, :, 0], ALU.subtract)
                nc.vector.tensor_tensor(ek[:, :, :, 1], exc(pb)[:, :, :, 1], middle(pb, L), ALU.subtract)
                nc.vector.tensor_tensor(eq[:, :, :, 1], inc(pf)[:, :, :, 1], middle(pf, L), ALU.subtract)
                nc.vector.tensor_tensor(eq[:, :, :, 0], middle(pb, L), exc(pb)[:, :, :, 0],
                                        ALU.subtract).then_inc(exps, 1)

            def factors(n):
                L = LEVELS[n]
                dve.wait_ge(exp_done, n + 1)
                ek, eq = (kq[:, n % 2, w].rearrange("p (n t) -> p n t", t=P) for w in range(2))
                ekh = halves(ek, L)
                nc.vector.tensor_tensor(ekh[:, :, :, 0], ekh[:, :, :, 0], halves(kf, L)[:, :, :, 0], ALU.mult)
                nc.vector.tensor_tensor(ekh[:, :, :, 1], ekh[:, :, :, 1], halves(kb, L)[:, :, :, 1], ALU.mult)
                nc.vector.tensor_tensor(eq, eq, q, ALU.mult).then_inc(pair_ready, 1)

            def take(n):
                if n >= 1:
                    dve.wait_ge(a_out, 4 * n)
                for b in range(4):
                    dve.wait_ge(a_ready, 4 * n + b + 1)
                    src = K.ps[:, b].rearrange("p (h c t) -> p h c t", h=2, c=CH)
                    mask = H.masks[:, n].unsqueeze(1).broadcast_to([P, CH, P])
                    for h in range(2):
                        ins = nc.vector.copy_predicated(H.at[:, 2 * b + h, 0:4:3], mask, src[:, h])
                    ins.then_inc(a_out, 1)

            exponents(0)
            for n in range(NL):
                if n + 1 < NL:
                    exponents(n + 1)
                factors(n)
                if n >= 1:
                    take(n - 1)
            dve.wait_ge(a_ready, 4 * (NL - 1))
            nc.vector.tensor_tensor(kq[:, NL % 2, 0].rearrange("p (n t) -> p n t", t=P), kf, kb,
                                    ALU.add).then_inc(pair_ready, 1)
            take(NL - 1)
            e = kq[:, (NL + 1) % 2].rearrange("p w (h c t) -> p w h c t", h=HG, c=CH)
            pre = H.pre.rearrange("p d (h c) t -> p d h c t", c=CH)
            end_f = pre[:, 0, :, 0, P:].broadcast_to([P, HG, P])
            end_b = pre[:, 1, :, 0, P:].broadcast_to([P, HG, P])
            nc.vector.tensor_tensor(e[:, 0, :, 0], end_f, pre[:, 0, :, 0, 1:], ALU.subtract)
            nc.vector.tensor_copy(e[:, 0, :, 1], pre[:, 1, :, 1, 0:P])
            nc.vector.tensor_copy(e[:, 1, :, 1], pre[:, 0, :, 1, 1:])
            nc.vector.tensor_tensor(e[:, 1, :, 0], end_b, pre[:, 1, :, 0, 0:P], ALU.subtract).then_inc(exps, 1)
            take(NL)
            dve.wait_ge(exp_done, NL + 1)
            nc.vector.tensor_tensor(e[:, 0, :, 0], e[:, 0, :, 0], kk[:, 0, :, 0], ALU.mult)
            nc.vector.tensor_tensor(e[:, 0, :, 1], e[:, 0, :, 1], kk[:, 1, :, 1], ALU.mult)
            nc.vector.tensor_tensor(e[:, 1], e[:, 1], H.q, ALU.mult).then_inc(pair_ready, 1)
            dve.wait_ge(a_ready, 4 * (NL + 2))
            src = K.ps[:, 0:4].rearrange("p b (h c t) -> p (b h) c t", h=2, c=CH)
            for h in range(HG):
                ins = nc.vector.tensor_copy(H.at[:, h, 1:3], src[:, h])
            link(ins)

        @block.sync
        def _(sp):
            mod.load_c(sp)
            mod.load(sp, 0, 24)
            mod.store(sp)

        @block.scalar
        def _(act):
            mod.silu(act)
            for n in range(NL + 1):
                act.wait_ge(exps, n + 1)
                b = n % 2 if n < NL else (NL + 1) % 2
                flat = kq[:, b].rearrange("p w n -> p (w n)")
                nc.scalar.activation(flat, flat, ACT.Exp).then_inc(exp_done, 1)
            mod.act_out(act)

        @block.tensor
        def _(pe):
            for n in range(NL + 2):
                pe.wait_ge(pair_ready, n + 1)
                b = n % 2
                keys = kq[:, b, 0].rearrange("p (h c t) -> p h c t", h=HG, c=CH)
                queries = (kq[:, b, 1].rearrange("p (h c t) -> p h c t", h=HG, c=CH) if n != NL else H.q)
                for h in range(HG):
                    if n >= 1 and h % 2 == 0:
                        pe.wait_ge(a_out, 4 * (n - 1) + h // 2 + 1)
                    for c in range(CH):
                        cq = c if n <= NL else 1 - c
                        o = K.ps[:, h // 2, ((h % 2) * 2 + c) * P:((h % 2) * 2 + c + 1) * P]
                        last = nc.tensor.matmul(o, keys[:, h, c], queries[:, h, cq], start=True, stop=True)
                    if h % 2:
                        last.then_inc(a_ready, 1)
                mod.pe(pe, 3 * n if n < 8 else 24, 3 * n + 3 if n < 8 else 24)


def stage_hg_out(K, S, H):
    nc, i = K.nc, K.i
    with S.open() as (block, sem):
        area = Area(K.arena, H.end)
        o = area.take(TT, D)
        sq = area.take(TT, D)
        gain = area.take(D)
        st = area.take(3, TT, HG)
        chain, w_loaded, g_loaded, silu_ready = sem("chain"), sem("w_loaded"), sem("g_loaded"), sem("silu")
        o_ready, sq_ready, v_ready, sd_ready = sem("o_ready"), sem("sq"), sem("veps"), sem("sd")
        oc_ready, y_ready, yt_ready, yt_out, p_ready = (sem("oc"), sem("y"), sem("yt"), sem("yt_out"),
                                                        sem("p_ready"))
        w = K.big.rearrange("p (k n) -> p k n", k=KD)

        @block.sync
        def _(sp):
            sp.dma_start(gain, i["hg_norm_g_2"].broadcast_to([P, D])).then_inc(g_loaded, 16)
            sp.dma_start(w, i["hg_w_out_2"][0].rearrange("(k p) n -> p k n", p=P)).then_inc(w_loaded, 16)

        @block.tensor
        def _(pe):
            for t in range(TT):
                for h in range(HG):
                    for s in range(TT):
                        last = nc.tensor.matmul(K.ps[:, 2 * t + h // 4, (h % 4) * P:(h % 4 + 1) * P],
                                                H.at[:, h, 2 * s + t], H.v[:, s, h * P:(h + 1) * P],
                                                start=(s == 0), stop=(s == 1))
                last.then_inc(o_ready, 1)
            for t in range(TT):
                pe.wait_ge(y_ready, t + 1)
                for k in range(KD):
                    last = nc.tensor.transpose(K.ps_low[:, k, t * P:(t + 1) * P],
                                               o[:, t, k * P:(k + 1) * P], K.ident[:])
            last.then_inc(yt_ready, 1)
            pe.wait_ge(w_loaded, 16)
            pe.wait_ge(yt_out, 1)
            product_out(K, pe, w, p_ready)

        @block.scalar
        def _(act):
            nc.scalar.activation(H.g, H.g, ACT.Silu).then_inc(silu_ready, 1)
            for t in range(TT):
                act.wait_ge(oc_ready, t + 1)
                nc.scalar.activation(sq[:, t], o[:, t], ACT.Square).then_inc(sq_ready, 1)
            act.wait_ge(v_ready, 1)
            nc.scalar.activation(st[:, 2], st[:, 1], ACT.Sqrt).then_inc(sd_ready, 1)

        @block.vector
        def _(dve):
            link = Link(dve, chain)
            for t in range(TT):
                dve.wait_ge(o_ready, t + 1)
                nc.vector.tensor_copy(o[:, t], K.ps[:, 2 * t:2 * t + 2].rearrange("p b n -> p (b n)")
                                      ).then_inc(oc_ready, 1)
            for t in range(TT):
                dve.wait_ge(sq_ready, t + 1)
                link(nc.vector.tensor_reduce(st[:, 0, t], sq[:, t].rearrange("p (h d) -> p h d", h=HG), AX.X,
                                             ALU.add))
            nc.vector.tensor_scalar(st[:, 1], st[:, 0], 1.0 / HD, EPS, ALU.mult, ALU.add).then_inc(v_ready, 1)
            dve.wait_ge(silu_ready, 1)
            dve.wait_ge(g_loaded, 16)
            for t in range(TT):
                link(nc.vector.tensor_tensor(H.g[:, t], H.g[:, t], gain, ALU.mult))
            dve.wait_ge(sd_ready, 1)
            link(nc.vector.reciprocal(st[:, 0], st[:, 2]))
            for t in range(TT):
                link(nc.vector.tensor_tensor(
                    o[:, t].rearrange("p (h d) -> p h d", h=HG), o[:, t].rearrange("p (h d) -> p h d", h=HG),
                    st[:, 0, t].unsqueeze(2).broadcast_to([P, HG, HD]), ALU.mult))
                nc.vector.tensor_tensor(o[:, t], o[:, t], H.g[:, t], ALU.mult).then_inc(y_ready, 1)
            dve.wait_ge(yt_ready, 1)
            nc.vector.tensor_copy(K.h_t[:].rearrange("p k t -> p (k t)"),
                                  K.ps_low.rearrange("p k t -> p (k t)")).then_inc(yt_out, 1)
            residual_out(K, dve, link, K.gate[:, 0], p_ready, sq[:, 0])


def hg_mixer(K, S):
    H = hg_memory(K)
    src = K.i["hg_w_in_2"][0]
    blocks = []
    for half in range(2):
        hs = slice(4 * half, 4 * half + 4)
        blocks.append(("cols", half * 512, H.q[:, hs].rearrange("p h c t -> p h (c t)")))
        for d in range(2):
            blocks.append(("cols", (1 + d) * D + half * 512, H.k[:, d, hs].rearrange("p h c t -> p h (c t)")))
        blocks.append(("rows", 3 * D + half * 512, H.v[:, :, half * 512:(half + 1) * 512]))
        blocks.append(("rows", 4 * D + half * 512, H.g[:, :, half * 512:(half + 1) * 512]))
    stage_projection(K, S, K.gain[:, 0], K.shift[:, 0], src, blocks, H.end)
    stage_hg_gates(K, S, H)
    stage_hg_attention(K, S, H)
    stage_hg_out(K, S, H)



def stage_lru(K, S, xb, yb, at):
    nc, i = K.nc, K.i
    with S.open() as (block, sem):
        area = Area(K.arena, at)
        padded = area.take(KD, SEQ + TAPS - 1)
        xc, r, th, ig, bb, aa = (area.take(KD, SEQ) for _ in range(6))
        hs = [area.take(KD, SEQ), bb]
        w = K.big.rearrange("p (k n) -> p k n", k=KD)
        cw = area.take(TAPS, KD)
        cb = area.take(KD)
        bias = area.take(4, KD)
        lam, ex, u, u2, poly = (area.take(2, KD) for _ in range(5))
        tmp = r.rearrange("p k t -> p (k t)")[:, 0:D]
        chain, loaded, wg_loaded, w_loaded = sem("chain"), sem("loaded"), sem("wg_loaded"), sem("w_loaded")
        z_ready, e_ready, xc_ready, g_ready = sem("z"), sem("e"), sem("xc"), sem("g")
        sig_done, nsp_ready, at_done = sem("sig"), sem("nsp"), sem("at")
        m_ready, sq_done, gelu_done, y_ready, o_ready = (sem("m"), sem("sq"), sem("gelu"), sem("y"),
                                                         sem("o"))
        th_used = sem("th_used")
        wg = [a.rearrange("p (n j) -> p n j", n=16) for a in (K.ring[:], K.arena[:, 28672:32768])]
        assert area.at <= 24576

        @block.sync
        def _(sp):
            for n, gate_w in enumerate((i["lru_w_a_2"], i["lru_w_x_2"])):
                src = gate_w[0].rearrange("d b (k p) j -> p (d b k) j", p=P)
                sp.dma_start(wg[n], src).then_inc(wg_loaded, 16)
            w_out = i["lru_w_out_2"][0].rearrange("(k p) n -> p k n", p=P)
            sp.dma_start(w[:, 0:4], w_out[:, 0:4]).then_inc(w_loaded, 16)
            sp.wait_ge(g_ready, 4)
            sp.dma_start(w[:, 4:8], w_out[:, 4:8]).then_inc(w_loaded, 16)

        @block.scalar
        def _(act):
            for j in range(TAPS):
                load_cols(act.dma_start, cw[:, j], i["lru_conv_w_2"][0, j:j + 1], KD).then_inc(loaded, 16)
            load_cols(act.dma_start, cb, i["lru_conv_b_2"], KD).then_inc(loaded, 16)
            for d in range(2):
                load_cols(act.dma_start, bias[:, 2 * d], i["lru_b_a_2"][0, d:d + 1], KD).then_inc(loaded, 16)
                load_cols(act.dma_start, bias[:, 2 * d + 1], i["lru_b_x_2"][0, d:d + 1], KD).then_inc(loaded, 16)
                load_cols(act.dma_start, lam[:, d], i["lru_lam_2"][0, d:d + 1], KD).then_inc(loaded, 16)
            act.wait_ge(z_ready, 1)
            nc.scalar.activation(ex, u, ACT.Exp).then_inc(e_ready, 1)
            for d in range(2):
                for which, dst in enumerate((r, ig)):
                    act.wait_ge(g_ready, 2 * d + which + 1)
                    if d == 1 and which == 0:
                        act.wait_ge(at_done, 1)
                    if d == 1 and which == 1:
                        act.wait_ge(th_used, 1)
                    for c in range(KD):
                        src = K.ps[:, 4 * which + c // 2, (c % 2) * SEQ:(c % 2 + 1) * SEQ]
                        ins = nc.scalar.activation(dst[:, c], src, ACT.Sigmoid,
                                                   bias=bias[:, 2 * d + which, c:c + 1])
                ins.then_inc(sig_done, 1)
                act.wait_ge(sig_done, d + 1)
                act.wait_ge(nsp_ready, 1)
                if d == 1:
                    act.wait_ge(th_used, 1)
                for c in range(KD):
                    nc.scalar.activation(th[:, c], r[:, c], ACT.Tanh, scale=lam[:, d, c:c + 1])
                    ins = nc.scalar.activation(aa[:, c], r[:, c], ACT.Exp, scale=lam[:, d, c:c + 1])
                ins.then_inc(at_done, 1)
                act.wait_ge(m_ready, d + 1)
                nc.scalar.activation(th, th, ACT.Sqrt).then_inc(sq_done, 1)
            nc.scalar.activation(yb, yb, ACT.Gelu_apprx_tanh).then_inc(gelu_done, 1)

        @block.tensor
        def _(pe):
            pe.wait_ge(wg_loaded, 32)
            pe.wait_ge(xc_ready, 1)
            for d in range(2):
                for which in range(2):
                    if d == 1:
                        pe.wait_ge(sig_done, 1)
                    for c in range(KD):
                        for kk in range(2):
                            n = (d * LRU_BLOCKS + c // 2) * 2 + kk
                            last = nc.tensor.matmul(
                                K.ps[:, 4 * which + c // 2, (c % 2) * SEQ:(c % 2 + 1) * SEQ],
                                wg[which][:, n, (c % 2) * P:(c % 2 + 1) * P], xc[:, (c // 2) * 2 + kk],
                                start=(kk == 0), stop=(kk == 1))
                    last.then_inc(g_ready, 1)
            pe.wait_ge(w_loaded, 32)
            pe.wait_ge(y_ready, 1)
            product_out(K, pe, w, o_ready)

        @block.vector
        def _(dve):
            link = Link(dve, chain)
            nc.vector.memset(padded, 0.0)
            dve.wait_ge(loaded, 16 * (TAPS + 1 + 6))
            link(nc.vector.scalar_tensor_tensor(u, lam, -1.0, lam, ALU.mult, ALU.min))
            dve.sem_inc(z_ready, 1)
            link(nc.vector.tensor_copy(padded[:, :, LEFT:LEFT + SEQ], xb))
            for c in range(KD):
                for j in range(TAPS):
                    src = padded[:, c, j:j + SEQ]
                    if j == 0:
                        ins = nc.vector.tensor_scalar(xc[:, c], src, cw[:, 0, c:c + 1], cb[:, c:c + 1],
                                                      ALU.mult, ALU.add)
                    else:
                        ins = nc.vector.scalar_tensor_tensor(xc[:, c], src, cw[:, j, c:c + 1], xc[:, c],
                                                             ALU.mult, ALU.add)
                    link(ins)
            dve.sem_inc(xc_ready, 1)
            dve.wait_ge(e_ready, 1)
            link(nc.vector.tensor_scalar(u2, ex, 2.0, None, ALU.add))
            link(nc.vector.reciprocal(u, u2))
            link(nc.vector.tensor_tensor(u, u, ex, ALU.mult))
            link(nc.vector.tensor_tensor(u2, u, u, ALU.mult))
            link(nc.vector.tensor_scalar(poly, u2, 1.0 / 17, 1.0 / 15, ALU.mult, ALU.add))
            for k in (13, 11, 9, 7, 5, 3, 1):
                link(nc.vector.tensor_tensor(poly, poly, u2, ALU.mult))
                link(nc.vector.tensor_scalar(poly, poly, 1.0 / k, None, ALU.add))
            link(nc.vector.tensor_tensor(poly, poly, u, ALU.mult))
            link(nc.vector.tensor_scalar(ex, lam, -1.0, 0.0, ALU.mult, ALU.max))
            link(nc.vector.scalar_tensor_tensor(lam, poly, 2.0, ex, ALU.mult, ALU.add))
            link(nc.vector.tensor_scalar(lam, lam, -LRU_C, None, ALU.mult))
            dve.sem_inc(nsp_ready, 1)
            for d in range(2):
                dve.wait_ge(at_done, d + 1)
                link(nc.vector.tensor_scalar(bb, th, -1.0, 1.0, ALU.mult, ALU.add))
                link(nc.vector.reciprocal(bb, bb))
                link(nc.vector.scalar_tensor_tensor(th, th, -2.0, bb, ALU.mult, ALU.mult))
                dve.sem_inc(m_ready, 1)
                link(nc.vector.tensor_tensor(bb, ig, xc, ALU.mult))
                dve.wait_ge(sq_done, d + 1)
                link(nc.vector.tensor_tensor(bb, bb, th, ALU.mult))
                for c in range(KD):
                    if d == 0:
                        ins = nc.vector.tensor_tensor_scan(hs[d][:, c], aa[:, c], bb[:, c], 0.0, ALU.mult,
                                                           ALU.add)
                    else:
                        ins = nc.vector.tensor_tensor_scan(hs[d][:, c][:, ::-1], aa[:, c][:, ::-1],
                                                           bb[:, c][:, ::-1], 0.0, ALU.mult, ALU.add)
                link(ins)
                dve.sem_inc(th_used, 1)
            link(nc.vector.tensor_tensor(hs[0], hs[0], hs[1], ALU.add))
            dve.wait_ge(gelu_done, 1)
            nc.vector.tensor_tensor(K.h_t[:], hs[0], yb, ALU.mult).then_inc(y_ready, 1)
            residual_out(K, dve, link, K.gate[:, 0], o_ready, tmp)


def lru_mixer(K, S):
    area = Area(K.arena)
    xb = area.take(KD, SEQ)
    yb = area.take(KD, SEQ)
    blocks = [("cols", n * 512, (xb, yb)[n // 2][:, 4 * (n % 2):4 * (n % 2) + 4]) for n in range(4)]
    stage_projection(K, S, K.gain[:, 0], K.shift[:, 0], K.i["lru_w_in_2"][0], blocks, area.at)
    stage_lru(K, S, xb, yb, area.at)



def stage_scores(K, S, l, q, s, keys, keys_t):
    nc = K.nc
    with S.open() as (block, sem):
        loaded, kt_ready, kt_out, s_ready, s_out = (sem("loaded"), sem("kt_ready"), sem("kt_out"),
                                                    sem("s_ready"), sem("s_out"))

        @block.sync
        def _(sp):
            sp.dma_start(keys, K.i["peer_keys_2"][l].rearrange("h w k d -> k (h w) d")).then_inc(loaded, 16)

        @block.tensor
        def _(pe):
            pe.wait_ge(loaded, 16)
            for n in range(HP):
                last = nc.tensor.transpose(K.ps[:, n // 4, (n % 4) * P:(n % 4 + 1) * P], keys[:, n], K.ident[:])
            last.then_inc(kt_ready, 1)
            pe.wait_ge(kt_out, 1)
            for t in range(TT):
                for n in range(HP):
                    last = nc.tensor.matmul(K.ps[:, 4 * (1 - t) + n // 4, (n % 4) * P:(n % 4 + 1) * P],
                                            q[:, n, t * P:(t + 1) * P], keys_t[:, n], start=True, stop=True)
                last.then_inc(s_ready, 1)

        @block.vector
        def _(dve):
            dve.wait_ge(kt_ready, 1)
            nc.vector.tensor_copy(keys_t.rearrange("p n k -> p (n k)"),
                                  K.ps[:, 0:4].rearrange("p b n -> p (b n)")).then_inc(kt_out, 1)
            for t in range(TT):
                dve.wait_ge(s_ready, t + 1)
                b0 = 4 * (1 - t)
                nc.vector.tensor_copy(s[:, t].rearrange("p n k -> p (n k)"),
                                      K.ps[:, b0:b0 + 4].rearrange("p b n -> p (b n)")).then_inc(s_out, 1)
            dve.wait_ge(s_out, 2)


def pipeline(engine, first, last, unroll, body, straight=True):
    start = first // unroll
    if straight:
        for u in range(unroll):
            body(first + u, u, True)
        start += 1
    with engine.Fori(start, last // unroll) as i:
        for u in range(unroll):
            body(i * unroll + u, u, False)


SLOTS = 4
HALF_J = NKEYS // 2
TG = 4
GROUPS = SEQ // TG
SCRATCH = HALF_J * SEQ
EXP_AT = 52

assert GROUPS == HALF_J


class Gates:

    def __init__(self, K, sem, half, bank):
        self.K, self.half, self.bank = K, half, bank
        flat = K.h_t[:].rearrange("p k t -> p (k t)")
        self.left = flat[:, 0:2 * TG * P].rearrange("p (b t i) -> p b t i", b=2, t=TG)
        at = 2 * TG * P
        self.right = flat[:, at:at + TG * P].rearrange("p (b t j) -> p b t j", b=2, t=TG)
        at += TG * P
        self.ramp = flat[:, at:at + P]
        self.number = flat[:, at + P:at + P + 2 * TG].rearrange("p (b t) -> p b t", b=2)
        self.act = K.arena[:, half * SCRATCH:(half + 1) * SCRATCH].rearrange("p (j t) -> p t j", t=SEQ)
        self.fetched, self.seen = sem("numbers_fetched"), sem("numbers_seen")
        self.left_ready, self.right_ready = sem("left_ready"), sem("right_ready")
        self.w_ready, self.w_out = sem("weights_ready"), sem("weights_out")

    def pool(self, pool, g, b, early):
        nc, K = self.K.nc, self.K
        if not early:
            pool.wait_ge(self.w_ready, g - 1)
        nc.gpsimd.tensor_copy(self.number[:, b], K.sel[:, 0, bass.ds(g * TG, TG)]).then_inc(self.fetched, 1)
        pool.wait_ge(self.fetched, g + 1)
        pool.sem_inc(self.seen, 1)
        for t in range(TG):
            ins = nc.gpsimd.tensor_scalar(self.left[:, b, t], self.ramp, self.number[:, b, t:t + 1], None,
                                          ALU.is_equal)
        ins.then_inc(self.left_ready, 1)

    def pe(self, pe, g, b, early):
        pe.wait_ge(self.left_ready, g + 1)
        pe.wait_ge(self.right_ready, g + 1)
        if not early or g >= 2:
            pe.wait_ge(self.w_out, g - 1)
        for t in range(TG):
            last = self.K.nc.tensor.matmul(self.K.ps[:, self.bank + b, t * HALF_J:(t + 1) * HALF_J],
                                           self.left[:, b, t], self.right[:, b, t], start=True, stop=True)
        last.then_inc(self.w_ready, 1)

    def build(self, dve, g, b, early):
        nc, K = self.K.nc, self.K
        if not early or g >= 2:
            dve.wait_ge(self.w_ready, g - 1)
        ramp = self.ramp[:, self.half * HALF_J:(self.half + 1) * HALF_J]
        for t in range(TG):
            ins = nc.vector.tensor_scalar(self.right[:, b, t], ramp, K.sel[:, 1, bass.ds(g * TG + t, 1)],
                                          K.sel[:, 2, bass.ds(g * TG + t, 1)], ALU.is_equal, ALU.mult)
        ins.then_inc(self.right_ready, 1)

    def weigh(self, dve, g, b):
        dve.wait_ge(self.w_ready, g + 1)
        piece = self.act[:, bass.ds(g * TG, TG)]
        weights = self.K.ps[:, self.bank + b, 0:TG * HALF_J].rearrange("p (t j) -> p t j", t=TG)
        self.K.nc.vector.tensor_tensor(piece, piece, weights, ALU.mult).then_inc(self.w_out, 1)


def slot_loads(n, s):
    return (n - s) * (16 // SLOTS) + 16


def stage_expert_inputs(K, S, l, s):
    nc = K.nc
    G = TT * PH
    table = K.i["peer_u_2"][l].rearrange("(i j) d -> j i d", j=NKEYS)
    with S.open() as (block, sem):
        area = Area(K.arena, SCRATCH + TT * HP * NKEYS)
        val = area.take(TT * HP, TOPK)
        idx = area.take(TT * HP, TOPK).bitcast(U32)
        idf = area.take(TT * HP, TOPK)
        cand = area.take(G, TOPK, TOPK)
        top = area.take(G, TOPK)
        pos = area.take(G, TOPK).bitcast(U32)
        part = area.take(G, TOPK).bitcast(U32)
        partf = area.take(G, TOPK)
        picked = area.take(2, G, TOPK)
        gates = area.take(G, TOPK)
        sums = area.take(G)
        onehot = area.take(G, TOPK, TOPK)
        ramp16 = area.take(TOPK)
        assert area.at <= 32768
        sf = s.rearrange("p t n k -> p (t n) k")

        u = K.ring[:].rearrange("p (s k d) -> p s k d", s=SLOTS, k=KD)
        u_t = K.split[:, 0:4 * D].rearrange("p (b w k e) -> p b w k e", b=2, w=2, k=KD)
        h = K.split[:, 4 * D:].rearrange("p (w k t) -> p w k t", w=2, k=KD)
        u_loaded = [sem(f"u_loaded{n}") for n in range(SLOTS)]
        chain, h_high, h_ready = sem("chain"), sem("h_high"), sem("h_ready")
        ut_high, ut_low = sem("ut_high"), sem("ut_low")
        a_ready, gelu_done, ut_ready = sem("a_ready"), sem("gelu_done"), sem("ut_ready")
        ramp_ready, gl_ready, e_ready = sem("ramp_ready"), sem("gl_ready"), sem("e_ready")
        sel_ready, sel_t_ready, sel_out = sem("sel_ready"), sem("sel_t_ready"), sem("sel_out")
        weights = Gates(K, sem, 0, 6)

        @block.sync
        def _(sp):
            def load(n, s, early):
                if not early:
                    sp.wait_ge(ut_ready, 2 * n - 2 * (SLOTS - 1))
                sp.dma_start(u[:, s].rearrange("p k d -> p (k d)"),
                             table[bass.ds(n, 1)].rearrange("a i d -> i (a d)")).then_inc(u_loaded[s], 16)

            pipeline(sp, 0, NKEYS, SLOTS, load)

        @block.gpsimd
        def _(pool):
            nc.gpsimd.iota(ramp16, pattern=[[1, TOPK]], base=0, channel_multiplier=0,
                           allow_small_or_imprecise_dtypes=True).then_inc(ramp_ready, 1)
            pool.wait_ge(h_ready, 1)
            nc.gpsimd.iota(weights.ramp, pattern=[[1, P]], base=0, channel_multiplier=0,
                           allow_small_or_imprecise_dtypes=True).then_inc(ramp_ready, 1)
            pool.wait_ge(ramp_ready, 2)
            pool.wait_ge(sel_out, 1)
            pipeline(pool, 0, GROUPS, 2, lambda g, b, early: weights.pool(pool, g, b, early))

        @block.tensor
        def _(pe):
            def products(n, b, early):
                pe.wait_ge(ut_high, 2 * n + 2)
                pe.wait_ge(ut_low, 2 * n + 2)
                if not early:
                    pe.wait_ge(gelu_done, n - 1)
                for k in range(KD):
                    for w, wh in ((0, 0), (0, 1), (1, 0)):
                        last = nc.tensor.matmul(K.ps[:, 4 + b, 0:SEQ], u_t[:, b, w, k], h[:, wh, k],
                                                start=(k == 0 and w == wh), stop=(k == KD - 1 and w == 1))
                last.then_inc(a_ready, 1)

            def chunk(n, s, early):
                b = s % 2
                pe.wait_ge(u_loaded[s], slot_loads(n, s))
                if not early or n >= 2:
                    pe.wait_ge(ut_high, 2 * n - 2)
                    pe.wait_ge(ut_low, 2 * n - 2)
                for k in range(KD):
                    last = nc.tensor.transpose(K.ps[:, 2 * b + k // 4, (k % 4) * P:(k % 4 + 1) * P],
                                               u[:, s, k], K.ident[:])
                    if k % 4 == 3:
                        last.then_inc(ut_ready, 1)
                if not early or n >= 1:
                    products(n - 1, 1 - b, early and n < 3)

            def chunk_and_gates(n, s, early):
                chunk(n, s, False)
                weights.pe(pe, n - HALF_J, s % 2, early)

            pe.wait_ge(h_ready, 1)
            pipeline(pe, 0, HALF_J, SLOTS, chunk)
            pe.wait_ge(sel_ready, 1)
            for n, src in enumerate((picked[:, 0], picked[:, 1], gates)):
                src = src.rearrange("p (t h) k -> p t (h k)", t=TT)
                for t in range(TT):
                    last = nc.tensor.transpose(K.ps[:, 6 + n // 2, (n % 2) * SEQ + t * P:(n % 2) * SEQ + (t + 1) * P],
                                               src[:, t], K.ident[:])
            last.then_inc(sel_t_ready, 1)
            pe.wait_ge(sel_out, 1)
            pipeline(pe, HALF_J, NKEYS, SLOTS, chunk_and_gates)
            products(NKEYS - 1, (NKEYS - 1) % 2, False)

        @block.scalar
        def _(act):
            def high(n, s, early):
                b = s % 2
                if not early or n >= 2:
                    act.wait_ge(a_ready, n - 1)
                for half in range(2):
                    act.wait_ge(ut_ready, 2 * n + half + 1)
                    nc.scalar.copy(u_t[:, b, 0, 4 * half:4 * half + 4].rearrange("p k e -> p (k e)"),
                                   K.ps[:, 2 * b + half]).then_inc(ut_high, 1)

            def gelu(n, b):
                act.wait_ge(a_ready, n + 1)
                nc.scalar.activation(K.arena[:, bass.ds(n * SEQ, SEQ)], K.ps[:, 4 + b, 0:SEQ],
                                     ACT.Gelu_apprx_tanh).then_inc(gelu_done, 1)

            def chunk(n, s, early):
                high(n, s, early)
                if not early or n >= 1:
                    gelu(n - 1, (s + 1) % 2)

            nc.scalar.copy(h[:, 0], K.h_t[:]).then_inc(h_high, 1)
            pipeline(act, 0, EXP_AT, SLOTS, chunk)
            act.wait_ge(gl_ready, 1)
            nc.scalar.activation(gates, gates, ACT.Exp).then_inc(e_ready, 1)
            pipeline(act, EXP_AT, HALF_J, SLOTS, chunk, straight=False)
            act.wait_ge(sel_t_ready, 1)
            pipeline(act, HALF_J, NKEYS, SLOTS, chunk, straight=False)
            gelu(NKEYS - 1, (NKEYS - 1) % 2)
            act.wait_ge(gelu_done, NKEYS)

        @block.vector
        def _(dve):
            link = Link(dve, chain)

            def low(n, s, early):
                b = s % 2
                if not early or n >= 2:
                    dve.wait_ge(a_ready, n - 1)
                for half in range(2):
                    dve.wait_ge(ut_high, 2 * n + half + 1)
                    pair = [u_t[:, b, w, 4 * half:4 * half + 4].rearrange("p k e -> p (k e)") for w in range(2)]
                    nc.vector.tensor_tensor(pair[1], K.ps[:, 2 * b + half], pair[0].bitcast(F32),
                                            ALU.subtract).then_inc(ut_low, 1)

            chunks = [0]

            def keep_up(count=1):
                for _ in range(count):
                    low(chunks[0], chunks[0] % SLOTS, True)
                    chunks[0] += 1

            def top16(values, out, places, n, per_chunk):
                for half in range(2):
                    cut = slice(8 * half, 8 * half + 8)
                    for g in range(n):
                        ins = nc.vector.max(out[:, g, cut], values[:, g])
                        if g == n - 1:
                            link(ins)
                        elif g % per_chunk == per_chunk - 1:
                            keep_up()
                    for g in range(n):
                        ins = nc.vector.max_index(places[:, g, cut], out[:, g, cut], values[:, g])
                        if g == n - 1:
                            link(ins)
                        elif g % per_chunk == per_chunk - 1:
                            keep_up()
                    if half == 0:
                        for g in range(n):
                            ins = nc.vector.match_replace(values[:, g], out[:, g, cut], values[:, g], -BIG)
                            if g == n - 1:
                                link(ins)
                            elif g % per_chunk == per_chunk - 1:
                                keep_up()

            dve.wait_ge(h_high, 1)
            nc.vector.tensor_tensor(h[:, 1], K.h_t[:], h[:, 0].bitcast(F32), ALU.subtract).then_inc(h_ready, 1)
            top16(sf, val, idx, TT * HP, 8)
            link(nc.vector.tensor_copy(idf, idx))
            v4 = val.rearrange("p (g w) k -> p g w k", w=2)
            for g in range(G):
                ins = nc.vector.tensor_tensor(cand[:, g], v4[:, g, 0].unsqueeze(2).broadcast_to([P, TOPK, TOPK]),
                                              v4[:, g, 1].unsqueeze(1).broadcast_to([P, TOPK, TOPK]), ALU.add)
                if g == G - 1:
                    link(ins)
                elif g % 5 == 4:
                    keep_up()
            keep_up()
            top16(cand.rearrange("p g a b -> p g (a b)"), top, pos, G, 5)
            nc.vector.tensor_tensor(gates, top, top[:, :, 0:1].broadcast_to([P, G, TOPK]),
                                    ALU.subtract).then_inc(gl_ready, 1)
            assert chunks[0] < EXP_AT
            dve.wait_ge(ramp_ready, 1)
            i4 = idf.rearrange("p (g w) k -> p g w k", w=2)
            rampb = ramp16.unsqueeze(1).broadcast_to([P, TOPK, TOPK])
            for w, (op, number) in enumerate(((ALU.logical_shift_right, 4), (ALU.bitwise_and, TOPK - 1))):
                link(nc.vector.tensor_scalar(part, pos, number, None, op))
                link(nc.vector.tensor_copy(partf, part))
                for g in range(G):
                    ins = nc.vector.tensor_tensor(onehot[:, g], partf[:, g].unsqueeze(2).broadcast_to([P, TOPK, TOPK]),
                                                  rampb, ALU.is_equal)
                    if g % 5 == 4:
                        keep_up()
                link(ins)
                for g in range(G):
                    ins = nc.vector.tensor_tensor(onehot[:, g], onehot[:, g],
                                                  i4[:, g, w].unsqueeze(1).broadcast_to([P, TOPK, TOPK]), ALU.mult)
                    if g % 5 == 4:
                        keep_up()
                link(ins)
                for q in range(4):
                    gs = slice(q * G // 4, (q + 1) * G // 4)
                    link(nc.vector.tensor_reduce(picked[:, w, gs].rearrange("p g k -> p (g k)"),
                                                 onehot[:, gs].rearrange("p g k a -> p (g k) a"), AX.X, ALU.add))
                    if q % 2:
                        keep_up()
            assert chunks[0] <= HALF_J
            keep_up(max(0, EXP_AT + 1 - chunks[0]))
            dve.wait_ge(e_ready, 1)
            link(nc.vector.tensor_reduce(sums, gates, AX.X, ALU.add))
            link(nc.vector.reciprocal(sums, sums))
            nc.vector.tensor_tensor(gates, gates, sums.unsqueeze(2).broadcast_to([P, G, TOPK]),
                                    ALU.mult).then_inc(sel_ready, 1)
            keep_up(HALF_J - chunks[0])
            dve.wait_ge(sel_t_ready, 1)
            nc.vector.tensor_copy(K.sel[:, 0:2].rearrange("p n t -> p (n t)"), K.ps[:, 6])
            nc.vector.tensor_copy(K.sel[:, 2], K.ps[:, 7, 0:SEQ]).then_inc(sel_out, 1)
            dve.wait_ge(sel_out, 1)
            dve.wait_ge(ramp_ready, 2)
            dve.wait_ge(gelu_done, HALF_J - 1)

            def chunk(n, s, early):
                g = n - HALF_J
                weights.build(dve, g, s % 2, early)
                low(n, s, False)
                if early and g == 0:
                    dve.wait_ge(gelu_done, HALF_J)
                if not early or g >= 1:
                    weights.weigh(dve, g - 1, 1 - s % 2)

            pipeline(dve, HALF_J, NKEYS, SLOTS, chunk)
            weights.weigh(dve, GROUPS - 1, (GROUPS - 1) % 2)
            dve.wait_ge(weights.w_out, GROUPS)


def stage_expert_outputs(K, S, l):
    nc = K.nc
    table = K.i["peer_v_2"][l].rearrange("(i j) d -> j i d", j=NKEYS)
    with S.open() as (block, sem):
        v_loaded = [sem(f"v_loaded{s}") for s in range(SLOTS)]
        v_high, v_low, g_high, g_low, p_done, chain = (sem("v_high"), sem("v_low"), sem("g_high"),
                                                       sem("g_low"), sem("p_done"), sem("chain"))
        v = K.ring[:].rearrange("p (s d) -> p s d", s=SLOTS)
        vs = K.split[:, 0:4 * D].rearrange("p (b w d) -> p b w d", b=2, w=2)
        g = K.split[:, 4 * D:4 * D + 4 * SEQ].rearrange("p (b w t) -> p b w t", b=2, w=2)
        weights = Gates(K, sem, 1, 0)
        tmp = K.ring[:, 0:D]

        @block.sync
        def _(sp):
            def load(n, s, early):
                if not early:
                    sp.wait_ge(v_low, 2 * n - 2 * (SLOTS - 1))
                sp.dma_start(v[:, s], table[bass.ds(n, 1)].rearrange("a i d -> i (a d)")
                             ).then_inc(v_loaded[s], 16)

            pipeline(sp, 0, NKEYS, SLOTS, load)

        @block.gpsimd
        def _(pool):
            pipeline(pool, 0, GROUPS, 2, lambda g, b, early: weights.pool(pool, g, b, early))

        @block.scalar
        def _(act):
            def chunk(n, s, early):
                b = s % 2
                if not early or n >= 2:
                    act.wait_ge(p_done, n - 1)
                nc.scalar.copy(g[:, b, 0], K.arena[:, bass.ds(n * SEQ, SEQ)]).then_inc(g_high, 1)
                act.wait_ge(v_loaded[s], slot_loads(n, s))
                for half in range(2):
                    cut = slice(half * 512, (half + 1) * 512)
                    nc.scalar.copy(vs[:, b, 0, cut], v[:, s, cut]).then_inc(v_high, 1)

            pipeline(act, 0, HALF_J, SLOTS, chunk)
            act.wait_ge(weights.w_out, GROUPS)
            pipeline(act, HALF_J, NKEYS, SLOTS, chunk, straight=False)

        @block.vector
        def _(dve):
            link = Link(dve, chain)

            def low(n, s, early):
                b = s % 2
                dve.wait_ge(g_high, n + 1)
                nc.vector.tensor_tensor(g[:, b, 1], K.arena[:, bass.ds(n * SEQ, SEQ)], g[:, b, 0].bitcast(F32),
                                        ALU.subtract).then_inc(g_low, 1)
                for half in range(2):
                    cut = slice(half * 512, (half + 1) * 512)
                    dve.wait_ge(v_high, 2 * n + half + 1)
                    nc.vector.tensor_tensor(vs[:, b, 1, cut], v[:, s, cut], vs[:, b, 0, cut].bitcast(F32),
                                            ALU.subtract).then_inc(v_low, 1)

            def chunk(n, s, early):
                weights.build(dve, n, s % 2, early)
                low(n, s, early)
                if not early or n >= 1:
                    weights.weigh(dve, n - 1, 1 - s % 2)

            pipeline(dve, 0, HALF_J, SLOTS, chunk)
            weights.weigh(dve, GROUPS - 1, (GROUPS - 1) % 2)
            dve.wait_ge(weights.w_out, GROUPS)
            pipeline(dve, HALF_J, NKEYS, SLOTS, low, straight=False)
            dve.wait_ge(p_done, NKEYS)
            dve.wait_ge(v_low, 2 * NKEYS)
            for t in range(TT):
                link(nc.vector.tensor_tensor(tmp, K.ps[:, 4 + 2 * t:6 + 2 * t].rearrange("p b n -> p (b n)"),
                                             K.gate[:, 1], ALU.mult))
                link(nc.vector.tensor_tensor(K.x[:, t], K.x[:, t], tmp, ALU.add))

        @block.tensor
        def _(pe):
            def products(n, s, start, stop):
                b = s % 2
                pe.wait_ge(g_low, n + 1)
                pe.wait_ge(v_low, 2 * n + 2)
                for t in range(TT):
                    for w, wv in ((0, 0), (0, 1), (1, 0)):
                        for half in range(2):
                            last = nc.tensor.matmul(K.ps[:, 4 + 2 * t + half], g[:, b, w, t * P:(t + 1) * P],
                                                    vs[:, b, wv, half * 512:(half + 1) * 512],
                                                    start=(start and w == wv), stop=(stop and w == 1))
                last.then_inc(p_done, 1)

            def chunk_and_gates(n, s, early):
                products(n, s, early and s == 0, False)
                weights.pe(pe, n, s % 2, early)

            pipeline(pe, 0, HALF_J, SLOTS, chunk_and_gates)
            pipeline(pe, HALF_J, NKEYS - SLOTS, SLOTS, lambda n, s, early: products(n, s, False, False),
                     straight=False)
            for s in range(SLOTS):
                products(NKEYS - SLOTS + s, s, False, s == SLOTS - 1)


def retrieval(K, S, l):
    area = Area(K.arena)
    q = area.take(HP, SEQ)
    keys = area.take(HP, P)
    keys_t = area.take(HP, P)
    s = Area(K.arena, SCRATCH).take(TT, HP, NKEYS)
    blocks = [("cols", n * 512, q[:, 4 * n:4 * n + 4]) for n in range(4)]
    stage_projection(K, S, K.gain[:, 1], K.shift[:, 1], K.i["peer_w_q_2"][l], blocks, area.at)
    stage_scores(K, S, l, q, s, keys, keys_t)
    stage_expert_inputs(K, S, l, s)
    stage_expert_outputs(K, S, l)


def stage_final(K, S):
    nc = K.nc
    with S.open() as (block, sem):
        area = Area(K.arena)
        gain = area.take(D)
        sq = area.take(D)
        st = area.take(3, TT)
        chain, loaded, ms, var, sd, y, stored = (sem("chain"), sem("loaded"), sem("ms"), sem("var"), sem("sd"),
                                                 sem("y"), sem("stored"))

        @block.sync
        def _(sp):
            sp.dma_start(gain, K.i["final_g_2"].rearrange("(a d) -> a d", a=1).broadcast_to([P, D])
                         ).then_inc(loaded, 16)
            for t in range(TT):
                sp.wait_ge(y, t + 1)
                sp.dma_start(K.out[0, t * P:(t + 1) * P], K.x[:, t]).then_inc(stored, 16)
            sp.wait_ge(stored, 16 * TT)

        @block.scalar
        def _(act):
            for t in range(TT):
                nc.scalar.activation(sq, K.x[:, t], ACT.Square, accum_out=st[:, 0, t:t + 1]).then_inc(ms, 1)
                act.wait_ge(ms, t + 1)
            act.wait_ge(var, 1)
            nc.scalar.activation(st[:, 2], st[:, 1], ACT.Sqrt).then_inc(sd, 1)

        @block.vector
        def _(dve):
            link = Link(dve, chain)
            dve.wait_ge(ms, TT)
            nc.vector.tensor_scalar(st[:, 1], st[:, 0], 1.0 / D, EPS, ALU.mult, ALU.add).then_inc(var, 1)
            dve.wait_ge(sd, 1)
            link(nc.vector.reciprocal(st[:, 0], st[:, 2]))
            dve.wait_ge(loaded, 16)
            for t in range(TT):
                nc.vector.scalar_tensor_tensor(K.x[:, t], K.x[:, t], st[:, 0, t:t + 1], gain, ALU.mult,
                                               ALU.mult).then_inc(y, 1)


def second_block(K, S):
    for l in range(DEPTH):
        stage_modulation(K, S, l)
        if l % 2 == 0:
            hg_mixer(K, S)
        else:
            lru_mixer(K, S)
        retrieval(K, S, l)
    stage_final(K, S)


def memory(nc, K):
    def sb(name, dims, dt=F32):
        return nc.alloc_sbuf_tensor(name, [P, *dims], dt)

    K.x = sb("x_rows", [TT, D])
    K.h_t = sb("h_cols", [KD, SEQ])
    K.ident = sb("identity", [P])
    K.ones = sb("ones", [P])
    K.causal = sb("causal", [P])
    K.pos = sb("position", [TT])
    K.invf = sb("inverse_frequency", [HALF])
    K.cos = sb("cosine", [TT, HALF])
    K.sin = sb("sine", [TT, HALF])
    K.g_norm = sb("norm_gain", [KD])
    K.gain = sb("mixer_gains", [2, KD])
    K.shift = sb("mixer_shifts", [2, KD])
    K.gate = sb("residual_gates", [2, D])
    K.sel = sb("chosen_experts", [3, SEQ])
    K.arena = sb("arena", [32768])
    K.ring = sb("weights_ring", [4096])
    K.mod_dram = nc.dram_tensor("modulation_rows", [DEPTH, 6 * D], F32).ap()
    K.split = sb("split_operands", [8192], mybir.dt.float32r)
    K.big = K.arena[:, 24576:32768]
    K.wslot = [w.rearrange("p (k n) -> p k n", k=KD) for w in (K.ring[:], K.arena[:, 28672:32768])]
    K.ps = nc.alloc_psum_tensor("psum", [P, 8, 512], F32)
    K.ps_low = K.ps[:, 0:4].rearrange("p b (c t) -> p (b c) t", c=2)
    K.ps_pair = [K.ps[:, 4:6], K.ps[:, 6:8]]

    area = Area(K.arena)
    K.glu = area.take(4, SEQ)
    K.low = area.take((Q_LORA + KV_LORA) // P, SEQ)
    K.zconv = area.take(TT, CONV_W)
    K.rows = area.take(TT, N_ROWS)
    K.y = area.take(TT, D)
    K.v = area.take(TT, HEADS, VD)
    K.q_t = area.take(HEADS, SEQ)
    K.k_t = area.take(HEADS, SEQ)
    K.g_q = area.take(Q_LORA // P)
    K.g_kv = area.take(KV_LORA // P)
    K.g_branch = area.take(KD)
    K.cb = area.take(3, 2)
    K.cw = area.take(2, CONV_K)
    K.sgb = area.take(SG_HEADS)
    K.sgw = area.take(SG_HEADS, P)
    K.pwb = area.take(CONV_W)
    K.gqk = area.take(2, QK)
    K.sgln = area.take(2, SG_W)
    K.first_end = area.at


def build(nc, ins, out):
    K = Names()
    K.nc, K.i, K.out = nc, ins, out
    K.layer = lambda name, l: ins[name][bass.ds(l, 1), :]
    memory(nc, K)
    S = Stages(nc)
    with nc.allow_non_contiguous_dma("parameters by channel, a few KB"):
        stage_setup(K, S)
        stage_rope_tables(K, S)
        first_block(K, S)
        second_block(K, S)


def kernel(**inputs):
    import numpy as _np
    import concourse.bacc as _bacc
    from concourse import mybir as _mybir
    from concourse.bass_utils import run_bass_kernel_spmd as _run

    half = ROPE // 2
    inputs = dict(inputs)
    inputs["inv_freq"] = (_np.float32(10000.0) ** (-_np.arange(half, dtype=_np.float32) / _np.float32(half))
                          ).astype(_np.float32)[None]
    nc = _bacc.Bacc("TRN2", target_bir_lowering=False, num_devices=1)
    arrays, aps = {}, {}
    for name, value in inputs.items():
        a = _np.ascontiguousarray(value)
        arrays[f"in_{name}_dram"] = a
        aps[name] = nc.dram_tensor(f"in_{name}_dram", a.shape, _mybir.dt.from_np(a.dtype),
                                   kind="ExternalInput").ap()
    out = nc.dram_tensor("out_0_dram", (1, SEQ, D), F32, kind="ExternalOutput").ap()
    build(nc, aps, out)
    r = _run(nc, [arrays], core_ids=[0])
    return r.results[0]["out_0_dram"]
```
